# Optimizing a Trainium2 kernel written in Bass

```python
import jax, jax.numpy as jnp
from jax import lax
import numpy as np

D_MODEL = 1024
BATCH = 1
SEQ = 512
DEPTH = 1
DEC_BATCH = 8
DEC_SEQ = 4
PAST_LEN = 256
PAGE_SIZE = 128

PLE_DIM = 256
D_FF = 2816
GLA_HEADS = 4
GLA_DK = 64
GLA_DV = 128
GLA_RANK = 16
GLA_GATE_TEMP = 16.0
GLA_CHUNK = 64
SB_HEADS = 8
SB_DH = 64
SB_QBLOCK = 128
SB_BIAS_INIT = -8.0
EPS = 1e-6
GLA_QK_W = GLA_HEADS * GLA_DK
GLA_V_W = GLA_HEADS * GLA_DV
SB_W = SB_HEADS * SB_DH
MIX_WIDTH = GLA_V_W + SB_W
IN_SIZES = (GLA_QK_W, GLA_QK_W, GLA_V_W, GLA_V_W, GLA_RANK, SB_W, SB_W, SB_W)
IN_WIDTH = 2 * GLA_QK_W + 2 * GLA_V_W + GLA_RANK + 3 * SB_W

kernel_name = 'hymba_gla_stickbreak_macaron_decoder_step'

def rmsnorm(x, w):
    xf = x.astype(jnp.float32)
    y = xf * lax.rsqrt(jnp.mean(xf * xf, axis=-1, keepdims=True) + EPS) * w.astype(jnp.float32)
    return y.astype(x.dtype)

def swiglu(h, w_in, w_out):
    gu = h @ w_in
    g, u = jnp.split(gu, 2, axis=-1)
    return (jax.nn.silu(g) * u) @ w_out

def project(h, w_in, gate_w, gate_b):
    B, T, _ = h.shape
    z = h @ w_in
    parts = []
    off = 0
    for s in IN_SIZES:
        parts.append(z[..., off:off + s])
        off += s
    gq, gk, gv, gg, glr, sq, sk, sv = parts
    gq = gq.astype(jnp.float32).reshape(B, T, GLA_HEADS, GLA_DK) * GLA_DK ** -0.5
    gk = gk.astype(jnp.float32).reshape(B, T, GLA_HEADS, GLA_DK)
    gv = gv.astype(jnp.float32).reshape(B, T, GLA_HEADS, GLA_DV)
    la = jax.nn.log_sigmoid((glr @ gate_w + gate_b).astype(jnp.float32)) / GLA_GATE_TEMP
    la = la.reshape(B, T, GLA_HEADS, GLA_DK)
    sq = sq.reshape(B, T, SB_HEADS, SB_DH)
    sk = sk.reshape(B, T, SB_HEADS, SB_DH)
    sv = sv.reshape(B, T, SB_HEADS, SB_DH)
    return gq, gk, gv, gg, la, sq, sk, sv

def gla_chunk_step(S, chunk):
    q, k, v, la = chunk
    C = q.shape[1]
    b = jnp.cumsum(la, axis=1)
    causal = jnp.tril(jnp.ones((C, C), dtype=bool))
    diff = b[:, :, None] - b[:, None, :]
    decay = jnp.exp(jnp.where(causal[None, :, :, None, None], diff, -jnp.inf))
    att = jnp.einsum('bthd,bshd,btshd->bhts', q, k, decay)
    o = (jnp.einsum('bhts,bshv->bthv', att, v)
         + jnp.einsum('bthd,bhdv->bthv', q * jnp.exp(b), S))
    b_last = b[:, -1]
    S_new = (jnp.exp(b_last)[..., None] * S
             + jnp.einsum('bshd,bshv->bhdv', k * jnp.exp(b_last[:, None] - b), v))
    return S_new, o

def gla_prompt(q, k, v, la):
    B, T = q.shape[0], q.shape[1]
    n = T // GLA_CHUNK

    def to_chunks(a):
        return a.reshape((B, n, GLA_CHUNK) + a.shape[2:]).swapaxes(0, 1)

    S0 = jnp.zeros((B, GLA_HEADS, GLA_DK, GLA_DV), jnp.float32)
    S, o = lax.scan(gla_chunk_step, S0, (to_chunks(q), to_chunks(k), to_chunks(v), to_chunks(la)))
    o = o.swapaxes(0, 1).reshape(B, T, GLA_HEADS, GLA_DV)
    return o, S

def sb_attend(q, k, v, q_pos, k_pos, bias):
    z = (jnp.einsum('bqhd,bkhd->bhqk', q.astype(jnp.float32), k.astype(jnp.float32)) * SB_DH ** -0.5
         + bias.astype(jnp.float32)[None, :, None, None])
    valid = (k_pos[None, :] < q_pos[:, None])[None, None]
    log_stay = jnp.where(valid, jax.nn.log_sigmoid(-z), 0.0)
    after = lax.cumsum(log_stay, axis=3, reverse=True) - log_stay
    w = jnp.where(valid, jnp.exp(jax.nn.log_sigmoid(z) + after), 0.0)
    return jnp.einsum('bhqk,bkhd->bqhd', w, v.astype(jnp.float32))

def sb_prompt(q, k, v, bias):
    B, T = q.shape[0], q.shape[1]
    nb = T // SB_QBLOCK
    qb = q.reshape(B, nb, SB_QBLOCK, SB_HEADS, SB_DH).swapaxes(0, 1)
    qpos = jnp.arange(T).reshape(nb, SB_QBLOCK)
    kpos = jnp.arange(T)
    o = lax.map(lambda a: sb_attend(a[0], k, v, a[1], kpos, bias), (qb, qpos))
    return o.swapaxes(0, 1).reshape(B, T, SB_HEADS, SB_DH)

def sb_sample(q, k, v, pool_k, pool_v, page_table, bias):
    Bd, Tn = q.shape[0], q.shape[1]
    past_k = pool_k[page_table].reshape(Bd, -1, SB_HEADS, SB_DH)
    past_v = pool_v[page_table].reshape(Bd, -1, SB_HEADS, SB_DH)
    past_len = past_k.shape[1]
    k_all = jnp.concatenate([past_k, k.astype(past_k.dtype)], axis=1)
    v_all = jnp.concatenate([past_v, v.astype(past_v.dtype)], axis=1)
    q_pos = past_len + jnp.arange(Tn)
    k_pos = jnp.arange(past_len + Tn)
    return sb_attend(q, k_all, v_all, q_pos, k_pos, bias)

def merge(o_gla, g_out, o_sb, gla_norm, sb_norm, w_out, dtype):
    B, T = o_gla.shape[0], o_gla.shape[1]
    a = rmsnorm(o_gla, gla_norm).reshape(B, T, GLA_V_W) * jax.nn.silu(g_out.astype(jnp.float32))
    s = rmsnorm(o_sb, sb_norm).reshape(B, T, SB_W)
    m = jnp.concatenate([a, s], axis=-1).astype(dtype)
    return m @ w_out

def layer(x, p, lp, mix_fn):
    x = x + 0.5 * rmsnorm(swiglu(rmsnorm(x, lp['f1_pre']), lp['f1_in'], lp['f1_out']), lp['f1_post'])
    h = rmsnorm(x, lp['mix_pre'])
    gq, gk, gv, gg, la, sq, sk, sv = project(h, lp['w_in'], lp['gate_w'], lp['gate_b'])
    o_gla, o_sb, new_state = mix_fn(gq, gk, gv, la, sq, sk, sv)
    m = merge(o_gla, gg, o_sb, lp['gla_norm'], lp['sb_norm'], lp['w_out'], x.dtype)
    x = x + rmsnorm(m, lp['mix_post'])
    x = x + 0.5 * rmsnorm(swiglu(rmsnorm(x, lp['f2_pre']), lp['f2_in'], lp['f2_out']), lp['f2_post'])
    gate = jax.nn.sigmoid(rmsnorm(x, lp['ple_pre']) @ lp['ple_w_gate'])
    e = p.astype(x.dtype) @ lp['ple_w_up']
    x = x + rmsnorm(gate * e, lp['ple_post'])
    return x, new_state

def setup_inputs(seed: int = 0) -> dict:
    key = jax.random.key(seed)
    ks = jax.random.split(key, 40)
    n_pages = PAST_LEN // PAGE_SIZE
    used = DEC_BATCH * n_pages
    n_pool = used + used // 4

    def nrm(k, shape, scale=1.0):
        return jax.random.normal(k, shape, jnp.float32) * scale

    def gain(k, n):
        return 1.0 + nrm(k, (DEPTH, n), 0.05)

    page_table = jax.random.permutation(ks[0], n_pool)[:used].reshape(DEC_BATCH, n_pages).astype(jnp.int32)
    return {
        'x_prompt': nrm(ks[1], (BATCH, SEQ, D_MODEL)),
        'x_sample': nrm(ks[2], (DEC_BATCH, DEC_SEQ, D_MODEL)),
        'cache_sb_k': nrm(ks[3], (DEPTH, n_pool, PAGE_SIZE, SB_HEADS, SB_DH)),
        'cache_sb_v': nrm(ks[4], (DEPTH, n_pool, PAGE_SIZE, SB_HEADS, SB_DH)),
        'state_gla': nrm(ks[5], (DEPTH, DEC_BATCH, GLA_HEADS, GLA_DK, GLA_DV)),
        'page_table': page_table,
        'p_prompt': nrm(ks[6], (DEPTH, BATCH, SEQ, PLE_DIM)),
        'p_sample': nrm(ks[7], (DEPTH, DEC_BATCH, DEC_SEQ, PLE_DIM)),
        'f1_pre': gain(ks[8], D_MODEL),
        'f1_in': nrm(ks[9], (DEPTH, D_MODEL, 2 * D_FF), D_MODEL ** -0.5),
        'f1_out': nrm(ks[10], (DEPTH, D_FF, D_MODEL), D_FF ** -0.5),
        'f1_post': gain(ks[11], D_MODEL),
        'mix_pre': gain(ks[12], D_MODEL),
        'w_in': nrm(ks[13], (DEPTH, D_MODEL, IN_WIDTH), D_MODEL ** -0.5),
        'gate_w': nrm(ks[14], (DEPTH, GLA_RANK, GLA_QK_W), GLA_RANK ** -0.5),
        'gate_b': nrm(ks[15], (DEPTH, GLA_QK_W), 0.1),
        'gla_norm': gain(ks[16], GLA_DV),
        'sb_norm': gain(ks[17], SB_DH),
        'sb_bias': SB_BIAS_INIT + nrm(ks[28], (DEPTH, SB_HEADS), 0.1),
        'w_out': nrm(ks[18], (DEPTH, MIX_WIDTH, D_MODEL), MIX_WIDTH ** -0.5),
        'mix_post': gain(ks[19], D_MODEL),
        'f2_pre': gain(ks[20], D_MODEL),
        'f2_in': nrm(ks[21], (DEPTH, D_MODEL, 2 * D_FF), D_MODEL ** -0.5),
        'f2_out': nrm(ks[22], (DEPTH, D_FF, D_MODEL), D_FF ** -0.5),
        'f2_post': gain(ks[23], D_MODEL),
        'ple_pre': gain(ks[24], D_MODEL),
        'ple_w_gate': nrm(ks[25], (DEPTH, D_MODEL, D_MODEL), D_MODEL ** -0.5),
        'ple_w_up': nrm(ks[26], (DEPTH, PLE_DIM, D_MODEL), PLE_DIM ** -0.5),
        'ple_post': gain(ks[27], D_MODEL),
    }

def reference(x_prompt, x_sample, cache_sb_k, cache_sb_v, state_gla, page_table, p_prompt, p_sample,
              f1_pre, f1_in, f1_out, f1_post, mix_pre, w_in, gate_w, gate_b, gla_norm, sb_norm, sb_bias,
              w_out, mix_post, f2_pre, f2_in, f2_out, f2_post, ple_pre, ple_w_gate, ple_w_up, ple_post):
    xp, xs = x_prompt, x_sample
    pk_list, pv_list, ps_list, sk_list, sv_list, ss_list = [], [], [], [], [], []
    for l in range(DEPTH):
        lp = {
            'f1_pre': f1_pre[l], 'f1_in': f1_in[l], 'f1_out': f1_out[l], 'f1_post': f1_post[l],
            'mix_pre': mix_pre[l], 'w_in': w_in[l], 'gate_w': gate_w[l], 'gate_b': gate_b[l],
            'gla_norm': gla_norm[l], 'sb_norm': sb_norm[l], 'w_out': w_out[l], 'mix_post': mix_post[l],
            'f2_pre': f2_pre[l], 'f2_in': f2_in[l], 'f2_out': f2_out[l], 'f2_post': f2_post[l],
            'ple_pre': ple_pre[l], 'ple_w_gate': ple_w_gate[l], 'ple_w_up': ple_w_up[l],
            'ple_post': ple_post[l],
        }
        bias_l = sb_bias[l]

        def mix_prompt(gq, gk, gv, la, sq, sk, sv, bias_l=bias_l):
            o_gla, S = gla_prompt(gq, gk, gv, la)
            o_sb = sb_prompt(sq, sk, sv, bias_l)
            return o_gla, o_sb, (sk, sv, S)

        def mix_sample(gq, gk, gv, la, sq, sk, sv, l=l, bias_l=bias_l):
            S, o_gla = gla_chunk_step(state_gla[l].astype(jnp.float32), (gq, gk, gv, la))
            o_sb = sb_sample(sq, sk, sv, cache_sb_k[l], cache_sb_v[l], page_table, bias_l)
            return o_gla, o_sb, (sk, sv, S)

        xp, (pk, pv, ps) = layer(xp, p_prompt[l], lp, mix_prompt)
        xs, (sk_, sv_, ss) = layer(xs, p_sample[l], lp, mix_sample)
        pk_list.append(pk); pv_list.append(pv); ps_list.append(ps)
        sk_list.append(sk_); sv_list.append(sv_); ss_list.append(ss)
    return (xp, xs, jnp.stack(pk_list), jnp.stack(pv_list), jnp.stack(ps_list),
            jnp.stack(sk_list), jnp.stack(sv_list), jnp.stack(ss_list))


_drawn_inputs = setup_inputs


def setup_inputs(seed=0):
    import zlib

    import numpy as np

    out = dict(_drawn_inputs(seed))
    spreads = {}
    factors = {'gla_norm': 3.476,
     'sb_bias': 8.0,
     'f2_pre': 2.957,
     'f2_post': 4.226,
     'ple_pre': 19.1,
     'ple_post': 3.482}
    for name, (base, spread) in spreads.items():
        noise = np.random.default_rng([zlib.crc32(name.encode()), seed]).standard_normal(out[name].shape)
        drawn = base * np.exp(spread * noise) if base else spread * noise
        out[name] = __import__('jax').numpy.asarray(drawn.astype(out[name].dtype))
    for name, factor in factors.items():
        out[name] = (out[name] * factor).astype(out[name].dtype)
    return out
```

```python
from contextlib import ExitStack

import concourse.bass as bass
from concourse import mybir

F32 = mybir.dt.float32
F32R = mybir.dt.float32r
I32 = mybir.dt.int32
U32 = mybir.dt.uint32
ALU = mybir.AluOpType
ACT = mybir.ActivationFunctionType

P = 128
D_MODEL = 1024
SEQ = 512
DEC_BATCH = 8
DEC_SEQ = 4
N_SAMPLE = DEC_BATCH * DEC_SEQ
T = SEQ + N_SAMPLE
HALF = T // 2
KD = D_MODEL // P
D_FF = 2816
N_PAGES = 2
PLE_DIM = 256
GLA_HEADS, GLA_DK, GLA_DV, GLA_RANK = 4, 64, 128, 16
SB_HEADS, SB_DH = 8, 64
EPS = 1e-6
MASKED = -1e30
LOWEST = -87.0
F_TILES = D_FF // P
GROUPS = (12, 10)
G_MAX = max(GROUPS)
SLOT = 8 * 256
LEVELS = 7
CH = 128
N_CH = SEQ // CH

VEC = {"f1_pre": 0, "f1_post": 8, "mix_pre": 16, "mix_post": 24, "f2_pre": 32, "f2_post": 40,
       "ple_pre": 48, "ple_post": 56, "gate_b": 64, "gla_norm": 66, "sb_norm": 67}
N_VEC = 68

GQ, GK, GG, SQ, SK, SV, GV = 0, 2, 4, 8, 12, 16, 20
W_IN_STEPS = [(0, GQ), (256, GK), (1024, GG), (1280, GG + 2),
              (1552, SQ), (1808, SQ + 2), (2064, SK), (2320, SK + 2), (2576, SV), (2832, SV + 2),
              (512, GV), (768, GV + 2)]
GLR_COL = 1536


class Step:

    def __init__(self, c, i=0):
        self.c, self.i = c, i
        self.n = c + 2 * i

    def parity(self, base):
        return (base + self.c) % 2

    def half(self, base):
        return (base + self.c) // 2 + self.i


def steps(eng, first, end, body):
    pairs = (end - first) // 2
    if pairs > 1:
        with eng.Fori(0, pairs) as i:
            body(Step(first, i))
            body(Step(first + 1, i))
    elif pairs:
        body(Step(first))
        body(Step(first + 1))
    if (end - first) % 2:
        body(Step(end - 1))


def plan():
    at, w, t = {}, 0, 0
    parts = [("vectors", 0, 1), ("x", 0, KD)]
    for name in ("f1", "f2"):
        parts += [(f"{name}_up0", GROUPS[0], GROUPS[0] + 1), (f"{name}_down0", KD, KD),
                  (f"{name}_up1", GROUPS[1], GROUPS[1]), (f"{name}_down1", KD, KD), (f"{name}_post", 0, 1)]
        if name == "f1":
            parts += [("in", 13, 14), ("natural", 0, 4), ("merge", 0, KD), ("out", 4, 4), ("p", 0, 2), ("out_post", 0, 1)]
    parts += [("embed", 1, 4), ("gate", 4, 5), ("gate_post", 0, 1), ("y", 0, 5)]
    for name, n_w, n_t in parts:
        at[name] = (w, t)
        w, t = w + n_w, t + n_t
    at["end"] = (w, t)
    return at


def flat(ap):
    return ap.rearrange("p a t -> p (a t)")


def build(nc, a, o):
    at = plan()
    widths = []
    for name in ("f1", "f2"):
        for g in GROUPS:
            widths += [SLOT] * g + [g * P] * KD
        if name == "f1":
            widths += [SLOT] * 12 + [KD * GLA_RANK] + [SLOT] * 4
    widths += [SLOT] * 5
    n_w = at["end"][0]
    assert len(widths) == n_w

    ctx = ExitStack()
    with ctx:
        def sb(name, shape, dt=F32, where=ctx):
            return where.enter_context(nc.sbuf_tensor(name, shape, dt))

        def sem(name):
            return ctx.enter_context(nc.semaphore(name))

        PS = ctx.enter_context(nc.psum_tensor("PS", [P, 8, 512], F32))

        x = sb("x", [P, KD, 2, HALF])
        y = sb("y", [P, KD, 2, HALF])
        raw = sb("raw", [P, 2, SLOT])
        w_hi = sb("w_hi", [P, 2, SLOT], F32R)
        w_lo = sb("w_lo", [P, 2, SLOT], F32R)
        ident = sb("ident", [P, P])
        ones = sb("ones", [P, P])
        tri = sb("tri", [P, P])
        ones64 = sb("ones64", [P, P])
        neg_diag = sb("neg_diag", [P, P])
        level_mask = sb("level_mask", [P, LEVELS, P])
        batch_mask = sb("batch_mask", [P, DEC_BATCH])
        neg_new = sb("neg_new", [N_SAMPLE, DEC_BATCH, DEC_SEQ])
        scan_keep = sb("scan_keep", [P, N_SAMPLE])
        eps = sb("eps", [P, 1])
        vec_rows = sb("vec_rows", [N_VEC, P])
        vec = sb("vec", [P, N_VEC])
        bias_row = sb("bias_row", [1, SB_HEADS])
        bias = sb("bias", [P, SB_HEADS])
        gate_w = sb("gate_w", [GLA_RANK, 2 * P])
        table = sb("table", [1, DEC_BATCH * N_PAGES], I32)
        sum_sq = sb("sum_sq", [P, T])
        sq = sb("sq", [P, 2, T])
        rstd = sb("rstd", [P, 2, 2, HALF])
        work = sb("work", [P, 2, T])
        glr = sb("glr", [GLA_RANK, 2, HALF])
        with nc.sbuf_tensor("p_hi", [P, 2, T], F32R) as p_hi, nc.sbuf_tensor("p_lo", [P, 2, T], F32R) as p_lo:
            pass
        extra = sb("extra", [P, 3 * 1280])
        with nc.sbuf_tensor("a_hi", [P, KD, T], F32R) as a_hi, nc.sbuf_tensor("a_lo", [P, KD, T], F32R) as a_lo:
            pass
        with ExitStack() as s:
            k_nat = sb("k_nat", [P, N_CH, 512], F32, s)
            v_nat = sb("v_nat", [P, N_CH, 512], F32, s)
            gv_nat = sb("gv_nat", [P, N_CH, 512], F32, s)
            new_nat = sb("new_nat", [N_SAMPLE, 3, 512], F32, s)
            state = sb("state", [P, N_CH, P], F32, s)
            kl_new = sb("kl_new", [N_SAMPLE, P], F32, s)
            decay_last = sb("decay_last", [P, N_CH + DEC_BATCH], F32, s)
        hold_a = sb("hold_a", [P, 2 * KD * T])
        with nc.sbuf_tensor("h_hi", [P, G_MAX, T], F32R) as h_hi, nc.sbuf_tensor("h_lo", [P, G_MAX, T], F32R) as h_lo:
            pass
        with nc.sbuf_tensor("proj", [P, 24, 2, HALF], F32) as proj:
            pass
        with nc.sbuf_tensor("rows", [P, 5, D_MODEL], F32) as rows, nc.sbuf_tensor("e", [P, KD, 2, HALF], F32) as e:
            pass
        hold_h = sb("hold_h", [P, 2 * G_MAX * T])

        def scratch(owner, at_, shape):
            n = 1
            for s_ in shape[1:]:
                n *= s_
            v = owner[0:shape[0], at_:at_ + n]
            if len(shape) == 3:
                return v.rearrange("p (a b) -> p a b", a=shape[1])
            if len(shape) == 4:
                return v.rearrange("p (a b c) -> p a b c", a=shape[1], b=shape[2])
            return v

        work_flat = work[:].rearrange("p a t -> p (a t)")
        gs = scratch(work_flat, 0, [P, 2, HALF])
        us = scratch(work_flat, T, [P, 2, HALF])
        es = sq[:, 0, :].rearrange("p (a t) -> p a t", a=2)
        dead = proj[:, SV:SV + 8].rearrange("p k a t -> p (k a t)")
        extra_flat = extra[:]

        sb_z = [scratch(dead, 1280 * n, [P, 1280]) for n in range(2)]
        sb_s = [scratch(dead, 2560, [P, 1280]), scratch(extra_flat, 0, [P, 1280])]
        sb_w = [scratch(extra_flat, 1280 * n, [P, 1280]) for n in (1, 2)]
        k_page = scratch(dead, 0, [P, 4, 512])
        k_turned = scratch(dead, 2048, [P, 2, 512])
        q_block = scratch(dead, 3072, [P, 4, DEC_BATCH, 8])
        bias_cols = scratch(dead, 3328, [P, 4, DEC_BATCH, 8])
        neg_cols = scratch(dead, 3584, [N_SAMPLE, 4, DEC_BATCH, 8])
        z_new = scratch(dead, 3840, [N_SAMPLE, 256])
        z_past = scratch(extra_flat, 0, [P, 512])
        s_past = scratch(extra_flat, 512, [P, 512])
        w_past = scratch(extra_flat, 1024, [P, 512])
        v_page = scratch(extra_flat, 1536, [P, 4, 512])
        s_new = scratch(extra_flat, 3584, [N_SAMPLE, 256])
        w_new = scratch(dead, 4096, [N_SAMPLE, 256])
        att = scratch(dead, 0, [P, 8, P])
        state_new = scratch(dead, 1024, [P, DEC_BATCH, P])
        state_old = scratch(dead, 2048, [P, DEC_BATCH, P])
        kl_batch = scratch(dead, 3072, [N_SAMPLE, DEC_BATCH, P])
        q_new = scratch(dead, 4096, [P, DEC_BATCH, 2, DEC_SEQ])
        att_new = scratch(dead, 4160, [N_SAMPLE, 2, N_SAMPLE])
        inter_new = scratch(dead, 4224, [P, DEC_BATCH, 2, DEC_SEQ])
        decay = [scratch(extra_flat, T * n, [P, T]) for n in (0, 1)]
        q_lev = [scratch(extra_flat, T * n, [P, T]) for n in (2, 3)]
        k_lev = [scratch(extra_flat, T * n, [P, T]) for n in (4, 5)]
        kl_nat = scratch(extra_flat, 6 * T, [P, N_CH, P])
        cum = scratch(work_flat, 0, [P, 2, T])
        la_raw, la_soft = rstd[:, 0].rearrange("p a t -> p (a t)"), sum_sq[:]
        q_dec, kl = sq[:, 0, :], sq[:, 1, :]

        names = """vec_in x_in table_in page_in0 page_in1 page_in2 page_in3 vpage_in0 vpage_in1 vpage_in2 vpage_in3
            state_in p_in raw_in0 raw_in1 out_done ident_made ones_made masks_made pool_step
            split_hi split_lo psum_full psum_free0 psum_free1 vec_ready bias_ready
            a_hi_ready a_lo_ready sq_ready sq_used sum_ready rstd_ready log_ready
            upd_ready x_ready g_ready exp_ready den_ready sig_ready silu_ready h_raw h_hi_ready h_lo_ready
            p_hi_ready p_lo_ready glr_ready
            z_full z_out z_masked abs_ready e_ready soft_log sp_ready c_full d_ready w_ready o_full o_out
            setup_new kt_full kt_out zs_full zs_out n_out
            la_full la_sum la_abs la_log la_soft_ready cum_ready
            eb_ready qe_ready kl_diff kl_exp kl_ready klt_full klt_out klb_ready last_ready
            lev_diff lev_exp lev_q lev_k lev_full att_out u_full state_ready
            og_full og_out inter_full inter_out on_full on_out sn_full sn_decayed sn_out
            qz_ready nat_stored state_stored new_stored m_mid pg_ready pg_exp pg_den pg_rec pg_out row_out g_held gg_held gg_exp gg_den gg_rec gg_ready m_sq m_norm m_ready rows_out""".split()
        sig = {n: sem(n) for n in names}
        raw_in = [sig["raw_in0"], sig["raw_in1"]]
        psum_free = [sig["psum_free0"], sig["psum_free1"]]
        page_in = [sig[f"page_in{n}"] for n in range(4)]
        vpage_in = [sig[f"vpage_in{n}"] for n in range(4)]

        W0 = {n: v[0] for n, v in at.items()}
        T0 = {n: v[1] for n, v in at.items()}
        NORMS = ["f1_pre", "f1_post", "mix_pre", "mix_post", "f2_pre", "f2_post", "ple_pre", "ple_post"]
        sum_ticket = [T0["f1_up0"] + 1, T0["f1_post"], T0["in"] + 1, T0["out_post"], T0["f2_up0"] + 1,
                      T0["f2_post"], T0["gate"] + 1, T0["gate_post"]]

        def banks(quad, first, n):
            return PS[:, 4 * quad + first:4 * quad + first + n, 0:HALF]

        def full(eng, t, quad_free=None):
            eng.wait_ge(sig["psum_full"], t + 1)

        def ticket(st, name):
            base = T0[name]
            if name in ("f1_up0", "f2_up0", "in", "gate") and st.c >= 1:
                base += 1
            return base + st.n, st.parity(base), st.half(base)

        block = ctx.enter_context(nc.Block())

        @block.sync
        def _(sp):
            def load(w, slot, parts, wait=True):
                if wait:
                    sp.wait_ge(sig["split_lo"], w - 1)
                for dst, src in parts:
                    sp.dma_start(dst, src).then_inc(raw_in[slot], 16)

            def up(name, g0):
                src = a[f"{name}_in"][0].rearrange("(k p) n -> p k n", p=P)

                def parts(st, slot):
                    dst = raw[:, slot, :].rearrange("p (k c n) -> p k c n", k=KD, c=2)
                    return [(dst[:, :, c, :], src[:, :, bass.ds(c * D_FF + (g0 + st.n) * P, P)]) for c in range(2)]
                return parts

            def down(name, g0, g):
                src = a[f"{name}_out"][0].rearrange("(f p) n -> p f n", p=P)

                def parts(st, slot):
                    dst = raw[:, slot, 0:g * P].rearrange("p (k n) -> p k n", k=g)
                    return [(dst[:, c * g // 2:(c + 1) * g // 2, :],
                             src[:, g0 + c * g // 2:g0 + (c + 1) * g // 2, bass.ds(st.n * P, P)]) for c in range(2)]
                return parts

            def wide(src, col, n=256):
                def parts(st, slot):
                    dst = raw[:, slot, 0:KD * n].rearrange("p (k n) -> p k n", k=KD)
                    v = src.rearrange("(k p) n -> p k n", p=P)
                    return [(dst[:, 4 * c:4 * c + 4, :], v[:, 4 * c:4 * c + 4, bass.ds(col(st), n)]) for c in range(2)]
                return parts

            def stage(name, n, parts, first=0):
                w0 = W0[name]
                steps(sp, first, n, lambda st: load(w0 + st.n, st.parity(w0), parts(st, st.parity(w0))))

            def pages():
                sp.wait_ge(sig["table_in"], 16)
                sp.wait_ge(sig["o_full"], SB_HEADS)
                sp.wait_ge(sig["d_ready"], SB_HEADS)
                page_no = [sp.value_load(table[0:1, j:j + 1], min_val=0, max_val=a["cache_sb_k"].shape[1] - 1)
                           for j in range(DEC_BATCH * N_PAGES)]
                for ring, cache, landed, used in ((k_page, a["cache_sb_k"], page_in, sig["kt_full"]),
                                                  (v_page, a["cache_sb_v"], vpage_in, sig["n_out"])):
                    for j in range(DEC_BATCH * N_PAGES):
                        if j >= 4:
                            sp.wait_ge(used, j - 3)
                        sp.dma_start(ring[:, j % 4, :], cache[0, bass.ds(page_no[j], 1)].rearrange(
                            "a s h d -> s (a h d)")).then_inc(landed[j % 4], 16)

            sp.dma_start(table[:], a["page_table"].rearrange("b n -> (b n)").unsqueeze(0)).then_inc(sig["table_in"], 16)
            for n in range(5):
                rows_n = P if n < 4 else N_SAMPLE
                src = a["x_prompt"][0, n * P:(n + 1) * P, :] if n < 4 else a["x_sample"].rearrange("b t d -> (b t) d")
                sp.dma_start(rows[0:rows_n, n, :], src).then_inc(sig["x_in"], 16)

            first = up("f1", 0)
            for n in range(2):
                load(n, n, first(Step(n), n), wait=False)
            stage("f1_up0", GROUPS[0], first, first=2)
            for name in ("f1", "f2"):
                if name == "f2":
                    stage("f2_up0", GROUPS[0], up(name, 0))
                stage(f"{name}_down0", KD, down(name, 0, GROUPS[0]))
                stage(f"{name}_up1", GROUPS[1], up(name, GROUPS[0]))
                stage(f"{name}_down1", KD, down(name, GROUPS[0], GROUPS[1]))
                if name == "f1":
                    for s_, (col, _t) in enumerate(W_IN_STEPS):
                        w = W0["in"] + s_
                        load(w, w % 2, wide(a["w_in"][0], lambda st: col)(None, w % 2))
                    w = W0["in"] + 12
                    load(w, w % 2, wide(a["w_in"][0], lambda st: GLR_COL, GLA_RANK)(None, w % 2))
                    out_parts = wide(a["w_out"][0], lambda st: st.n * 256)
                    for n in range(2):
                        w = W0["out"] + n
                        load(w, w % 2, out_parts(Step(n), w % 2))
                    pages()
                    stage("out", 4, out_parts, first=2)
            w = W0["embed"]
            up_w = a["ple_w_up"][0].rearrange("(k p) n -> p k n", p=P)
            load(w, w % 2, [(raw[:, w % 2, k * D_MODEL:(k + 1) * D_MODEL], up_w[:, k, :]) for k in range(2)])
            stage("gate", 4, wide(a["ple_w_gate"][0], lambda st: st.n * 256))
            for n in range(5):
                t = T0["y"] + n
                sp.wait_ge(psum_free[t % 2], t // 2 + 1)
                dst = o[0][0, n * P:(n + 1) * P, :] if n < 4 else o[1].rearrange("b t d -> (b t) d")
                sp.dma_start(dst, rows[0:P if n < 4 else N_SAMPLE, n, :]).then_inc(sig["out_done"], 16)
            sp.wait_ge(sig["out_done"], 16 * 5)
            sp.wait_ge(sig["nat_stored"], 16 * 4)
            sp.wait_ge(sig["state_stored"], 16 * 2)
            sp.wait_ge(sig["new_stored"], 16 * 2)

        @block.tensor
        def _(pe):
            mm = nc.tensor.matmul

            def open_ticket(t, quad, use):
                pe.wait_ge(psum_free[quad], use)

            def open_t(t):
                open_ticket(t, t % 2, t // 2)

            def weights(w):
                pe.wait_ge(sig["split_lo"], w + 1)

            def dense(quad, slot, tiles, n_k, rhs, ready=None, stride=None, width=P):
                stride = stride or tiles * width
                for k in range(n_k):
                    if ready:
                        ready(k)
                    for c in range(tiles):
                        cols = slice(k * stride + c * width, k * stride + (c + 1) * width)
                        for n, (wt, act) in enumerate(((w_hi, rhs[0]), (w_hi, rhs[1]), (w_lo, rhs[0]))):
                            for half in range(2):
                                last = mm(PS[0:width, 4 * quad + 2 * c + half, 0:HALF], wt[:, slot, cols],
                                          act[:, k, half * HALF:(half + 1) * HALF],
                                          start=(k == 0 and n == 0), stop=(k == n_k - 1 and n == 2))
                return last

            def sum_norm(j):
                t = sum_ticket[j]
                open_t(t)
                pe.wait_ge(sig["sq_used"], 8 * (j + 1))
                for half in range(2):
                    last = mm(PS[:, 4 * (t % 2) + half, 0:HALF], ones[:], sum_sq[:, half * HALF:(half + 1) * HALF],
                              start=True, stop=True)
                last.then_inc(sig["psum_full"], 1)

            def product(name, n, tiles, n_k, rhs, ready=None, norm=None):
                def body(st, ready=None):
                    t, quad, use = ticket(st, name)
                    weights(W0[name] + st.n)
                    open_ticket(t, quad, use)
                    dense(quad, st.parity(W0[name]), tiles, n_k, rhs, ready).then_inc(sig["psum_full"], 1)
                body(Step(0), ready)
                if norm is not None:
                    sum_norm(norm)
                steps(pe, 1, n, body)

            A = (a_hi, a_lo)
            H = (h_hi, h_lo)

            def a_tiles(stage_no):
                return lambda k: pe.wait_ge(sig["a_lo_ready"], 8 * stage_no + k + 1)

            def h_tiles(first):
                return lambda k: pe.wait_ge(sig["h_lo_ready"], first + k + 1)

            def ffn(name, stage_no, first, norm):
                product(f"{name}_up0", GROUPS[0], 2, KD, A, a_tiles(stage_no), norm)
                product(f"{name}_down0", KD, 1, GROUPS[0], H, h_tiles(first))
                product(f"{name}_up1", GROUPS[1], 2, KD, A)
                product(f"{name}_down1", KD, 1, GROUPS[1], H, h_tiles(first + GROUPS[0]))
                sum_norm(norm + 1)

            pe.wait_ge(sig["masks_made"], 1)
            pe.wait_ge(sig["vec_in"], 16 * 14)
            nc.tensor.transpose(PS[:, 0, 0:N_VEC], vec_rows[:], ident[0:N_VEC, 0:N_VEC])
            mm(PS[:, 1, 0:SB_HEADS], ones[0:1, :], bias_row[:], start=True, stop=True).then_inc(sig["psum_full"], 1)
            pe.wait_ge(sig["x_in"], 16 * 5)
            for k in range(KD):
                t = T0["x"] + k
                open_t(t)
                for n in range(4):
                    nc.tensor.transpose(PS[:, 4 * (t % 2), n * P:(n + 1) * P], rows[:, n, k * P:(k + 1) * P], ident[:])
                nc.tensor.transpose(PS[:, 4 * (t % 2) + 1, 0:N_SAMPLE], rows[0:N_SAMPLE, 4, k * P:(k + 1) * P],
                                    ident[0:N_SAMPLE, 0:N_SAMPLE]).then_inc(sig["psum_full"], 1)
            ffn("f1", 0, 0, 0)

            product("in", 12, 2, KD, A, a_tiles(1), 2)
            st = Step(12)
            t, quad, use = ticket(st, "in")
            weights(W0["in"] + 12)
            open_ticket(t, quad, use)
            dense(quad, st.parity(W0["in"]), 1, KD, A, width=GLA_RANK).then_inc(sig["psum_full"], 1)

            for n, tile in enumerate((SK, SV, GV)):
                t = T0["natural"] + n
                open_t(t)
                for c in range(N_CH):
                    for f in range(4):
                        last = nc.tensor.transpose(PS[:, 4 * (t % 2) + c, f * P:(f + 1) * P],
                                                   flat(proj[:, tile + f])[:, c * P:(c + 1) * P], ident[:])
                last.then_inc(sig["psum_full"], 1)
            t = T0["natural"] + 3
            open_t(t)
            for n, tile in enumerate((SK, SV, GV)):
                for f in range(4):
                    last = nc.tensor.transpose(PS[0:N_SAMPLE, 4 * (t % 2) + n, f * P:(f + 1) * P],
                                               flat(proj[:, tile + f])[:, SEQ:T], ident[:])
            last.then_inc(sig["psum_full"], 1)

            for quad in range(2):
                pe.wait_ge(psum_free[quad], (T0["merge"] + 1 - quad) // 2)

            def prompt_z(h):
                r, p = slice(64 * (h % 2), 64 * (h % 2) + 64), h // 2
                k_, q_ = flat(proj[:, SK + p]), flat(proj[:, SQ + p])
                pe.wait_ge(sig["z_out"], h)
                for j in range(4):
                    mm(PS[:, 0, j * P:(j + 1) * P], k_[r, j * P:(j + 1) * P], q_[r, j * P:(j + 1) * P],
                       start=True, stop=True)
                mm(PS[:, 1, 0:384], k_[r, 0:P], q_[r, P:SEQ], start=True, stop=True)
                mm(PS[:, 2, 0:256], k_[r, P:2 * P], q_[r, 2 * P:SEQ], start=True, stop=True)
                mm(PS[:, 2, 256:384], k_[r, 2 * P:3 * P], q_[r, 3 * P:SEQ], start=True,
                   stop=True).then_inc(sig["z_full"], 1)

            def prompt_sums(h):
                s_ = sb_s[h % 2]
                pe.wait_ge(sig["sp_ready"], h + 1)
                pe.wait_ge(sig["d_ready"], h)
                mm(PS[:, 4, :], tri[:], s_[:, 0:512], start=True, stop=True)
                mm(PS[:, 5, 0:384], tri[:], s_[:, 512:896], start=True, stop=False)
                mm(PS[:, 5, 0:384], ones[:], s_[:, 128:512], start=False, stop=False)
                mm(PS[:, 5, 128:384], ones[:], s_[:, 896:1152], start=False, stop=False)
                mm(PS[:, 5, 256:384], ones[:], s_[:, 1152:1280], start=False, stop=True)
                mm(PS[:, 6, 0:384], tri[:], s_[:, 896:1280], start=True, stop=False)
                mm(PS[:, 6, 0:256], ones[:], s_[:, 256:512], start=False, stop=False)
                mm(PS[:, 6, 128:256], ones[:], s_[:, 1152:1280], start=False, stop=False)
                mm(PS[:, 6, 256:384], ones[:], s_[:, 384:512], start=False, stop=True).then_inc(sig["c_full"], 1)

            def prompt_out(h):
                r, bank, w_ = slice(64 * (h % 2), 64 * (h % 2) + 64), 3 + 4 * (h % 2), sb_w[h % 2]
                pe.wait_ge(sig["w_ready"], h + 1)
                if h >= 2:
                    pe.wait_ge(sig["o_out"], h - 1)
                out, off = PS[r, bank], [512, 896, 1152]
                for j in range(4):
                    v_ = v_nat[:, j, h * SB_DH:(h + 1) * SB_DH]
                    last = mm(out[:, j * P:(j + 1) * P], v_, w_[:, j * P:(j + 1) * P], start=(j == 0), stop=(j in (0, 3)))
                    if j < 3:
                        n = (3 - j) * P
                        mm(out[:, (j + 1) * P:SEQ], v_, w_[:, off[j]:off[j] + n], start=(j == 0), stop=False)
                last.then_inc(sig["o_full"], 1)

            prompt_z(0)
            for h in range(SB_HEADS):
                if h + 1 < SB_HEADS:
                    prompt_z(h + 1)
                prompt_sums(h)
                if h >= 1:
                    prompt_out(h - 1)
            prompt_out(SB_HEADS - 1)

            pe.wait_ge(sig["setup_new"], 1)
            pe.wait_ge(sig["d_ready"], SB_HEADS)

            def turn_page(j):
                pe.wait_ge(page_in[j % 4], 16 * (j // 4 + 1))
                if j >= 2:
                    pe.wait_ge(sig["kt_out"], j - 1)
                for f in range(4):
                    last = nc.tensor.transpose(PS[:, 4 + j % 2, f * P:(f + 1) * P],
                                               k_page[:, j % 4, f * P:(f + 1) * P], ident[:])
                last.then_inc(sig["kt_full"], 1)

            n_pages = DEC_BATCH * N_PAGES
            turn_page(0)
            for j in range(n_pages):
                if j + 1 < n_pages:
                    turn_page(j + 1)
                pe.wait_ge(sig["kt_out"], j + 1)
                b, pg = j // N_PAGES, j % N_PAGES
                for p in range(4):
                    col = pg * 256 + p * 64 + b * 8
                    last = mm(PS[:, 6, col:col + 8], k_turned[:, j % 2, p * P:(p + 1) * P], q_block[:, p, b, :],
                              start=True, stop=True)
            pe.wait_ge(sig["o_out"], SB_HEADS)
            for p in range(4):
                last = mm(PS[0:N_SAMPLE, 7, p * 64:(p + 1) * 64], flat(proj[:, SK + p])[:, SEQ:T],
                          q_block[:, p].rearrange("p b n -> p (b n)"), start=True, stop=True)
            last.then_inc(sig["zs_full"], 1)
            pe.wait_ge(sig["sp_ready"], SB_HEADS + 2)
            new = slice(0, N_SAMPLE)
            mm(PS[:, 0, :], tri[:], s_past, start=True, stop=False)
            mm(PS[:, 0, 0:256], ones[:], s_past[:, 256:512], start=False, stop=False)
            mm(PS[:, 0, 0:256], ones[new, :], s_new, start=False, stop=False)
            mm(PS[:, 0, 256:512], ones[new, :], s_new, start=False, stop=True)
            mm(PS[new, 1, 0:256], tri[new, new], s_new, start=True, stop=True).then_inc(sig["c_full"], 1)
            pe.wait_ge(sig["w_ready"], SB_HEADS + 2)
            for p in range(4):
                mm(PS[:, 2 + p, 0:64], new_nat[:, 1, p * P:(p + 1) * P], w_new[:, p * 64:(p + 1) * 64],
                   start=True, stop=False)
            for j in range(n_pages):
                b, pg = j // N_PAGES, j % N_PAGES
                pe.wait_ge(vpage_in[j % 4], 16 * (j // 4 + 1))
                for p in range(4):
                    col = p * 64 + b * 8
                    last = mm(PS[:, 2 + p, b * 8:b * 8 + 8], v_page[:, j % 4, p * P:(p + 1) * P],
                              w_past[:, pg * 256 + col:pg * 256 + col + 8], start=False, stop=(j == n_pages - 1))
                last.then_inc(sig["n_out"], 1)

            pe.wait_ge(sig["on_out"], 1)
            for p in range(2):
                for half in range(2):
                    last = mm(PS[:, 2 * p + half, 0:HALF], gate_w[:, p * P:(p + 1) * P], glr[:, half],
                              start=True, stop=True)
                last.then_inc(sig["la_full"], 1)
            pe.wait_ge(sig["la_sum"], 2)
            for p in range(2):
                n_att = (LEVELS + 1) * p
                if p:
                    pe.wait_ge(sig["sn_out"], p)
                    pe.wait_ge(sig["og_out"], 2 * p)
                    pe.wait_ge(sig["on_out"], 1 + p)
                pe.wait_ge(sig["kl_ready"], p + 1)
                for c in range(N_CH):
                    nc.tensor.transpose(PS[:, 6, c * P:(c + 1) * P], kl[:, c * P:(c + 1) * P], ident[:])
                nc.tensor.transpose(PS[0:N_SAMPLE, 7, 0:P], kl[:, SEQ:T], ident[:]).then_inc(sig["klt_full"], 1)
                for li in range(LEVELS + 1):
                    if li == 0:
                        q_, k_ = flat(proj[:, GQ + p]), flat(proj[:, GK + p])
                    else:
                        q_, k_ = q_lev[li % 2], k_lev[li % 2]
                        pe.wait_ge(sig["lev_q"], LEVELS * p + li)
                        pe.wait_ge(sig["lev_k"], LEVELS * p + li)
                    if li in (1, 2):
                        pe.wait_ge(sig["att_out"], n_att + li)
                    elif n_att + li >= 2:
                        pe.wait_ge(sig["att_out"], n_att + li - 1)
                    b0 = 2 * (li % 2)
                    for hh in range(2):
                        r = slice(64 * hh, 64 * hh + 64)
                        for c in range(N_CH):
                            tok = slice(c * P, (c + 1) * P)
                            last = mm(PS[:, b0 + hh, tok], k_[r, tok], q_[r, tok], start=True, stop=True)
                        if li <= 2:
                            last = mm(PS[0:N_SAMPLE, 4 + hh, 0:N_SAMPLE],
                                      k_[r, SEQ:T], q_[r, SEQ:T], start=True, stop=True)
                    last.then_inc(sig["lev_full"], 1)
                pe.wait_ge(sig["klt_out"], p + 1)
                pe.wait_ge(sig["att_out"], n_att + LEVELS + 1)
                for hh in range(2):
                    h = 2 * p + hh
                    for c in range(N_CH):
                        last = mm(PS[64 * hh:64 * hh + 64, 5, c * P:(c + 1) * P],
                                  kl_nat[:, c, 64 * hh:64 * hh + 64], gv_nat[:, c, h * P:(h + 1) * P],
                                  start=True, stop=True)
                last.then_inc(sig["u_full"], 1)
                pe.wait_ge(sig["state_ready"], N_CH * (p + 1))
                pe.wait_ge(sig["qe_ready"], 2 * (p + 1))
                for hh in range(2):
                    h, r = 2 * p + hh, slice(64 * hh, 64 * hh + 64)
                    for c in range(N_CH):
                        tok = slice(c * P, (c + 1) * P)
                        last = mm(PS[:, hh, tok], gv_nat[:, c, h * P:(h + 1) * P], att[:, hh * N_CH + c, :],
                                  start=True, stop=(c == 0))
                        if c:
                            last = mm(PS[:, hh, tok], state[r, c - 1, :], q_dec[r, tok], start=False, stop=True)
                    last.then_inc(sig["og_full"], 1)
                pe.wait_ge(sig["state_in"], 16 * (p + 1))
                for b in range(DEC_BATCH):
                    last = mm(PS[:, 2, b * 8:b * 8 + 8], state_old[:, b, :],
                              q_new[:, b].rearrange("p h t -> p (h t)"), start=True, stop=True)
                last.then_inc(sig["inter_full"], 1)
                for hh in range(2):
                    h = 2 * p + hh
                    last = mm(PS[:, 3, hh * N_SAMPLE:(hh + 1) * N_SAMPLE], new_nat[:, 2, h * P:(h + 1) * P],
                              att_new[:, hh, :], start=True, stop=True)
                last.then_inc(sig["on_full"], 1)
                pe.wait_ge(sig["klb_ready"], p + 1)
                for b in range(DEC_BATCH):
                    last = mm(PS[:, [6, 7, 4, 5][b // 2], (b % 2) * 256:(b % 2) * 256 + 256], kl_batch[:, b, :],
                              new_nat[:, 2, p * 256:(p + 1) * 256], start=True, stop=True)
                last.then_inc(sig["sn_full"], 1)

            pe.wait_ge(sig["sn_out"], 2)
            pe.wait_ge(sig["og_out"], 4)
            pe.wait_ge(sig["on_out"], 3)
            for i in range(KD):
                t = T0["merge"] + i
                open_t(t)
                pe.wait_ge(sig["m_sq"], i + 1)
                for half in range(2):
                    last = mm(PS[:, 4 * (t % 2) + half, 0:HALF], (ones if i < 4 else ones64)[:],
                              sq[:, i % 2, half * HALF:(half + 1) * HALF], start=True, stop=True)
                last.then_inc(sig["psum_full"], 1)
            product("out", 4, 2, KD, A, a_tiles(2))
            pe.wait_ge(sig["p_in"], 16 * 5)
            for k in range(2):
                t = T0["p"] + k
                open_t(t)
                for n in range(4):
                    nc.tensor.transpose(PS[:, 4 * (t % 2), n * P:(n + 1) * P], rows[:, n, k * P:(k + 1) * P], ident[:])
                nc.tensor.transpose(PS[:, 4 * (t % 2) + 1, 0:N_SAMPLE], rows[0:N_SAMPLE, 4, k * P:(k + 1) * P],
                                    ident[0:N_SAMPLE, 0:N_SAMPLE]).then_inc(sig["psum_full"], 1)
            sum_norm(3)
            ffn("f2", 3, F_TILES, 4)
            w = W0["embed"]
            weights(w)
            for s_ in range(4):
                t = T0["embed"] + s_
                open_t(t)
                for k in range(2):
                    for c in range(2):
                        for n, (wt, act) in enumerate(((w_hi, p_hi), (w_hi, p_lo), (w_lo, p_hi))):
                            for half in range(2):
                                col = k * D_MODEL + (2 * s_ + c) * P
                                last = mm(PS[:, 4 * (t % 2) + 2 * c + half, 0:HALF], wt[:, w % 2, col:col + P],
                                          act[:, k, half * HALF:(half + 1) * HALF],
                                          start=(k == 0 and n == 0), stop=(k == 1 and n == 2))
                last.then_inc(sig["psum_full"], 1)
            product("gate", 4, 2, KD, A, a_tiles(4), 6)
            sum_norm(7)
            for n in range(5):
                t = T0["y"] + n
                open_t(t)
                if n == 0:
                    pe.wait_ge(sig["x_ready"], 8 * 4)
                m = P if n < 4 else N_SAMPLE
                for k in range(KD):
                    last = nc.tensor.transpose(PS[0:m, 4 * (t % 2) + k // 4, (k % 4) * P:(k % 4 + 1) * P],
                                               flat(x[:, k])[:, n * P:n * P + m], ident[:])
                last.then_inc(sig["psum_full"], 1)

        up_base = {"f1_up0": 0, "f1_up1": GROUPS[0], "f2_up0": F_TILES, "f2_up1": F_TILES + GROUPS[0]}
        h_slot = lambda name: 0

        @block.scalar
        def _(act):
            fn = nc.scalar.activation

            def split(st, name, t):
                nxt, w0 = Step(st.c + 1, st.i), W0[name]
                slot, width = nxt.parity(w0), widths[w0 + st.c + 1]
                act.wait_ge(raw_in[slot], 32 * (nxt.half(w0) + 1))
                act.wait_ge(sig["psum_full"], t)
                fn(w_hi[:, slot, 0:width], raw[:, slot, 0:width], ACT.Copy).then_inc(sig["split_hi"], 1)

            def norm(j):
                t, r = sum_ticket[j], rstd[:, j % 2]
                full(act, t)
                fn(r, banks(t % 2, 0, 2), ACT.Ln, bias=eps[:], scale=1.0 / D_MODEL).then_inc(psum_free[t % 2], 1)
                act.wait_ge(psum_free[t % 2], t // 2 + 1)
                fn(r, r, ACT.Exp, scale=-0.5).then_inc(sig["rstd_ready"], 1)

            def square(j, k, src):
                n = 8 * j + k
                if n >= 2:
                    act.wait_ge(sig["sq_used"], n - 1)
                fn(sq[:, k % 2, :], src, ACT.Square).then_inc(sig["sq_ready"], 1)

            def input_tile(k, name, j):
                c = VEC[name] + k
                fn(a_hi[:, k, :], flat(x[:, k]), ACT.Copy, scale=vec[:, c:c + 1]).then_inc(sig["a_hi_ready"], 1)
                square(j, k, flat(x[:, k]))

            def boundary(b, name, j):
                for k in range(KD):
                    act.wait_ge(sig["x_ready"], 8 * b + k + 1)
                    input_tile(k, name, j)

            def stage(name, n, body, after_first=None):
                def one(st):
                    t, quad, use = ticket(st, name)
                    if W0[name] + st.c + 1 < n_w:
                        split(st, name, t)
                    if st.c == 0 and after_first is not None:
                        norm(after_first)
                    body(st, t, quad, use)
                one(Step(0))
                steps(act, 1, n - 1, one)
                one(Step(n - 1))

            def up(name):
                base = up_base[name]
                h0 = base % F_TILES

                def body(st, t, quad, use):
                    n = base + st.n
                    act.wait_ge(sig["g_held"], n + 1)
                    fn(es, es, ACT.Exp, scale=-1.0).then_inc(sig["exp_ready"], 1)
                    act.wait_ge(sig["exp_ready"], n + 1)
                    fn(es, es, ACT.Identity, bias=1.0).then_inc(sig["den_ready"], 1)
                    act.wait_ge(sig["h_raw"], n + 1)
                    fn(h_hi[:, bass.ds(st.n, 1), :].rearrange("p a t -> p (a t)"), flat(us),
                       ACT.Copy).then_inc(sig["h_hi_ready"], 1)
                return body

            def down0(st, t, quad, use):
                full(act, t)
                fn(y[:, bass.ds(st.n, 1)].rearrange("p k a t -> p (k a) t"), banks(quad, 0, 2),
                   ACT.Copy).then_inc(psum_free[quad], 1)

            def down1(j):
                def body(st, t, quad, use):
                    act.wait_ge(psum_free[quad], use + 1)
                    n = 8 * j + st.n
                    act.wait_ge(sig["sq_used"], n - 1)
                    fn(sq[:, st.parity(0), :], y[:, bass.ds(st.n, 1)].rearrange("p k a t -> p (k a t)"),
                       ACT.Square).then_inc(sig["sq_ready"], 1)
                return body

            def ffn(name, j):
                stage(f"{name}_up0", GROUPS[0], up(f"{name}_up0"), after_first=j)
                stage(f"{name}_down0", KD, down0)
                stage(f"{name}_up1", GROUPS[1], up(f"{name}_up1"))
                stage(f"{name}_down1", KD, down1(j + 1))
                norm(j + 1)

            nc.scalar.preload_act_table_set("natural_log_exp_and_others")
            for name in NORMS:
                act.dma_start(vec_rows[VEC[name]:VEC[name] + 8, :],
                              a[name][0].rearrange("(k p) -> k p", p=P)).then_inc(sig["vec_in"], 16)
            act.dma_start(vec_rows[64:66, :], a["gate_b"][0].rearrange("(k p) -> k p", p=P)).then_inc(sig["vec_in"], 16)
            act.dma_start(vec_rows[66:67, :], a["gla_norm"]).then_inc(sig["vec_in"], 16)
            for n in range(2):
                act.dma_start(vec_rows[67:68, n * 64:(n + 1) * 64], a["sb_norm"]).then_inc(sig["vec_in"], 16)
            act.dma_start(bias_row[:], a["sb_bias"]).then_inc(sig["vec_in"], 16)
            act.dma_start(gate_w[:], a["gate_w"][0]).then_inc(sig["vec_in"], 16)

            act.wait_ge(raw_in[0], 32)
            fn(w_hi[:, 0, :], raw[:, 0, :], ACT.Copy).then_inc(sig["split_hi"], 1)
            act.wait_ge(sig["vec_ready"], 3)
            for k in range(KD):
                t = T0["x"] + k
                act.wait_ge(psum_free[t % 2], t // 2 + 1)
                input_tile(k, "f1_pre", 0)
            ffn("f1", 0)
            boundary(0, "mix_pre", 2)
            stage("in", 13, lambda st, t, quad, use: None, after_first=2)

            for n, dst in ((0, k_nat), (2, gv_nat)):
                t = T0["natural"] + n
                full(act, t)
                fn(dst[:], PS[:, 4 * (t % 2):4 * (t % 2) + 4, :], ACT.Copy).then_inc(psum_free[t % 2], 1)

            act.wait_ge(sig["psum_full"], T0["merge"])

            def logits(h):
                z_ = sb_z[h % 2]
                act.wait_ge(sig["z_full"], h + 1)
                if h >= 2:
                    act.wait_ge(sig["d_ready"], h - 1)
                fn(z_[:, 0:512], PS[:, 0, :], ACT.Identity, bias=bias[:, h:h + 1], scale=SB_DH ** -0.5)
                fn(z_[:, 512:1280].rearrange("p (a n) -> p a n", a=2), PS[:, 1:3, 0:384], ACT.Identity,
                   bias=bias[:, h:h + 1], scale=SB_DH ** -0.5).then_inc(sig["z_out"], 1)

            def log_part(n, s_):
                act.wait_ge(sig["abs_ready"], n + 1)
                fn(s_, s_, ACT.Exp, scale=-1.0).then_inc(sig["e_ready"], 1)
                act.wait_ge(sig["e_ready"], n + 1)
                fn(s_, s_, ACT.Ln, bias=1.0).then_inc(sig["soft_log"], 1)

            def weight(n, w_):
                act.wait_ge(sig["d_ready"], n + 1)
                fn(w_, w_, ACT.Exp).then_inc(sig["w_ready"], 1)

            logits(0)
            log_part(0, sb_s[0])
            for h in range(SB_HEADS):
                if h + 1 < SB_HEADS:
                    logits(h + 1)
                    log_part(h + 1, sb_s[(h + 1) % 2])
                weight(h, sb_w[h % 2])

            for j in range(DEC_BATCH * N_PAGES):
                act.wait_ge(sig["kt_full"], j + 1)
                fn(k_turned[:, j % 2, :], PS[:, 4 + j % 2, :], ACT.Copy).then_inc(sig["kt_out"], 1)
            log_part(SB_HEADS, s_past)
            log_part(SB_HEADS + 1, s_new)
            weight(SB_HEADS, w_past)
            weight(SB_HEADS + 1, w_new)

            for p in range(2):
                act.wait_ge(sig["la_abs"], p + 1)
                fn(la_soft, la_soft, ACT.Exp, scale=-1.0).then_inc(sig["la_log"], 1)
                act.wait_ge(sig["la_log"], 2 * p + 1)
                fn(la_soft, la_soft, ACT.Ln, bias=1.0).then_inc(sig["la_log"], 1)
            for p in range(2):
                act.wait_ge(sig["cum_ready"], 2)
                if p:
                    act.wait_ge(sig["lev_k"], LEVELS * p)
                    act.wait_ge(sig["lev_q"], LEVELS * p)
                fn(decay[0], cum[:, p, :], ACT.Exp, scale=1.0 / 16).then_inc(sig["eb_ready"], 1)
                if p:
                    act.wait_ge(sig["state_ready"], N_CH * p)
                    act.wait_ge(sig["sn_decayed"], p)
                fn(decay_last[:, 0:N_CH], cum[:, p, CH - 1:SEQ:CH], ACT.Exp, scale=1.0 / 16)
                fn(decay_last[:, N_CH:], cum[:, p, SEQ + DEC_SEQ - 1:T:DEC_SEQ], ACT.Exp,
                   scale=1.0 / 16).then_inc(sig["last_ready"], 1)
                act.wait_ge(sig["kl_diff"], p + 1)
                fn(decay[1], decay[1], ACT.Exp, scale=1.0 / 16).then_inc(sig["kl_exp"], 1)
                for li in range(1, LEVELS + 1):
                    n_tok = T if li <= 2 else SEQ
                    act.wait_ge(sig["lev_diff"], LEVELS * p + li)
                    d_ = decay[li % 2][:, 0:n_tok]
                    fn(d_, d_, ACT.Exp, scale=1.0 / 16).then_inc(sig["lev_exp"], 1)
                    if li == 2:
                        act.wait_ge(sig["klt_full"], p + 1)
                        if p:
                            act.wait_ge(sig["u_full"], p)
                        fn(kl_nat, PS[:, 6, :].rearrange("p (c n) -> p c n", c=N_CH), ACT.Copy)
                        fn(kl_new[:], PS[0:N_SAMPLE, 7, 0:P], ACT.Copy).then_inc(sig["klt_out"], 1)
                for hh in range(2):
                    h = 2 * p + hh
                    act.wait_ge(sig["og_full"], h + 1)
                    fn(flat(y[:, h])[:, 0:SEQ], PS[:, hh, :], ACT.Copy).then_inc(sig["og_out"], 1)
                act.wait_ge(sig["inter_full"], p + 1)
                if p:
                    act.wait_ge(sig["on_out"], 1 + p)
                fn(inter_new.rearrange("p b h t -> p (b h t)"), PS[:, 2, 0:64], ACT.Copy).then_inc(sig["inter_out"], 1)

            act.wait_ge(sig["nat_stored"], 16 * 4)
            act.wait_ge(sig["state_stored"], 16 * 2)
            act.wait_ge(sig["sn_out"], 2)

            def head_square(i):
                if i >= 2:
                    full(act, T0["merge"] + i - 2)
                elif i == 1:
                    act.wait_ge(sig["klt_full"], 2)
                act.wait_ge(sig["og_out"], 4)
                act.wait_ge(sig["on_out"], 3)
                fn(sq[:, i % 2, :], flat(y[:, i]), ACT.Square).then_inc(sig["m_sq"], 1)

            def out_gate(i):
                e_ = work[:, i % 2, :]
                act.wait_ge(sig["gg_held"], i + 1)
                fn(e_, e_, ACT.Exp, scale=-1.0).then_inc(sig["gg_exp"], 1)
                act.wait_ge(sig["gg_exp"], i + 1)
                fn(e_, e_, ACT.Identity, bias=1.0).then_inc(sig["gg_den"], 1)

            head_square(0)
            for i in range(KD):
                if i < 4:
                    out_gate(i)
                if i + 1 < KD:
                    head_square(i + 1)
                t, r = T0["merge"] + i, rstd[:, i % 2]
                full(act, t)
                if i >= 2:
                    act.wait_ge(sig["m_ready"], i - 1)
                fn(r, banks(t % 2, 0, 2), ACT.Ln, bias=eps[:],
                   scale=1.0 / (GLA_DV if i < 4 else SB_DH)).then_inc(psum_free[t % 2], 1)
                act.wait_ge(psum_free[t % 2], t // 2 + 1)
                fn(r, r, ACT.Exp, scale=-0.5).then_inc(sig["m_norm"], 1)
                act.wait_ge(sig["m_ready"], i + 1)
                fn(a_hi[:, i, :], decay[i % 2], ACT.Copy).then_inc(sig["a_hi_ready"], 1)

            def out_body(st, t, quad, use):
                full(act, t)
                fn(y[:, 2 * st.c:2 * st.c + 2].rearrange("p k a t -> p (k a) t"), banks(quad, 0, 4),
                   ACT.Copy).then_inc(psum_free[quad], 1)
                act.wait_ge(psum_free[quad], use + 1)
                for c in range(2):
                    square(3, 2 * st.c + c, flat(y[:, 2 * st.c + c]))

            for n in range(4):
                t, quad, use = ticket(Step(n), "out")
                split(Step(n), "out", t)
                out_body(Step(n), t, quad, use)
            act.wait_ge(sig["a_lo_ready"], 24)
            for k in range(2):
                t = T0["p"] + k
                full(act, t)
                fn(p_hi[:, k, 0:SEQ], PS[:, 4 * (t % 2), :], ACT.Copy)
                fn(p_hi[:, k, SEQ:T], PS[:, 4 * (t % 2) + 1, 0:N_SAMPLE], ACT.Copy).then_inc(sig["p_hi_ready"], 1)
            norm(3)
            boundary(1, "f2_pre", 4)
            ffn("f2", 4)
            boundary(2, "ple_pre", 6)
            split(Step(0), "embed", T0["embed"])
            for n in range(4):
                t = T0["embed"] + n
                full(act, t)
                fn(e[:, 2 * n:2 * n + 2].rearrange("p k a t -> p (k a) t"), banks(t % 2, 0, 4),
                   ACT.Copy).then_inc(psum_free[t % 2], 1)
            g_ = work[:].rearrange("p a t -> p (a t)")
            for n in range(4):
                t, quad, use = ticket(Step(n), "gate")
                if n < 3:
                    split(Step(n), "gate", t)
                if n == 0:
                    norm(6)
                act.wait_ge(sig["pg_ready"], n + 1)
                fn(g_, g_, ACT.Exp, scale=-1.0).then_inc(sig["pg_exp"], 1)
                act.wait_ge(sig["pg_exp"], n + 1)
                fn(g_, g_, ACT.Identity, bias=1.0).then_inc(sig["pg_den"], 1)
                act.wait_ge(sig["pg_out"], n + 1)
                for c in range(2):
                    square(7, 2 * n + c, flat(y[:, 2 * n + c]))
            norm(7)
            for n in range(0, 5, 2):
                t, m = T0["y"] + n, (P if n < 4 else N_SAMPLE)
                full(act, t)
                fn(rows[0:m, n, :].rearrange("p (a n) -> p a n", a=2), PS[0:m, 4 * (t % 2):4 * (t % 2) + 2, :],
                   ACT.Copy).then_inc(psum_free[t % 2], 1)

        @block.vector
        def _(dve):
            v = nc.vector

            def split(st, name):
                nxt, w0 = Step(st.c + 1, st.i), W0[name]
                slot, width = nxt.parity(w0), widths[w0 + st.c + 1]
                dve.wait_ge(sig["split_hi"], w0 + nxt.n + 1)
                v.tensor_tensor(w_lo[:, slot, 0:width], raw[:, slot, 0:width],
                                w_hi[:, slot, 0:width].bitcast(F32), ALU.subtract).then_inc(sig["split_lo"], 1)

            def input_tile(k, name, stage_no):
                c = VEC[name] + k
                dve.wait_ge(sig["a_hi_ready"], 8 * stage_no + k + 1)
                v.scalar_tensor_tensor(a_lo[:, k, :], flat(x[:, k]), vec[:, c:c + 1], a_hi[:, k, :].bitcast(F32),
                                       ALU.mult, ALU.subtract).then_inc(sig["a_lo_ready"], 1)

            def boundary(b, j, post, pre=None, stage_no=None):
                dve.wait_ge(sig["rstd_ready"], j + 1)

                def update(k):
                    n, c = 8 * b + k, VEC[post] + k
                    if n >= 2:
                        dve.wait_ge(sig["x_ready"], n - 1)
                    v.scalar_tensor_tensor(work[:, k % 2, :], flat(y[:, k]), vec[:, c:c + 1], flat(rstd[:, j % 2]),
                                           ALU.mult, ALU.mult).then_inc(sig["upd_ready"], 1)
                update(0)
                for k in range(KD):
                    if k + 1 < KD:
                        update(k + 1)
                    if pre:
                        input_tile(k, pre, stage_no)

            def stage(name, n, body, after_first=None):
                def one(st):
                    t, quad, use = ticket(st, name)
                    split(st, name)
                    if st.c == 0 and after_first is not None:
                        dve.wait_ge(sig["rstd_ready"], after_first + 1)
                    body(st, t, quad, use)
                one(Step(0))
                steps(dve, 1, n - 1, one)
                one(Step(n - 1))

            def up(name, j):
                base = up_base[name]

                def body(st, t, quad, use):
                    n, r = base + st.n, rstd[:, j % 2]
                    full(dve, t)
                    dve.wait_ge(sig["h_lo_ready"], n)
                    v.tensor_tensor(gs, banks(quad, 0, 2), r, ALU.mult).then_inc(sig["g_ready"], 1)
                    dve.wait_ge(sig["g_ready"], n + 1)
                    v.tensor_scalar(es, gs, LOWEST, None, ALU.max).then_inc(sig["g_held"], 1)
                    v.tensor_tensor(us, banks(quad, 2, 2), r, ALU.mult).then_inc(psum_free[quad], 1)
                    dve.wait_ge(sig["den_ready"], n + 1)
                    v.reciprocal(es, es).then_inc(sig["sig_ready"], 1)
                    dve.wait_ge(sig["sig_ready"], n + 1)
                    v.tensor_tensor(gs, gs, es, ALU.mult).then_inc(sig["silu_ready"], 1)
                    dve.wait_ge(psum_free[quad], use + 1)
                    dve.wait_ge(sig["silu_ready"], n + 1)
                    v.tensor_tensor(us, us, gs, ALU.mult).then_inc(sig["h_raw"], 1)
                    dve.wait_ge(sig["h_hi_ready"], n + 1)
                    hs = bass.ds(st.n, 1)
                    v.tensor_tensor(h_lo[:, hs, :].rearrange("p a t -> p (a t)"), flat(us),
                                    h_hi[:, hs, :].bitcast(F32).rearrange("p a t -> p (a t)"),
                                    ALU.subtract).then_inc(sig["h_lo_ready"], 1)
                return body

            def down1(st, t, quad, use):
                full(dve, t)
                yt = y[:, bass.ds(st.n, 1)].rearrange("p k a t -> p (k a) t")
                v.tensor_tensor(yt, banks(quad, 0, 2), yt, ALU.add).then_inc(psum_free[quad], 1)

            def ffn(name, j):
                stage(f"{name}_up0", GROUPS[0], up(f"{name}_up0", j), after_first=j)
                stage(f"{name}_down0", KD, lambda st, t, quad, use: None)
                stage(f"{name}_up1", GROUPS[1], up(f"{name}_up1", j))
                stage(f"{name}_down1", KD, down1)

            full(dve, 0)
            v.tensor_copy(vec[:], PS[:, 0, 0:N_VEC]).then_inc(sig["vec_ready"], 1)
            v.tensor_copy(bias[:], PS[:, 1, 0:SB_HEADS]).then_inc(psum_free[0], 1)
            dve.wait_ge(sig["vec_ready"], 1)
            for name in ("f1_post", "f2_post"):
                c = VEC[name]
                v.tensor_scalar(vec[:, c:c + 8], vec[:, c:c + 8], 0.5, None, ALU.mult).then_inc(sig["vec_ready"], 1)
            for k in range(KD + 1):
                if k < KD:
                    t = T0["x"] + k
                    full(dve, t)
                    v.tensor_copy(flat(x[:, k])[:, SEQ:T], PS[:, 4 * (t % 2) + 1, 0:N_SAMPLE])
                    v.tensor_copy(flat(x[:, k])[:, 0:SEQ], PS[:, 4 * (t % 2), :]).then_inc(psum_free[t % 2], 1)
                if k == 2:
                    dve.wait_ge(sig["split_hi"], 1)
                    v.tensor_tensor(w_lo[:, 0, :], raw[:, 0, :], w_hi[:, 0, :].bitcast(F32),
                                    ALU.subtract).then_inc(sig["split_lo"], 1)
                if k >= 1:
                    input_tile(k - 1, "f1_pre", 0)
            ffn("f1", 0)
            boundary(0, 1, "f1_post", "mix_pre", 1)

            def project(st, t, quad, use):
                full(dve, t)
                if st.c == 12:
                    v.tensor_tensor(glr[:], PS[0:GLA_RANK, 4 * quad:4 * quad + 2, 0:HALF], rstd[0:GLA_RANK, 0],
                                    ALU.mult).then_inc(psum_free[quad], 1)
                elif st.c == 0:
                    for c in range(2):
                        ins = v.scalar_tensor_tensor(proj[:, GQ + c], banks(quad, 2 * c, 2), GLA_DK ** -0.5,
                                                     rstd[:, 0], ALU.mult, ALU.mult)
                    ins.then_inc(psum_free[quad], 1)
                else:
                    v.tensor_tensor(proj[:, bass.ds(2 * st.n, 2)],
                                    banks(quad, 0, 4).rearrange("p (c a) t -> p c a t", c=2),
                                    rstd[:, 0:1].broadcast_to([P, 2, 2, HALF]), ALU.mult).then_inc(psum_free[quad], 1)

            stage("in", 13, project, after_first=2)
            for n, dst, src in ((1, v_nat[:], lambda q: PS[:, 4 * q:4 * q + 4, :]),
                                (3, new_nat[:], lambda q: PS[0:N_SAMPLE, 4 * q:4 * q + 3, :])):
                t = T0["natural"] + n
                full(dve, t)
                v.tensor_copy(dst, src(t % 2)).then_inc(psum_free[t % 2], 1)

            def magnitudes(h):
                z_ = sb_z[h % 2]
                dve.wait_ge(sig["z_out"], h + 1)
                diag = z_[:, 0:512].rearrange("p (j q) -> p j q", j=4)
                v.tensor_tensor(diag, diag, neg_diag[:].unsqueeze(1).broadcast_to([P, 4, P]),
                                ALU.add).then_inc(sig["z_masked"], 1)
                dve.wait_ge(sig["z_masked"], h + 1)
                if h >= 2:
                    dve.wait_ge(sig["c_full"], h - 1)
                v.scalar_tensor_tensor(sb_s[h % 2], z_, -1.0, z_, ALU.mult, ALU.max).then_inc(sig["abs_ready"], 1)

            def softplus(n, z_, s_):
                dve.wait_ge(sig["soft_log"], n + 1)
                v.scalar_tensor_tensor(s_, z_, 0.0, s_, ALU.max, ALU.add).then_inc(sig["sp_ready"], 1)

            def exponents(h):
                z_, w_ = sb_z[h % 2], sb_w[h % 2]
                dve.wait_ge(sig["c_full"], h + 1)
                if h >= 2:
                    dve.wait_ge(sig["o_full"], h - 1)
                v.tensor_tensor(w_[:, 0:512], z_[:, 0:512], PS[:, 4, :], ALU.subtract)
                v.tensor_tensor(w_[:, 512:1280].rearrange("p (a n) -> p a n", a=2),
                                z_[:, 512:1280].rearrange("p (a n) -> p a n", a=2), PS[:, 5:7, 0:384],
                                ALU.subtract).then_inc(sig["d_ready"], 1)

            def head_out(h):
                r = slice(64 * (h % 2), 64 * (h % 2) + 64)
                dve.wait_ge(sig["o_full"], h + 1)
                v.tensor_copy(flat(y[:, 4 + h // 2])[r, 0:SEQ], PS[r, 3 + 4 * (h % 2), :]).then_inc(sig["o_out"], 1)

            magnitudes(0)
            softplus(0, sb_z[0], sb_s[0])
            for h in range(SB_HEADS):
                if h + 1 < SB_HEADS:
                    magnitudes(h + 1)
                exponents(h)
                if h + 1 < SB_HEADS:
                    softplus(h + 1, sb_z[(h + 1) % 2], sb_s[(h + 1) % 2])
                if h >= 1:
                    head_out(h - 1)
            head_out(SB_HEADS - 1)

            new = slice(0, N_SAMPLE)
            cols = bias_cols.rearrange("p a b c -> p (a b c)")
            dve.wait_ge(sig["setup_new"], 1)
            dve.wait_ge(sig["zs_full"], 1)
            v.scalar_tensor_tensor(z_past.rearrange("p (a n) -> p a n", a=2),
                                   PS[:, 6, :].rearrange("p (a n) -> p a n", a=2), SB_DH ** -0.5,
                                   cols.unsqueeze(1).broadcast_to([P, 2, 256]), ALU.mult, ALU.add).then_inc(sig["zs_out"], 1)
            v.scalar_tensor_tensor(z_new, PS[new, 7, 0:256], SB_DH ** -0.5, cols[new, :], ALU.mult,
                                   ALU.add).then_inc(sig["zs_out"], 1)
            dve.wait_ge(sig["zs_out"], 2)
            v.tensor_tensor(z_new, z_new, neg_cols.rearrange("p a b c -> p (a b c)"), ALU.add).then_inc(sig["z_masked"], 1)
            v.scalar_tensor_tensor(s_past, z_past, -1.0, z_past, ALU.mult, ALU.max).then_inc(sig["abs_ready"], 1)
            dve.wait_ge(sig["z_masked"], SB_HEADS + 1)
            v.scalar_tensor_tensor(s_new, z_new, -1.0, z_new, ALU.mult, ALU.max).then_inc(sig["abs_ready"], 1)
            softplus(SB_HEADS, z_past, s_past)
            softplus(SB_HEADS + 1, z_new, s_new)
            dve.wait_ge(sig["c_full"], SB_HEADS + 1)
            v.tensor_tensor(w_past, z_past, PS[:, 0, :], ALU.subtract).then_inc(sig["d_ready"], 1)
            v.tensor_tensor(w_new, z_new, PS[new, 1, 0:256], ALU.subtract).then_inc(sig["d_ready"], 1)
            dve.wait_ge(sig["n_out"], DEC_BATCH * N_PAGES)
            for hh in range(2):
                r = slice(64 * hh, 64 * hh + 64)
                dst = y[r, 4:8].rearrange("p k a t -> p k (a t)")[:, :, SEQ:T].rearrange("p k (b t) -> p k b t", t=DEC_SEQ)
                src = PS[r, 2:6, 0:64].rearrange("p k (b h t) -> p k h b t", h=2, t=DEC_SEQ)[:, :, hh]
                ins = v.tensor_copy(dst, src)
            ins.then_inc(sig["on_out"], 1)

            for p in range(2):
                dve.wait_ge(sig["la_full"], p + 1)
                dve.wait_ge(sig["cum_ready"], p)
                v.tensor_scalar(rstd[:, 0], PS[:, 2 * p:2 * p + 2, 0:HALF], vec[:, 64 + p:65 + p], None,
                                ALU.add).then_inc(sig["la_sum"], 1)
                dve.wait_ge(sig["la_sum"], p + 1)
                v.scalar_tensor_tensor(la_soft, la_raw, -1.0, la_raw, ALU.mult, ALU.max).then_inc(sig["la_abs"], 1)
                dve.wait_ge(sig["la_log"], 2 * p + 2)
                v.scalar_tensor_tensor(la_raw, la_raw, 0.0, la_soft, ALU.min, ALU.subtract).then_inc(sig["la_soft_ready"], 1)
                dve.wait_ge(sig["la_soft_ready"], p + 1)
                for c in range(N_CH):
                    tok = slice(c * P, (c + 1) * P)
                    v.tensor_tensor_scan(cum[:, p, tok], ones[:], la_raw[:, tok], 0.0, ALU.mult, ALU.add)
                v.tensor_tensor_scan(cum[:, p, SEQ:T], scan_keep[:], la_raw[:, SEQ:T], 0.0, ALU.mult,
                                     ALU.add).then_inc(sig["cum_ready"], 1)
            for p in range(2):
                n_att = (LEVELS + 1) * p
                gq, gk = flat(proj[:, GQ + p]), flat(proj[:, GK + p])
                dve.wait_ge(sig["cum_ready"], 2)
                chunks = cum[:, p, 0:SEQ].rearrange("p (c t) -> p c t", t=CH)
                batches = cum[:, p, SEQ:T].rearrange("p (c t) -> p c t", t=DEC_SEQ)
                if p:
                    dve.wait_ge(sig["lev_k"], LEVELS * p)
                    dve.wait_ge(sig["lev_q"], LEVELS * p)
                v.tensor_tensor(decay[1][:, 0:SEQ].rearrange("p (c t) -> p c t", t=CH),
                                chunks[:, :, CH - 1:CH].broadcast_to([P, N_CH, CH]), chunks, ALU.subtract)
                v.tensor_tensor(decay[1][:, SEQ:T].rearrange("p (c t) -> p c t", t=DEC_SEQ),
                                batches[:, :, DEC_SEQ - 1:DEC_SEQ].broadcast_to([P, DEC_BATCH, DEC_SEQ]), batches,
                                ALU.subtract).then_inc(sig["kl_diff"], 1)
                dve.wait_ge(sig["eb_ready"], p + 1)
                if p:
                    dve.wait_ge(sig["og_full"], 2 * p)
                    dve.wait_ge(sig["inter_full"], p)
                    dve.wait_ge(sig["qe_ready"], 2 * p)
                v.tensor_tensor(q_dec, gq, decay[0], ALU.mult).then_inc(sig["qe_ready"], 1)
                v.memset(q_new, 0.0).then_inc(sig["qz_ready"], 1)
                dve.wait_ge(sig["qe_ready"], 2 * p + 1)
                dve.wait_ge(sig["qz_ready"], p + 1)
                for hh in range(2):
                    r = slice(64 * hh, 64 * hh + 64)
                    ins = v.tensor_copy(q_new[r, :, hh, :], q_dec[r, SEQ:T].rearrange("p (b t) -> p b t", t=DEC_SEQ))
                ins.then_inc(sig["qe_ready"], 1)
                dve.wait_ge(sig["kl_exp"], p + 1)
                if p:
                    dve.wait_ge(sig["klt_full"], p)
                v.tensor_tensor(kl, gk, decay[1], ALU.mult).then_inc(sig["kl_ready"], 1)

                def level_diff(li):
                    half, n_tok = 1 << (li - 1), (T if li <= 2 else SEQ)
                    if li >= 3:
                        dve.wait_ge(sig["lev_k"], LEVELS * p + li - 2)
                        dve.wait_ge(sig["lev_q"], LEVELS * p + li - 2)
                    elif li == 1:
                        dve.wait_ge(sig["kl_ready"], p + 1)
                    b_ = cum[:, p, 0:n_tok].rearrange("p (n a t) -> p n a t", a=2, t=half)
                    d_ = decay[li % 2][:, 0:n_tok].rearrange("p (n a t) -> p n a t", a=2, t=half)
                    ref = b_[:, :, 0, half - 1:half].broadcast_to([P, n_tok // (2 * half), half])
                    v.tensor_tensor(d_[:, :, 0, :], ref, b_[:, :, 0, :], ALU.subtract)
                    v.tensor_tensor(d_[:, :, 1, :], b_[:, :, 1, :], ref, ALU.subtract).then_inc(sig["lev_diff"], 1)

                def level_q(li):
                    n_tok = T if li <= 2 else SEQ
                    dve.wait_ge(sig["lev_exp"], LEVELS * p + li)
                    if n_att + li >= 3:
                        dve.wait_ge(sig["lev_full"], n_att + li - 1)
                    v.tensor_tensor(q_lev[li % 2][:, 0:n_tok], gq[:, 0:n_tok], decay[li % 2][:, 0:n_tok],
                                    ALU.mult).then_inc(sig["lev_q"], 1)

                def level_scores(li):
                    dve.wait_ge(sig["lev_full"], n_att + li + 1)
                    src = PS[:, 2 * (li % 2):2 * (li % 2) + 2, :].rearrange("p a (c t) -> p (a c) t", t=P)
                    src_new = PS[0:N_SAMPLE, 4:6, 0:N_SAMPLE]
                    if li == 0:
                        v.tensor_tensor(att_new, src_new, ident[0:N_SAMPLE, 0:N_SAMPLE].unsqueeze(1).broadcast_to(
                            [N_SAMPLE, 2, N_SAMPLE]), ALU.mult)
                        v.tensor_tensor(att, src, ident[:].unsqueeze(1).broadcast_to([P, 8, P]),
                                        ALU.mult).then_inc(sig["att_out"], 1)
                        return
                    dve.wait_ge(sig["att_out"], n_att + li)
                    mask = level_mask[:, li - 1, :].bitcast(U32)
                    if li <= 2:
                        v.copy_predicated(att_new, mask[0:N_SAMPLE, 0:N_SAMPLE].unsqueeze(1).broadcast_to(
                            [N_SAMPLE, 2, N_SAMPLE]), src_new)
                    v.copy_predicated(att, mask.unsqueeze(1).broadcast_to([P, 8, P]), src).then_inc(sig["att_out"], 1)

                if p:
                    dve.wait_ge(sig["on_full"], p)
                level_diff(1)
                for li in range(1, LEVELS + 1):
                    if li < LEVELS:
                        level_diff(li + 1)
                    level_q(li)
                    level_scores(li - 1)
                    if li == 4:
                        dve.wait_ge(sig["klt_out"], p + 1)
                        if p:
                            dve.wait_ge(sig["sn_full"], p)
                        v.tensor_tensor(kl_batch, kl_new[:].unsqueeze(1).broadcast_to([N_SAMPLE, DEC_BATCH, P]),
                                        batch_mask[0:N_SAMPLE, :].unsqueeze(2).broadcast_to([N_SAMPLE, DEC_BATCH, P]),
                                        ALU.mult).then_inc(sig["klb_ready"], 1)
                level_scores(LEVELS)
                dve.wait_ge(sig["u_full"], p + 1)
                dve.wait_ge(sig["last_ready"], p + 1)
                if p:
                    dve.wait_ge(sig["state_stored"], 16 * p)
                    dve.wait_ge(sig["state_ready"], N_CH * p)
                v.tensor_copy(state[:, 0, :], PS[:, 5, 0:P]).then_inc(sig["state_ready"], 1)
                for c in range(1, N_CH):
                    dve.wait_ge(sig["state_ready"], N_CH * p + c)
                    v.scalar_tensor_tensor(state[:, c, :], state[:, c - 1, :], decay_last[:, c:c + 1],
                                           PS[:, 5, c * P:(c + 1) * P], ALU.mult, ALU.add).then_inc(sig["state_ready"], 1)
                dve.wait_ge(sig["on_full"], p + 1)
                dve.wait_ge(sig["inter_out"], p + 1)
                for hh in range(2):
                    ins = v.tensor_tensor(flat(y[:, 2 * p + hh])[:, SEQ:T].rearrange("p (b t) -> p b t", t=DEC_SEQ),
                                          PS[:, 3, hh * N_SAMPLE:(hh + 1) * N_SAMPLE].rearrange("p (b t) -> p b t", t=DEC_SEQ),
                                          inter_new[:, :, hh, :], ALU.add)
                ins.then_inc(sig["on_out"], 1)
                dve.wait_ge(sig["sn_full"], p + 1)
                dve.wait_ge(sig["sn_decayed"], p + 1)
                for hh in range(2):
                    r = slice(64 * hh, 64 * hh + 64)
                    for part, b0 in ((0, 6), (1, 4)):
                        src = PS[r, b0:b0 + 2, :].rearrange("p a (b h v) -> p (a b) h v", b=2, h=2)[:, :, hh, :]
                        st_ = state_new[r, 4 * part:4 * part + 4, :]
                        ins = v.tensor_tensor(st_, src, st_, ALU.add)
                ins.then_inc(sig["sn_out"], 1)

            def hold_gate(i):
                if i >= 2:
                    dve.wait_ge(sig["gg_ready"], i - 1)
                v.tensor_scalar(work[:, i % 2, :], flat(proj[:, GG + i]), LOWEST, None, ALU.max).then_inc(sig["gg_held"], 1)

            def out_gate(i):
                e_ = work[:, i % 2, :]
                dve.wait_ge(sig["gg_den"], i + 1)
                v.reciprocal(e_, e_).then_inc(sig["gg_rec"], 1)
                dve.wait_ge(sig["gg_rec"], i + 1)
                g_ = flat(proj[:, GG + i])
                v.tensor_tensor(g_, g_, e_, ALU.mult).then_inc(sig["gg_ready"], 1)
            hold_gate(0)
            hold_gate(1)
            for i in range(KD):
                if i < 4:
                    out_gate(i)
                if i + 2 < 4:
                    hold_gate(i + 2)
                m_, c = decay[i % 2], (VEC["gla_norm"] if i < 4 else VEC["sb_norm"])
                dve.wait_ge(sig["m_norm"], i + 1)
                if i >= 2:
                    dve.wait_ge(sig["a_lo_ready"], 16 + i - 1)
                out = v.scalar_tensor_tensor(m_, flat(y[:, i]), vec[:, c:c + 1], flat(rstd[:, i % 2]), ALU.mult, ALU.mult)
                if i < 4:
                    out.then_inc(sig["m_mid"], 1)
                    dve.wait_ge(sig["m_mid"], i + 1)
                    dve.wait_ge(sig["gg_ready"], i + 1)
                    out = v.tensor_tensor(m_, m_, flat(proj[:, GG + i]), ALU.mult)
                out.then_inc(sig["m_ready"], 1)
                dve.wait_ge(sig["a_hi_ready"], 16 + i + 1)
                v.tensor_tensor(a_lo[:, i, :], m_, a_hi[:, i, :].bitcast(F32), ALU.subtract).then_inc(sig["a_lo_ready"], 1)
            for n in range(4):
                split(Step(n), "out")
            for k in range(2):
                t = T0["p"] + k
                dve.wait_ge(sig["p_hi_ready"], k + 1)
                v.tensor_tensor(p_lo[:, k, 0:SEQ], PS[:, 4 * (t % 2), :], p_hi[:, k, 0:SEQ].bitcast(F32), ALU.subtract)
                v.tensor_tensor(p_lo[:, k, SEQ:T], PS[:, 4 * (t % 2) + 1, 0:N_SAMPLE], p_hi[:, k, SEQ:T].bitcast(F32),
                                ALU.subtract).then_inc(psum_free[t % 2], 1)
            boundary(1, 3, "mix_post", "f2_pre", 3)
            ffn("f2", 4)
            boundary(2, 5, "f2_post", "ple_pre", 4)
            split(Step(0), "embed")
            g_ = work[:].rearrange("p a t -> p (a t)")
            for n in range(4):
                t, quad, use = ticket(Step(n), "gate")
                if n < 3:
                    split(Step(n), "gate")
                dve.wait_ge(sig["rstd_ready"], 7)
                full(dve, t)
                dve.wait_ge(sig["x_ready"], 8 * 3)
                dve.wait_ge(sig["pg_out"], n)
                v.tensor_tensor(work[:].rearrange("p c (a t) -> p c a t", a=2),
                                banks(quad, 0, 4).rearrange("p (c a) t -> p c a t", c=2),
                                rstd[:, 0:1].broadcast_to([P, 2, 2, HALF]), ALU.mult).then_inc(psum_free[quad], 1)
                dve.wait_ge(psum_free[quad], use + 1)
                v.tensor_scalar(g_, g_, LOWEST, None, ALU.max).then_inc(sig["pg_ready"], 1)
                dve.wait_ge(sig["pg_den"], n + 1)
                v.reciprocal(g_, g_).then_inc(sig["pg_rec"], 1)
                dve.wait_ge(sig["pg_rec"], n + 1)
                v.tensor_tensor(y[:, 2 * n:2 * n + 2].rearrange("p k a t -> p (k a t)"), g_,
                                e[:, 2 * n:2 * n + 2].rearrange("p k a t -> p (k a t)"), ALU.mult).then_inc(sig["pg_out"], 1)
            boundary(3, 7, "ple_post")
            for n in (1, 3):
                t = T0["y"] + n
                full(dve, t)
                v.tensor_copy(rows[:, n, :].rearrange("p (a n) -> p a n", a=2),
                              PS[:, 4 * (t % 2):4 * (t % 2) + 2, :]).then_inc(psum_free[t % 2], 1)

        @block.gpsimd
        def _(pool):
            g = nc.gpsimd
            made = [0]

            def then(ins):
                ins.then_inc(sig["pool_step"], 1)
                made[0] += 1
                pool.wait_ge(sig["pool_step"], made[0])

            then(g.memset(ident[:], 0.0))
            then(g.affine_select(out=ident[:], in_=ident[:], compare_op=ALU.not_equal, fill=1.0, base=0,
                                 pattern=[[-1, P]], channel_multiplier=1))
            then(g.memset(ones[:], 1.0))
            then(g.memset(eps[:], EPS))
            pool.sem_inc(sig["masks_made"], 1)
            then(g.memset(ones64[:], 1.0))
            then(g.memset(ones64[0:64, 64:P], 0.0))
            then(g.memset(ones64[64:P, 0:64], 0.0))
            then(g.affine_select(out=tri[:], in_=ones[:], compare_op=ALU.is_ge, fill=0.0, base=0,
                                 pattern=[[-1, P]], channel_multiplier=1))
            then(g.memset(neg_diag[:], 0.0))
            then(g.affine_select(out=neg_diag[:], in_=neg_diag[:], compare_op=ALU.is_gt, fill=MASKED, base=0,
                                 pattern=[[1, P]], channel_multiplier=-1))

            def add_square(j, k):
                n = 8 * j + k
                pool.wait_ge(sig["sq_ready"], n + 1)
                if k == 0:
                    if j:
                        full(pool, sum_ticket[j - 1])
                    g.tensor_copy(sum_sq[:], sq[:, 0, :]).then_inc(sig["sq_used"], 1)
                else:
                    pool.wait_ge(sig["sq_used"], n)
                    g.tensor_tensor(sum_sq[:], sum_sq[:], sq[:, k % 2, :], ALU.add).then_inc(sig["sq_used"], 1)

            def boundary(b, j=None):
                for k in range(KD + 1):
                    if k < KD:
                        pool.wait_ge(sig["upd_ready"], 8 * b + k + 1)
                        xt = flat(x[:, k])
                        g.tensor_tensor(xt, work[:, k % 2, :], xt, ALU.add).then_inc(sig["x_ready"], 1)
                    if k >= 1 and j is not None:
                        add_square(j, k - 1)

            for k in range(KD):
                add_square(0, k)
            then(g.memset(level_mask[:], 0.0))
            for l in range(LEVELS):
                half, n = 1 << l, P >> (l + 1)
                m_ = level_mask[:, l, :].rearrange("p (n a t) -> p n a t", a=2, t=half)[:, :, 1, :]
                then(g.memset(m_, 1.0))
                then(g.affine_select(out=m_, in_=m_, compare_op=ALU.is_ge, fill=0.0, base=0,
                                     pattern=[[-2 * half, n], [0, half]], channel_multiplier=1))
                then(g.affine_select(out=m_, in_=m_, compare_op=ALU.is_ge, fill=0.0, base=half - 1,
                                     pattern=[[2 * half, n], [0, half]], channel_multiplier=-1))
            then(g.memset(batch_mask[:], 1.0))
            then(g.affine_select(out=batch_mask[:], in_=batch_mask[:], compare_op=ALU.is_ge, fill=0.0, base=0,
                                 pattern=[[-DEC_SEQ, DEC_BATCH]], channel_multiplier=1))
            then(g.affine_select(out=batch_mask[:], in_=batch_mask[:], compare_op=ALU.is_ge, fill=0.0,
                                 base=DEC_SEQ - 1, pattern=[[DEC_SEQ, DEC_BATCH]], channel_multiplier=-1))
            nn = neg_new[:].rearrange("p b t -> p (b t)")
            then(g.tensor_tensor(nn, level_mask[0:N_SAMPLE, 0, 0:N_SAMPLE], level_mask[0:N_SAMPLE, 1, 0:N_SAMPLE], ALU.add))
            then(g.tensor_scalar(nn, nn, -MASKED, MASKED, ALU.mult, ALU.add))
            then(g.memset(scan_keep[:], 1.0))
            then(g.memset(scan_keep[:, 0:N_SAMPLE:DEC_SEQ], 0.0))
            pool.sem_inc(sig["masks_made"], 1)

            for k in range(KD):
                add_square(1, k)
            boundary(0, 2)
            for n, dst, src in ((0, o[2][0, 0].rearrange("(c p) h d -> p c (h d)", p=P), k_nat[:]),
                                (1, o[3][0, 0].rearrange("(c p) h d -> p c (h d)", p=P), v_nat[:]),
                                (3, o[5][0].rearrange("b t h d -> (b t) (h d)"), new_nat[:, 0, :]),
                                (3, o[6][0].rearrange("b t h d -> (b t) (h d)"), new_nat[:, 1, :])):
                t = T0["natural"] + n
                pool.wait_ge(psum_free[t % 2], t // 2 + 1)
                pool.dma_start(dst, src).then_inc(sig["nat_stored"], 16)

            pool.wait_ge(sig["o_full"], SB_HEADS)
            pool.wait_ge(sig["d_ready"], SB_HEADS)
            then(g.memset(q_block, 0.0))
            for hh in range(2):
                r = slice(64 * hh, 64 * hh + 64)
                q_ = proj[r, SQ:SQ + 4].rearrange("p k a t -> p k (a t)")[:, :, SEQ:T].rearrange(
                    "p k (b t) -> p k b t", t=DEC_SEQ)
                then(g.tensor_copy(q_block[r].rearrange("p k b (h t) -> p k b h t", h=2)[:, :, :, hh], q_))
                then(g.tensor_copy(neg_cols.rearrange("p k b (h t) -> p k b h t", h=2)[:, :, :, hh],
                                   neg_new[:].unsqueeze(1).broadcast_to([N_SAMPLE, 4, DEC_BATCH, DEC_SEQ])))
            for p in range(4):
                then(g.tensor_copy(bias_cols[:, p].rearrange("p b (h t) -> p b h t", h=2),
                                   bias[:, 2 * p:2 * p + 2].unsqueeze(1).unsqueeze(3).broadcast_to(
                                       [P, DEC_BATCH, 2, DEC_SEQ])))
            pool.sem_inc(sig["setup_new"], 1)

            old = a["state_gla"][0].rearrange("b (p h) d v -> p (h d) b v", p=2)
            new_out = o[7][0].rearrange("b (p h) d v -> p (h d) b v", p=2)
            state_out = o[4][0, 0].rearrange("(p h) d v -> p (h d) v", p=2)
            pool.wait_ge(sig["n_out"], DEC_BATCH * N_PAGES)
            pool.dma_start(state_old, old[0]).then_inc(sig["state_in"], 16)
            for p in range(2):
                for li in range(1, LEVELS + 1):
                    n_tok, n_att = (T if li <= 2 else SEQ), (LEVELS + 1) * p
                    pool.wait_ge(sig["lev_exp"], LEVELS * p + li)
                    if n_att + li >= 3:
                        pool.wait_ge(sig["lev_full"], n_att + li - 1)
                    g.tensor_tensor(k_lev[li % 2][:, 0:n_tok], flat(proj[:, GK + p])[:, 0:n_tok],
                                    decay[li % 2][:, 0:n_tok], ALU.mult).then_inc(sig["lev_k"], 1)
                pool.wait_ge(sig["last_ready"], p + 1)
                pool.wait_ge(sig["state_in"], 16 * (p + 1))
                if p:
                    pool.wait_ge(sig["new_stored"], 16)
                g.tensor_tensor(state_new, state_old,
                                decay_last[:, N_CH:].unsqueeze(2).broadcast_to([P, DEC_BATCH, P]),
                                ALU.mult).then_inc(sig["sn_decayed"], 1)
                pool.wait_ge(sig["state_ready"], N_CH * (p + 1))
                pool.dma_start(state_out[p], state[:, N_CH - 1, :]).then_inc(sig["state_stored"], 16)
                pool.wait_ge(sig["sn_out"], p + 1)
                pool.dma_start(new_out[p], state_new).then_inc(sig["new_stored"], 16)
                if p == 0:
                    pool.wait_ge(sig["inter_full"], 1)
                    pool.dma_start(state_old, old[1]).then_inc(sig["state_in"], 16)

            pool.wait_ge(sig["m_ready"], KD)
            for n in range(5):
                rows_n = P if n < 4 else N_SAMPLE
                src = a["p_prompt"][0, 0, n * P:(n + 1) * P, :] if n < 4 else a["p_sample"][0].rearrange("b t d -> (b t) d")
                pool.dma_start(rows[0:rows_n, n, 0:PLE_DIM], src).then_inc(sig["p_in"], 16)
            for k in range(KD):
                add_square(3, k)
            boundary(1, 4)
            for k in range(KD):
                add_square(5, k)
            boundary(2, 6)
            for k in range(KD):
                add_square(7, k)
            boundary(3)


_INS = ["x_prompt", "x_sample", "cache_sb_k", "cache_sb_v", "state_gla", "page_table", "p_prompt", "p_sample",
        "f1_pre", "f1_in", "f1_out", "f1_post", "mix_pre", "w_in", "gate_w", "gate_b", "gla_norm", "sb_norm",
        "sb_bias", "w_out", "mix_post", "f2_pre", "f2_in", "f2_out", "f2_post", "ple_pre", "ple_w_gate",
        "ple_w_up", "ple_post"]
_OUTS = [(1, SEQ, D_MODEL), (DEC_BATCH, DEC_SEQ, D_MODEL), (1, 1, SEQ, SB_HEADS, SB_DH),
         (1, 1, SEQ, SB_HEADS, SB_DH), (1, 1, GLA_HEADS, GLA_DK, GLA_DV),
         (1, DEC_BATCH, DEC_SEQ, SB_HEADS, SB_DH), (1, DEC_BATCH, DEC_SEQ, SB_HEADS, SB_DH),
         (1, DEC_BATCH, GLA_HEADS, GLA_DK, GLA_DV)]


def kernel(**inputs):
    import numpy as np
    import concourse.bacc as bacc
    from concourse.bass_utils import run_bass_kernel_spmd

    nc = bacc.Bacc("TRN2", target_bir_lowering=False, num_devices=1)
    arrays, ins = {}, {}
    for name in _INS:
        v = np.ascontiguousarray(inputs[name])
        arrays[f"in_{name}"] = v
        ins[name] = nc.dram_tensor(f"in_{name}", v.shape, mybir.dt.from_np(v.dtype), kind="ExternalInput").ap()
    outs = [nc.dram_tensor(f"out_{i}", s, F32, kind="ExternalOutput").ap() for i, s in enumerate(_OUTS)]
    build(nc, ins, outs)
    r = run_bass_kernel_spmd(nc, [arrays], core_ids=[0])
    return tuple(r.results[0][f"out_{i}"] for i in range(len(_OUTS)))
```

```python
from contextlib import ExitStack

import concourse.bass as bass
from concourse import mybir

F32 = mybir.dt.float32
F32R = mybir.dt.float32r
I32 = mybir.dt.int32
U32 = mybir.dt.uint32
ALU = mybir.AluOpType
ACT = mybir.ActivationFunctionType

P = 128
D_MODEL = 1024
SEQ = 512
DEC_BATCH = 8
DEC_SEQ = 4
N_SAMPLE = DEC_BATCH * DEC_SEQ
T = SEQ + N_SAMPLE
HALF = T // 2
KD = D_MODEL // P
D_FF = 2816
N_PAGES = 2
PLE_DIM = 256
GLA_HEADS, GLA_DK, GLA_DV, GLA_RANK = 4, 64, 128, 16
SB_HEADS, SB_DH = 8, 64
EPS = 1e-6
MASKED = -1e30
F_TILES = D_FF // P
GROUPS = (12, 10)
G_MAX = max(GROUPS)
SLOT = 8 * 256
LEVELS = 7
CH = 128
N_CH = SEQ // CH

VEC = {"f1_pre": 0, "f1_post": 8, "mix_pre": 16, "mix_post": 24, "f2_pre": 32, "f2_post": 40,
       "ple_pre": 48, "ple_post": 56, "gate_b": 64, "gla_norm": 66, "sb_norm": 67}
N_VEC = 68

GQ, GK, GG, SQ, SK, SV, GV = 0, 2, 4, 8, 12, 16, 20
W_IN_STEPS = [(0, GQ), (256, GK), (1024, GG), (1280, GG + 2),
              (1552, SQ), (1808, SQ + 2), (2064, SK), (2320, SK + 2), (2576, SV), (2832, SV + 2),
              (512, GV), (768, GV + 2)]
GLR_COL = 1536


class Step:

    def __init__(self, c, i=0):
        self.c, self.i = c, i
        self.n = c + 2 * i

    def parity(self, base):
        return (base + self.c) % 2

    def half(self, base):
        return (base + self.c) // 2 + self.i


def steps(eng, first, end, body):
    pairs = (end - first) // 2
    if pairs > 1:
        with eng.Fori(0, pairs) as i:
            body(Step(first, i))
            body(Step(first + 1, i))
    elif pairs:
        body(Step(first))
        body(Step(first + 1))
    if (end - first) % 2:
        body(Step(end - 1))


def plan():
    at, w, t = {}, 0, 0
    parts = [("vectors", 0, 1), ("x", 0, KD)]
    for name in ("f1", "f2"):
        parts += [(f"{name}_up0", GROUPS[0], GROUPS[0] + 1), (f"{name}_down0", KD, KD),
                  (f"{name}_up1", GROUPS[1], GROUPS[1]), (f"{name}_down1", KD, KD)]
        parts += [(f"{name}_post", 0, 1)] if name == "f1" else [("embed_first", 0, 1), (f"{name}_post", 0, 1)]
        if name == "f1":
            parts += [("in", 13, 14), ("natural", 0, 4), ("merge", 0, KD), ("out", 4, 4), ("p", 0, 2), ("out_post", 0, 1)]
    parts += [("embed", 1, 3), ("gate", 4, 5), ("gate_post", 0, 1), ("y", 0, KD)]
    for name, n_w, n_t in parts:
        at[name] = (w, t)
        w, t = w + n_w, t + n_t
    at["end"] = (w, t)
    return at


def flat(ap):
    return ap.rearrange("p a t -> p (a t)")


def build(nc, a, o):
    at = plan()
    widths = []
    for name in ("f1", "f2"):
        for g in GROUPS:
            widths += [SLOT] * g + [g * P] * KD
        if name == "f1":
            widths += [SLOT] * 12 + [KD * GLA_RANK] + [SLOT] * 4
    widths += [SLOT] * 5
    n_w = at["end"][0]
    assert len(widths) == n_w

    ctx = ExitStack()
    with ctx:
        def sb(name, shape, dt=F32, where=ctx):
            return where.enter_context(nc.sbuf_tensor(name, shape, dt))

        def sem(name):
            return ctx.enter_context(nc.semaphore(name))

        PS = ctx.enter_context(nc.psum_tensor("PS", [P, 8, 512], F32))

        x = sb("x", [P, KD, 2, HALF])
        y = sb("y", [P, KD, 2, HALF])
        raw = sb("raw", [P, 2, SLOT])
        w_hi = sb("w_hi", [P, 2, SLOT], F32R)
        w_lo = sb("w_lo", [P, 2, SLOT], F32R)
        ident = sb("ident", [P, P])
        ones = sb("ones", [P, P])
        tri = sb("tri", [P, P])
        ones64 = sb("ones64", [P, P])
        neg_diag = sb("neg_diag", [P, P])
        level_mask = sb("level_mask", [P, LEVELS, P])
        batch_mask = sb("batch_mask", [P, DEC_BATCH])
        neg_new = sb("neg_new", [N_SAMPLE, DEC_BATCH, DEC_SEQ])
        scan_keep = sb("scan_keep", [P, N_SAMPLE])
        eps = sb("eps", [P, 1])
        vec_rows = sb("vec_rows", [N_VEC, P])
        vec = sb("vec", [P, N_VEC])
        bias_row = sb("bias_row", [1, SB_HEADS])
        bias = sb("bias", [P, SB_HEADS])
        gate_w = sb("gate_w", [GLA_RANK, 2 * P])
        table = sb("table", [1, DEC_BATCH * N_PAGES], I32)
        sum_sq = sb("sum_sq", [P, T])
        sq = sb("sq", [P, 2, T])
        rstd = sb("rstd", [P, 2, 2, HALF])
        work = sb("work", [P, 2, T])
        glr = sb("glr", [GLA_RANK, 2, HALF])
        with nc.sbuf_tensor("p_hi", [P, 2, T], F32R) as p_hi, nc.sbuf_tensor("p_lo", [P, 2, T], F32R) as p_lo:
            pass
        extra = sb("extra", [P, 3 * 1280])
        with nc.sbuf_tensor("a_hi", [P, KD, T], F32R) as a_hi, nc.sbuf_tensor("a_lo", [P, KD, T], F32R) as a_lo:
            pass
        with ExitStack() as s:
            k_nat = sb("k_nat", [P, N_CH, 512], F32, s)
            v_nat = sb("v_nat", [P, N_CH, 512], F32, s)
            gv_nat = sb("gv_nat", [P, N_CH, 512], F32, s)
            new_nat = sb("new_nat", [N_SAMPLE, 3, 512], F32, s)
            state = sb("state", [P, N_CH, P], F32, s)
            kl_new = sb("kl_new", [N_SAMPLE, P], F32, s)
            decay_last = sb("decay_last", [P, N_CH + DEC_BATCH], F32, s)
        hold_a = sb("hold_a", [P, 2 * KD * T])
        with nc.sbuf_tensor("h_hi", [P, G_MAX, T], F32R) as h_hi, nc.sbuf_tensor("h_lo", [P, G_MAX, T], F32R) as h_lo:
            pass
        with nc.sbuf_tensor("proj", [P, 24, 2, HALF], F32) as proj:
            pass
        with nc.sbuf_tensor("rows", [P, 5, D_MODEL], F32) as rows, nc.sbuf_tensor("e", [P, KD, 2, HALF], F32) as e:
            pass
        hold_h = sb("hold_h", [P, 2 * G_MAX * T])

        def scratch(owner, at_, shape):
            n = 1
            for s_ in shape[1:]:
                n *= s_
            v = owner[0:shape[0], at_:at_ + n]
            if len(shape) == 3:
                return v.rearrange("p (a b) -> p a b", a=shape[1])
            if len(shape) == 4:
                return v.rearrange("p (a b c) -> p a b c", a=shape[1], b=shape[2])
            return v

        work_flat = work[:].rearrange("p a t -> p (a t)")
        gs = scratch(work_flat, 0, [P, 2, HALF])
        us = scratch(work_flat, T, [P, 2, HALF])
        dead = proj[:, SV:SV + 8].rearrange("p k a t -> p (k a t)")
        extra_flat = extra[:]

        sb_z = [scratch(dead, 1280 * n, [P, 1280]) for n in range(2)]
        sb_s = [scratch(dead, 2560, [P, 1280]), scratch(extra_flat, 0, [P, 1280])]
        sb_w = [scratch(extra_flat, 1280 * n, [P, 1280]) for n in (1, 2)]
        y_flat = y[:].rearrange("p k a t -> p (k a t)")
        sq_flat = sq[:].rearrange("p a t -> p (a t)")
        k_page = scratch(y_flat, 0, [P, 4, 512])
        v_page = [k_nat[:, c] for c in range(N_CH)] + [v_nat[:, c] for c in range(N_CH)]
        k_turned = scratch(work_flat, 0, [P, 2, 512])
        q_pad = [rstd[:, n].rearrange("p a t -> p (a t)") for n in range(2)]
        q_block = scratch(sq_flat, 0, [P, 4, DEC_BATCH, 8])
        bias_cols = scratch(sq_flat, 256, [P, 4, DEC_BATCH, 8])
        neg_cols = scratch(sq_flat, 512, [N_SAMPLE, 4, DEC_BATCH, 8])
        z_new = scratch(sq_flat, 768, [N_SAMPLE, 256])
        z_past = scratch(dead, 3840, [P, 512])
        s_past = scratch(extra_flat, 0, [P, 512])
        s_new = scratch(extra_flat, 512, [N_SAMPLE, 256])
        w_past = scratch(y_flat, 0, [P, 512])
        w_new = scratch(y_flat, 512, [N_SAMPLE, 256])
        att = scratch(dead, 0, [P, 8, P])
        state_new = scratch(dead, 1024, [P, DEC_BATCH, P])
        state_old = scratch(dead, 2048, [P, DEC_BATCH, P])
        kl_batch = scratch(dead, 3072, [N_SAMPLE, DEC_BATCH, P])
        q_new = scratch(dead, 4096, [P, DEC_BATCH, 2, DEC_SEQ])
        att_new = scratch(dead, 4160, [N_SAMPLE, 2, N_SAMPLE])
        inter_new = scratch(dead, 4224, [P, DEC_BATCH, 2, DEC_SEQ])
        decay = [scratch(extra_flat, T * n, [P, T]) for n in (0, 1)]
        q_lev = [scratch(extra_flat, T * n, [P, T]) for n in (2, 3)]
        k_lev = [scratch(extra_flat, T * n, [P, T]) for n in (4, 5)]
        kl_nat = scratch(extra_flat, 6 * T, [P, N_CH, P])
        cum = scratch(work_flat, 0, [P, 2, T])
        la_raw, la_soft = rstd[:, 0].rearrange("p a t -> p (a t)"), sum_sq[:]
        q_dec, kl = sq[:, 0, :], sq[:, 1, :]

        names = """vec_in x_in table_in page_in0 page_in1 page_in2 page_in3 vpage_in0 vpage_in1 vpage_in2 vpage_in3 vpage_in4 vpage_in5 vpage_in6 vpage_in7
            state_in p_in raw_in0 raw_in1 out_done ident_made ones_made masks_made pool_step
            split_hi split_lo psum_full psum_free0 psum_free1 vec_ready bias_ready
            a_hi_ready a_lo_ready sq_ready sq_used sum_ready rstd_ready log_ready
            upd_ready x_ready g_ready silu_ready h_raw h_hi_ready h_lo_ready
            p_hi_ready p_lo_ready glr_ready
            z_full z_out z_masked abs_ready e_ready soft_log sp_ready c_full d_ready w_ready o_full o_out
            setup_new kt_full kt_out zs_full zs_out n_out
            la_full la_sum la_abs la_log la_soft_ready cum_ready
            eb_ready qe_ready kl_diff kl_exp kl_ready klt_full klt_out klb_ready last_ready
            lev_diff lev_exp lev_q lev_k lev_full att_out u_full state_ready
            og_full og_out inter_full inter_out on_full on_out sn_full sn_decayed sn_out
            qz_ready q_pad_ready k_stored v_stored nat_stored state_stored new_stored m_mid pg_ready pg_sig pg_out gg_ready m_sq m_norm m_ready rows_out""".split()
        sig = {n: sem(n) for n in names}
        raw_in = [sig["raw_in0"], sig["raw_in1"]]
        psum_free = [sig["psum_free0"], sig["psum_free1"]]
        page_in = [sig[f"page_in{n}"] for n in range(4)]
        vpage_in = [sig[f"vpage_in{n}"] for n in range(8)]

        W0 = {n: v[0] for n, v in at.items()}
        T0 = {n: v[1] for n, v in at.items()}
        NORMS = ["f1_pre", "f1_post", "mix_pre", "mix_post", "f2_pre", "f2_post", "ple_pre", "ple_post"]
        sum_ticket = [T0["f1_up0"] + 1, T0["f1_post"], T0["in"] + 1, T0["out_post"], T0["f2_up0"] + 1,
                      T0["f2_post"], T0["gate"] + 1, T0["gate_post"]]

        def banks(quad, first, n):
            return PS[:, 4 * quad + first:4 * quad + first + n, 0:HALF]

        def full(eng, t, quad_free=None):
            eng.wait_ge(sig["psum_full"], t + 1)

        def ticket(st, name):
            base = T0[name]
            if name in ("f1_up0", "f2_up0", "in", "gate") and st.c >= 1:
                base += 1
            return base + st.n, st.parity(base), st.half(base)

        def embed_ticket(s_):
            return T0["embed"] + s_ - 1 if s_ else T0["embed_first"]

        SPLIT_EARLY = ("f1_up0", "in", "f2_up0")

        block = ctx.enter_context(nc.Block())

        @block.sync
        def _(sp):
            def load(w, slot, parts, wait=True):
                if wait:
                    sp.wait_ge(sig["split_lo"], w - 1)
                for dst, src in parts:
                    sp.dma_start(dst, src).then_inc(raw_in[slot], 16)

            def up(name, g0):
                src = a[f"{name}_in"][0].rearrange("(k p) n -> p k n", p=P)

                def parts(st, slot):
                    dst = raw[:, slot, :].rearrange("p (k c n) -> p k c n", k=KD, c=2)
                    return [(dst[:, :, c, :], src[:, :, bass.ds(c * D_FF + (g0 + st.n) * P, P)]) for c in range(2)]
                return parts

            def down(name, g0, g):
                src = a[f"{name}_out"][0].rearrange("(f p) n -> p f n", p=P)

                def parts(st, slot):
                    dst = raw[:, slot, 0:g * P].rearrange("p (k n) -> p k n", k=g)
                    return [(dst[:, c * g // 2:(c + 1) * g // 2, :],
                             src[:, g0 + c * g // 2:g0 + (c + 1) * g // 2, bass.ds(st.n * P, P)]) for c in range(2)]
                return parts

            def wide(src, col, n=256):
                def parts(st, slot):
                    dst = raw[:, slot, 0:KD * n].rearrange("p (k n) -> p k n", k=KD)
                    v = src.rearrange("(k p) n -> p k n", p=P)
                    return [(dst[:, 4 * c:4 * c + 4, :], v[:, 4 * c:4 * c + 4, bass.ds(col(st), n)]) for c in range(2)]
                return parts

            def stage(name, n, parts, first=0):
                w0 = W0[name]
                steps(sp, first, n, lambda st: load(w0 + st.n, st.parity(w0), parts(st, st.parity(w0))))

            def pages():
                sp.wait_ge(sig["table_in"], 16)
                page_no = [sp.value_load(table[0:1, j:j + 1], min_val=0, max_val=a["cache_sb_k"].shape[1] - 1)
                           for j in range(DEC_BATCH * N_PAGES)]

                def page(dst, cache, j, landed):
                    sp.dma_start(dst, cache[0, bass.ds(page_no[j], 1)].rearrange("a s h d -> s (a h d)")).then_inc(landed, 16)

                sp.wait_ge(sig["upd_ready"], KD)
                for j in range(DEC_BATCH * N_PAGES):
                    if j >= 4:
                        sp.wait_ge(sig["kt_full"], j - 3)
                    page(k_page[:, j % 4, :], a["cache_sb_k"], j, page_in[j % 4])
                for j in range(DEC_BATCH * N_PAGES):
                    if j == 0:
                        sp.wait_ge(sig["k_stored"], 16)
                    elif j == 4:
                        sp.wait_ge(sig["v_stored"], 16)
                        sp.wait_ge(sig["o_full"], SB_HEADS)
                    if j >= 8:
                        sp.wait_ge(sig["n_out"], j - 7)
                    page(v_page[j % 8], a["cache_sb_v"], j, vpage_in[j % 8])

            sp.dma_start(table[:], a["page_table"].rearrange("b n -> (b n)").unsqueeze(0)).then_inc(sig["table_in"], 16)
            for n in range(5):
                rows_n = P if n < 4 else N_SAMPLE
                src = a["x_prompt"][0, n * P:(n + 1) * P, :] if n < 4 else a["x_sample"].rearrange("b t d -> (b t) d")
                sp.dma_start(rows[0:rows_n, n, :], src).then_inc(sig["x_in"], 16)

            first = up("f1", 0)
            for n in range(2):
                load(n, n, first(Step(n), n), wait=False)
            stage("f1_up0", GROUPS[0], first, first=2)
            for name in ("f1", "f2"):
                if name == "f2":
                    stage("f2_up0", GROUPS[0], up(name, 0))
                stage(f"{name}_down0", KD, down(name, 0, GROUPS[0]))
                stage(f"{name}_up1", GROUPS[1], up(name, GROUPS[0]))
                stage(f"{name}_down1", KD, down(name, GROUPS[0], GROUPS[1]))
                if name == "f1":
                    for s_, (col, _t) in enumerate(W_IN_STEPS):
                        w = W0["in"] + s_
                        load(w, w % 2, wide(a["w_in"][0], lambda st: col)(None, w % 2))
                    w = W0["in"] + 12
                    load(w, w % 2, wide(a["w_in"][0], lambda st: GLR_COL, GLA_RANK)(None, w % 2))
                    out_parts = wide(a["w_out"][0], lambda st: st.n * 256)
                    for n in range(2):
                        w = W0["out"] + n
                        load(w, w % 2, out_parts(Step(n), w % 2))
                    pages()
                    stage("out", 4, out_parts, first=2)
            w = W0["embed"]
            up_w = a["ple_w_up"][0].rearrange("(k p) n -> p k n", p=P)
            load(w, w % 2, [(raw[:, w % 2, k * D_MODEL:(k + 1) * D_MODEL], up_w[:, k, :]) for k in range(2)])
            stage("gate", 4, wide(a["ple_w_gate"][0], lambda st: st.n * 256))
            for part in range(2):
                for quad in range(2):
                    sp.wait_ge(psum_free[quad], (T0["y"] + 4 * (part + 1) + 1 - quad) // 2)
                cols = slice(part * 512, (part + 1) * 512)
                sp.dma_start(o[0][0].rearrange("(n p) d -> p n d", p=P)[:, :, cols],
                             rows[:, 0:4, cols]).then_inc(sig["out_done"], 16)
                sp.dma_start(o[1].rearrange("b t d -> (b t) d")[:, cols],
                             rows[0:N_SAMPLE, 4, cols]).then_inc(sig["out_done"], 16)
            sp.wait_ge(sig["out_done"], 16 * 4)
            sp.wait_ge(sig["k_stored"], 16)
            sp.wait_ge(sig["v_stored"], 16)
            sp.wait_ge(sig["nat_stored"], 16 * 2)
            sp.wait_ge(sig["state_stored"], 16 * 2)
            sp.wait_ge(sig["new_stored"], 16 * 2)

        @block.tensor
        def _(pe):
            mm = nc.tensor.matmul

            def open_ticket(t, quad, use):
                pe.wait_ge(psum_free[quad], use)

            def open_t(t):
                open_ticket(t, t % 2, t // 2)

            def weights(w):
                pe.wait_ge(sig["split_lo"], w + 1)

            def dense(quad, slot, tiles, n_k, rhs, ready=None, stride=None, width=P):
                stride = stride or tiles * width
                for k in range(n_k):
                    if ready:
                        ready(k)
                    for c in range(tiles):
                        cols = slice(k * stride + c * width, k * stride + (c + 1) * width)
                        for n, (wt, act) in enumerate(((w_hi, rhs[0]), (w_hi, rhs[1]), (w_lo, rhs[0]))):
                            for half in range(2):
                                last = mm(PS[0:width, 4 * quad + 2 * c + half, 0:HALF], wt[:, slot, cols],
                                          act[:, k, half * HALF:(half + 1) * HALF],
                                          start=(k == 0 and n == 0), stop=(k == n_k - 1 and n == 2))
                return last

            def sum_norm(j):
                t = sum_ticket[j]
                open_t(t)
                pe.wait_ge(sig["sq_used"], 8 * (j + 1))
                for half in range(2):
                    last = mm(PS[:, 4 * (t % 2) + half, 0:HALF], ones[:], sum_sq[:, half * HALF:(half + 1) * HALF],
                              start=True, stop=True)
                last.then_inc(sig["psum_full"], 1)

            def product(name, n, tiles, n_k, rhs, ready=None, norm=None):
                def body(st, ready=None):
                    t, quad, use = ticket(st, name)
                    weights(W0[name] + st.n)
                    open_ticket(t, quad, use)
                    dense(quad, st.parity(W0[name]), tiles, n_k, rhs, ready).then_inc(sig["psum_full"], 1)
                body(Step(0), ready)
                if norm is not None:
                    sum_norm(norm)
                steps(pe, 1, n, body)

            A = (a_hi, a_lo)
            H = (h_hi, h_lo)

            def a_tiles(stage_no):
                return lambda k: pe.wait_ge(sig["a_lo_ready"], 8 * stage_no + k + 1)

            def h_tiles(first):
                return lambda k: pe.wait_ge(sig["h_lo_ready"], first + k + 1)

            def embed(s_):
                t, slot = embed_ticket(s_), W0["embed"] % 2
                weights(W0["embed"])
                open_t(t)
                for k in range(2):
                    for c in range(2):
                        for n, (wt, act) in enumerate(((w_hi, p_hi), (w_hi, p_lo), (w_lo, p_hi))):
                            for half in range(2):
                                col = k * D_MODEL + (2 * s_ + c) * P
                                last = mm(PS[:, 4 * (t % 2) + 2 * c + half, 0:HALF], wt[:, slot, col:col + P],
                                          act[:, k, half * HALF:(half + 1) * HALF],
                                          start=(k == 0 and n == 0), stop=(k == 1 and n == 2))
                last.then_inc(sig["psum_full"], 1)

            def ffn(name, stage_no, first, norm):
                product(f"{name}_up0", GROUPS[0], 2, KD, A, a_tiles(stage_no), norm)
                product(f"{name}_down0", KD, 1, GROUPS[0], H, h_tiles(first))
                product(f"{name}_up1", GROUPS[1], 2, KD, A)
                product(f"{name}_down1", KD, 1, GROUPS[1], H, h_tiles(first + GROUPS[0]))
                if name == "f2":
                    embed(0)
                sum_norm(norm + 1)

            pe.wait_ge(sig["masks_made"], 1)
            pe.wait_ge(sig["vec_in"], 16 * 14)
            nc.tensor.transpose(PS[:, 0, 0:N_VEC], vec_rows[:], ident[0:N_VEC, 0:N_VEC])
            mm(PS[:, 1, 0:SB_HEADS], ones[0:1, :], bias_row[:], start=True, stop=True).then_inc(sig["psum_full"], 1)
            pe.wait_ge(sig["x_in"], 16 * 5)
            for k in range(KD):
                t = T0["x"] + k
                open_t(t)
                for n in range(4):
                    nc.tensor.transpose(PS[:, 4 * (t % 2), n * P:(n + 1) * P], rows[:, n, k * P:(k + 1) * P], ident[:])
                nc.tensor.transpose(PS[:, 4 * (t % 2) + 1, 0:N_SAMPLE], rows[0:N_SAMPLE, 4, k * P:(k + 1) * P],
                                    ident[0:N_SAMPLE, 0:N_SAMPLE]).then_inc(sig["psum_full"], 1)
            ffn("f1", 0, 0, 0)

            product("in", 12, 2, KD, A, a_tiles(1), 2)
            st = Step(12)
            t, quad, use = ticket(st, "in")
            weights(W0["in"] + 12)
            open_ticket(t, quad, use)
            dense(quad, st.parity(W0["in"]), 1, KD, A, width=GLA_RANK).then_inc(sig["psum_full"], 1)

            for n, tile in enumerate((SK, SV, GV)):
                t = T0["natural"] + n
                open_t(t)
                for c in range(N_CH):
                    for f in range(4):
                        last = nc.tensor.transpose(PS[:, 4 * (t % 2) + c, f * P:(f + 1) * P],
                                                   flat(proj[:, tile + f])[:, c * P:(c + 1) * P], ident[:])
                last.then_inc(sig["psum_full"], 1)
            t = T0["natural"] + 3
            open_t(t)
            for n, tile in enumerate((SK, SV, GV)):
                for f in range(4):
                    last = nc.tensor.transpose(PS[0:N_SAMPLE, 4 * (t % 2) + n, f * P:(f + 1) * P],
                                               flat(proj[:, tile + f])[:, SEQ:T], ident[:])
            last.then_inc(sig["psum_full"], 1)

            for quad in range(2):
                pe.wait_ge(psum_free[quad], (T0["merge"] + 1 - quad) // 2)

            def prompt_z(h):
                p = h // 2
                k_, q_ = flat(proj[:, SK + p]), q_pad[h % 2]
                pe.wait_ge(sig["z_out"], h)
                pe.wait_ge(sig["q_pad_ready"], h + 1)
                for j in range(4):
                    mm(PS[:, 0, j * P:(j + 1) * P], k_[:, j * P:(j + 1) * P], q_[:, j * P:(j + 1) * P],
                       start=True, stop=True)
                mm(PS[:, 1, 0:384], k_[:, 0:P], q_[:, P:SEQ], start=True, stop=True)
                mm(PS[:, 2, 0:256], k_[:, P:2 * P], q_[:, 2 * P:SEQ], start=True, stop=True)
                mm(PS[:, 2, 256:384], k_[:, 2 * P:3 * P], q_[:, 3 * P:SEQ], start=True,
                   stop=True).then_inc(sig["z_full"], 1)

            def turn_page(j):
                pe.wait_ge(page_in[j % 4], 16 * (j // 4 + 1))
                pe.wait_ge(sig["kt_out"], j)
                for f in range(4):
                    last = nc.tensor.transpose(PS[:, 7, f * P:(f + 1) * P], k_page[:, j % 4, f * P:(f + 1) * P], ident[:])
                last.then_inc(sig["kt_full"], 1)

            def page_z(b):
                pe.wait_ge(sig["kt_out"], N_PAGES * (b + 1))
                pe.wait_ge(sig["z_out"], b + 2)
                for pg in range(N_PAGES):
                    for p in range(4):
                        col = 384 + pg * 32 + p * 8
                        last = mm(PS[:, 2, col:col + 8], k_turned[:, pg, p * P:(p + 1) * P], q_block[:, p, b, :],
                                  start=True, stop=True)
                return last

            def prompt_sums(h):
                s_ = sb_s[h % 2]
                pe.wait_ge(sig["sp_ready"], h + 1)
                pe.wait_ge(sig["d_ready"], h)
                mm(PS[:, 4, :], tri[:], s_[:, 0:512], start=True, stop=True)
                mm(PS[:, 5, 0:384], tri[:], s_[:, 512:896], start=True, stop=False)
                mm(PS[:, 5, 0:384], ones[:], s_[:, 128:512], start=False, stop=False)
                mm(PS[:, 5, 128:384], ones[:], s_[:, 896:1152], start=False, stop=False)
                mm(PS[:, 5, 256:384], ones[:], s_[:, 1152:1280], start=False, stop=True)
                mm(PS[:, 6, 0:384], tri[:], s_[:, 896:1280], start=True, stop=False)
                mm(PS[:, 6, 0:256], ones[:], s_[:, 256:512], start=False, stop=False)
                mm(PS[:, 6, 128:256], ones[:], s_[:, 1152:1280], start=False, stop=False)
                mm(PS[:, 6, 256:384], ones[:], s_[:, 384:512], start=False, stop=True).then_inc(sig["c_full"], 1)

            def prompt_out(h):
                r, bank, w_ = slice(64 * (h % 2), 64 * (h % 2) + 64), 3, sb_w[h % 2]
                pe.wait_ge(sig["w_ready"], h + 1)
                pe.wait_ge(sig["o_out"], h)
                out, off = PS[r, bank], [512, 896, 1152]
                for j in range(4):
                    v_ = v_nat[:, j, h * SB_DH:(h + 1) * SB_DH]
                    last = mm(out[:, j * P:(j + 1) * P], v_, w_[:, j * P:(j + 1) * P], start=(j == 0), stop=(j in (0, 3)))
                    if j < 3:
                        n = (3 - j) * P
                        mm(out[:, (j + 1) * P:SEQ], v_, w_[:, off[j]:off[j] + n], start=(j == 0), stop=False)
                last.then_inc(sig["o_full"], 1)

            prompt_z(0)
            for h in range(SB_HEADS):
                if h == 0:
                    prompt_z(1)
                    pe.wait_ge(sig["setup_new"], 1)
                elif h + 1 < SB_HEADS:
                    page_z(h - 1)
                    prompt_z(h + 1)
                else:
                    page_z(h - 1).then_inc(sig["z_full"], 1)
                turn_page(2 * h)
                prompt_sums(h)
                turn_page(2 * h + 1)
                if h >= 1:
                    prompt_out(h - 1)
            page_z(SB_HEADS - 1).then_inc(sig["z_full"], 1)
            prompt_out(SB_HEADS - 1)

            n_pages = DEC_BATCH * N_PAGES
            pe.wait_ge(sig["kt_out"], n_pages)
            for p in range(4):
                last = mm(PS[0:N_SAMPLE, 7, p * 64:(p + 1) * 64], flat(proj[:, SK + p])[:, SEQ:T],
                          q_block[:, p].rearrange("p b n -> p (b n)"), start=True, stop=True)
            last.then_inc(sig["zs_full"], 1)

            def gate_logits(p):
                for half in range(2):
                    last = mm(PS[:, 6 + half, 0:HALF], gate_w[:, p * P:(p + 1) * P], glr[:, half], start=True, stop=True)
                last.then_inc(sig["la_full"], 1)

            pe.wait_ge(sig["d_ready"], SB_HEADS)
            pe.wait_ge(sig["zs_out"], 2)
            gate_logits(0)
            pe.wait_ge(sig["sp_ready"], SB_HEADS + 2)
            new = slice(0, N_SAMPLE)
            mm(PS[:, 0, :], tri[:], s_past, start=True, stop=False)
            mm(PS[:, 0, 0:256], ones[:], s_past[:, 256:512], start=False, stop=False)
            mm(PS[:, 0, 0:256], ones[new, :], s_new, start=False, stop=False)
            mm(PS[:, 0, 256:512], ones[new, :], s_new, start=False, stop=True)
            mm(PS[new, 1, 0:256], tri[new, new], s_new, start=True, stop=True).then_inc(sig["c_full"], 1)
            pe.wait_ge(sig["la_sum"], 1)
            gate_logits(1)
            pe.wait_ge(sig["w_ready"], SB_HEADS + 2)
            pe.wait_ge(sig["o_out"], SB_HEADS)
            for p in range(4):
                mm(PS[:, 2 + p, 0:64], new_nat[:, 1, p * P:(p + 1) * P], w_new[:, p * 64:(p + 1) * 64],
                   start=True, stop=False)
            for j in range(n_pages):
                b, pg = j // N_PAGES, j % N_PAGES
                pe.wait_ge(vpage_in[j % 8], 16 * (j // 8 + 1))
                for p in range(4):
                    col = p * 64 + b * 8
                    last = mm(PS[:, 2 + p, b * 8:b * 8 + 8], v_page[j % 8][:, p * P:(p + 1) * P],
                              w_past[:, pg * 256 + col:pg * 256 + col + 8], start=False, stop=(j == n_pages - 1))
                last.then_inc(sig["n_out"], 1)

            pe.wait_ge(sig["on_out"], 1)
            pe.wait_ge(sig["la_sum"], 2)
            for p in range(2):
                n_att = (LEVELS + 1) * p
                if p:
                    pe.wait_ge(sig["sn_out"], p)
                    pe.wait_ge(sig["og_out"], 2 * p)
                    pe.wait_ge(sig["on_out"], 1 + p)
                pe.wait_ge(sig["kl_ready"], p + 1)
                for c in range(N_CH):
                    nc.tensor.transpose(PS[:, 6, c * P:(c + 1) * P], kl[:, c * P:(c + 1) * P], ident[:])
                nc.tensor.transpose(PS[0:N_SAMPLE, 7, 0:P], kl[:, SEQ:T], ident[:]).then_inc(sig["klt_full"], 1)
                for li in range(LEVELS + 1):
                    if li == 0:
                        q_, k_ = flat(proj[:, GQ + p]), flat(proj[:, GK + p])
                    else:
                        q_, k_ = q_lev[li % 2], k_lev[li % 2]
                        pe.wait_ge(sig["lev_q"], LEVELS * p + li)
                        pe.wait_ge(sig["lev_k"], LEVELS * p + li)
                    if li in (1, 2):
                        pe.wait_ge(sig["att_out"], n_att + li)
                    elif n_att + li >= 2:
                        pe.wait_ge(sig["att_out"], n_att + li - 1)
                    b0 = 2 * (li % 2)
                    for hh in range(2):
                        r = slice(64 * hh, 64 * hh + 64)
                        for c in range(N_CH):
                            tok = slice(c * P, (c + 1) * P)
                            last = mm(PS[:, b0 + hh, tok], k_[r, tok], q_[r, tok], start=True, stop=True)
                        if li <= 2:
                            last = mm(PS[0:N_SAMPLE, 4 + hh, 0:N_SAMPLE],
                                      k_[r, SEQ:T], q_[r, SEQ:T], start=True, stop=True)
                    last.then_inc(sig["lev_full"], 1)
                pe.wait_ge(sig["klt_out"], p + 1)
                pe.wait_ge(sig["att_out"], n_att + LEVELS + 1)
                for hh in range(2):
                    h = 2 * p + hh
                    for c in range(N_CH):
                        last = mm(PS[64 * hh:64 * hh + 64, 5, c * P:(c + 1) * P],
                                  kl_nat[:, c, 64 * hh:64 * hh + 64], gv_nat[:, c, h * P:(h + 1) * P],
                                  start=True, stop=True)
                last.then_inc(sig["u_full"], 1)
                pe.wait_ge(sig["state_ready"], N_CH * (p + 1))
                pe.wait_ge(sig["qe_ready"], 2 * (p + 1))
                for hh in range(2):
                    h, r = 2 * p + hh, slice(64 * hh, 64 * hh + 64)
                    for c in range(N_CH):
                        tok = slice(c * P, (c + 1) * P)
                        last = mm(PS[:, hh, tok], gv_nat[:, c, h * P:(h + 1) * P], att[:, hh * N_CH + c, :],
                                  start=True, stop=(c == 0))
                        if c:
                            last = mm(PS[:, hh, tok], state[r, c - 1, :], q_dec[r, tok], start=False, stop=True)
                    last.then_inc(sig["og_full"], 1)
                pe.wait_ge(sig["state_in"], 16 * (p + 1))
                for b in range(DEC_BATCH):
                    last = mm(PS[:, 2, b * 8:b * 8 + 8], state_old[:, b, :],
                              q_new[:, b].rearrange("p h t -> p (h t)"), start=True, stop=True)
                last.then_inc(sig["inter_full"], 1)
                for hh in range(2):
                    h = 2 * p + hh
                    last = mm(PS[:, 3, hh * N_SAMPLE:(hh + 1) * N_SAMPLE], new_nat[:, 2, h * P:(h + 1) * P],
                              att_new[:, hh, :], start=True, stop=True)
                last.then_inc(sig["on_full"], 1)
                pe.wait_ge(sig["klb_ready"], p + 1)
                for b in range(DEC_BATCH):
                    last = mm(PS[:, [6, 7, 4, 5][b // 2], (b % 2) * 256:(b % 2) * 256 + 256], kl_batch[:, b, :],
                              new_nat[:, 2, p * 256:(p + 1) * 256], start=True, stop=True)
                last.then_inc(sig["sn_full"], 1)

            pe.wait_ge(sig["sn_out"], 2)
            pe.wait_ge(sig["og_out"], 4)
            pe.wait_ge(sig["on_out"], 3)
            for i in range(KD):
                t = T0["merge"] + i
                open_t(t)
                pe.wait_ge(sig["m_sq"], i + 1)
                for half in range(2):
                    last = mm(PS[:, 4 * (t % 2) + half, 0:HALF], (ones if i < 4 else ones64)[:],
                              sq[:, i % 2, half * HALF:(half + 1) * HALF], start=True, stop=True)
                last.then_inc(sig["psum_full"], 1)
            product("out", 4, 2, KD, A, a_tiles(2))
            pe.wait_ge(sig["p_in"], 16 * 5)
            for k in range(2):
                t = T0["p"] + k
                open_t(t)
                for n in range(4):
                    nc.tensor.transpose(PS[:, 4 * (t % 2), n * P:(n + 1) * P], rows[:, n, k * P:(k + 1) * P], ident[:])
                nc.tensor.transpose(PS[:, 4 * (t % 2) + 1, 0:N_SAMPLE], rows[0:N_SAMPLE, 4, k * P:(k + 1) * P],
                                    ident[0:N_SAMPLE, 0:N_SAMPLE]).then_inc(sig["psum_full"], 1)
            sum_norm(3)
            ffn("f2", 3, F_TILES, 4)
            for s_ in range(1, 4):
                embed(s_)
            product("gate", 4, 2, KD, A, a_tiles(4), 6)
            sum_norm(7)
            for k in range(KD):
                t = T0["y"] + k
                open_t(t)
                pe.wait_ge(sig["x_ready"], 8 * 3 + k + 1)
                for n in range(4):
                    nc.tensor.transpose(PS[:, 4 * (t % 2), n * P:(n + 1) * P], flat(x[:, k])[:, n * P:(n + 1) * P],
                                        ident[:])
                nc.tensor.transpose(PS[0:N_SAMPLE, 4 * (t % 2) + 1, 0:P], flat(x[:, k])[:, SEQ:T],
                                    ident[:]).then_inc(sig["psum_full"], 1)

        up_base = {"f1_up0": 0, "f1_up1": GROUPS[0], "f2_up0": F_TILES, "f2_up1": F_TILES + GROUPS[0]}
        h_slot = lambda name: 0

        @block.scalar
        def _(act):
            fn = nc.scalar.activation

            def split(st, name, t):
                nxt, w0 = Step(st.c + 1, st.i), W0[name]
                slot, width = nxt.parity(w0), widths[w0 + st.c + 1]
                act.wait_ge(raw_in[slot], 32 * (nxt.half(w0) + 1))
                if t is not None:
                    act.wait_ge(sig["psum_full"], t)
                fn(w_hi[:, slot, 0:width], raw[:, slot, 0:width], ACT.Copy).then_inc(sig["split_hi"], 1)

            def norm(j):
                t, r = sum_ticket[j], rstd[:, j % 2]
                full(act, t)
                fn(r, banks(t % 2, 0, 2), ACT.Ln, bias=eps[:], scale=1.0 / D_MODEL).then_inc(psum_free[t % 2], 1)
                act.wait_ge(psum_free[t % 2], t // 2 + 1)
                fn(r, r, ACT.Exp, scale=-0.5).then_inc(sig["rstd_ready"], 1)

            def square(j, k, src):
                n = 8 * j + k
                if n >= 2:
                    act.wait_ge(sig["sq_used"], n - 1)
                fn(sq[:, k % 2, :], src, ACT.Square).then_inc(sig["sq_ready"], 1)

            def input_tile(k, name, j):
                c = VEC[name] + k
                fn(a_hi[:, k, :], flat(x[:, k]), ACT.Copy, scale=vec[:, c:c + 1]).then_inc(sig["a_hi_ready"], 1)
                square(j, k, flat(x[:, k]))

            def boundary(b, name, j, behind=None):
                for k in range(KD):
                    act.wait_ge(sig["x_ready"], 8 * b + k + 1)
                    input_tile(k, name, j)
                    if behind and k in (1, 3, 5):
                        behind(k // 2 + 1)

            def stage(name, n, body, after_first=None, table=None):
                def one(st):
                    t, quad, use = ticket(st, name)
                    if W0[name] + st.c + 1 < n_w and (st.c or name not in SPLIT_EARLY):
                        split(st, name, t)
                    if st.c == 0 and after_first is not None:
                        norm(after_first)
                        nc.scalar.preload_act_table(table)
                    body(st, t, quad, use)
                one(Step(0))
                steps(act, 1, n - 1, one)
                one(Step(n - 1))

            def up(name):
                base = up_base[name]
                h0 = base % F_TILES

                def body(st, t, quad, use):
                    n = base + st.n
                    act.wait_ge(sig["g_ready"], n + 1)
                    fn(gs, gs, ACT.Silu).then_inc(sig["silu_ready"], 1)
                    act.wait_ge(sig["h_raw"], n + 1)
                    fn(h_hi[:, bass.ds(st.n, 1), :].rearrange("p a t -> p (a t)"), flat(us),
                       ACT.Copy).then_inc(sig["h_hi_ready"], 1)
                return body

            def down0(st, t, quad, use):
                full(act, t)
                fn(y[:, bass.ds(st.n, 1)].rearrange("p k a t -> p (k a) t"), banks(quad, 0, 2),
                   ACT.Copy).then_inc(psum_free[quad], 1)

            def down1(j):
                def body(st, t, quad, use):
                    act.wait_ge(psum_free[quad], use + 1)
                    n = 8 * j + st.n
                    act.wait_ge(sig["sq_used"], n - 1)
                    fn(sq[:, st.parity(0), :], y[:, bass.ds(st.n, 1)].rearrange("p k a t -> p (k a t)"),
                       ACT.Square).then_inc(sig["sq_ready"], 1)
                return body

            def ffn(name, j):
                stage(f"{name}_up0", GROUPS[0], up(f"{name}_up0"), after_first=j, table=ACT.Silu)
                stage(f"{name}_down0", KD, down0)
                stage(f"{name}_up1", GROUPS[1], up(f"{name}_up1"))
                nc.scalar.preload_act_table_set("natural_log_exp_and_others")
                stage(f"{name}_down1", KD, down1(j + 1))
                if name == "f1":
                    split(Step(0), "in", T0["f1_post"])
                else:
                    split(Step(0), "embed", T0["embed_first"])
                norm(j + 1)

            nc.scalar.preload_act_table_set("natural_log_exp_and_others")
            for name in NORMS:
                act.dma_start(vec_rows[VEC[name]:VEC[name] + 8, :],
                              a[name][0].rearrange("(k p) -> k p", p=P)).then_inc(sig["vec_in"], 16)
            act.dma_start(vec_rows[64:66, :], a["gate_b"][0].rearrange("(k p) -> k p", p=P)).then_inc(sig["vec_in"], 16)
            act.dma_start(vec_rows[66:67, :], a["gla_norm"]).then_inc(sig["vec_in"], 16)
            for n in range(2):
                act.dma_start(vec_rows[67:68, n * 64:(n + 1) * 64], a["sb_norm"]).then_inc(sig["vec_in"], 16)
            act.dma_start(bias_row[:], a["sb_bias"]).then_inc(sig["vec_in"], 16)
            act.dma_start(gate_w[:], a["gate_w"][0]).then_inc(sig["vec_in"], 16)

            act.wait_ge(raw_in[0], 32)
            fn(w_hi[:, 0, :], raw[:, 0, :], ACT.Copy).then_inc(sig["split_hi"], 1)
            split(Step(0), "f1_up0", None)
            act.wait_ge(sig["vec_ready"], 3)
            for k in range(KD):
                t = T0["x"] + k
                act.wait_ge(psum_free[t % 2], t // 2 + 1)
                input_tile(k, "f1_pre", 0)
            ffn("f1", 0)
            boundary(0, "mix_pre", 2)

            def in_body(st, t, quad, use):
                if st.c == 12:
                    act.wait_ge(psum_free[1 - quad], (t + 1) // 2)
                    fn(proj[:, GG:GG + 4], proj[:, GG:GG + 4], ACT.Silu).then_inc(sig["gg_ready"], 1)
                    nc.scalar.preload_act_table_set("natural_log_exp_and_others")

            stage("in", 13, in_body, after_first=2, table=ACT.Silu)

            for n, dst in ((0, k_nat), (2, gv_nat)):
                t = T0["natural"] + n
                full(act, t)
                fn(dst[:], PS[:, 4 * (t % 2):4 * (t % 2) + 4, :], ACT.Copy).then_inc(psum_free[t % 2], 1)

            act.wait_ge(sig["psum_full"], T0["merge"])

            def turned(j):
                act.wait_ge(sig["kt_full"], j + 1)
                fn(k_turned[:, j % 2, :], PS[:, 7, :], ACT.Copy).then_inc(sig["kt_out"], 1)

            def page_logits(b):
                return fn(z_past.rearrange("p (q b n) -> p q b n", q=8, b=DEC_BATCH)[:, :, b, :],
                          PS[:, 2, 384:448].rearrange("p (q n) -> p q n", q=8), ACT.Copy)

            def logits(h):
                z_ = sb_z[h % 2]
                act.wait_ge(sig["z_full"], h + 1)
                if h >= 2:
                    page_logits(h - 2)
                if h >= 2:
                    act.wait_ge(sig["d_ready"], h - 1)
                fn(z_[:, 0:512], PS[:, 0, :], ACT.Identity, bias=bias[:, h:h + 1], scale=SB_DH ** -0.5)
                fn(z_[:, 512:1280].rearrange("p (a n) -> p a n", a=2), PS[:, 1:3, 0:384], ACT.Identity,
                   bias=bias[:, h:h + 1], scale=SB_DH ** -0.5).then_inc(sig["z_out"], 1)

            def log_part(n, s_):
                act.wait_ge(sig["abs_ready"], n + 1)
                fn(s_, s_, ACT.Exp, scale=-1.0).then_inc(sig["e_ready"], 1)
                act.wait_ge(sig["e_ready"], n + 1)
                fn(s_, s_, ACT.Ln, bias=1.0).then_inc(sig["soft_log"], 1)

            def weight(n, w_):
                act.wait_ge(sig["d_ready"], n + 1)
                fn(w_, w_, ACT.Exp).then_inc(sig["w_ready"], 1)

            logits(0)
            log_part(0, sb_s[0])
            for h in range(SB_HEADS):
                if h + 1 < SB_HEADS:
                    logits(h + 1)
                else:
                    act.wait_ge(sig["z_full"], h + 2)
                    page_logits(h - 1).then_inc(sig["z_out"], 1)
                turned(2 * h)
                if h + 1 < SB_HEADS:
                    log_part(h + 1, sb_s[(h + 1) % 2])
                turned(2 * h + 1)
                weight(h, sb_w[h % 2])

            act.wait_ge(sig["z_full"], SB_HEADS + 2)
            page_logits(SB_HEADS - 1).then_inc(sig["z_out"], 1)
            log_part(SB_HEADS, s_past)
            log_part(SB_HEADS + 1, s_new)
            weight(SB_HEADS, w_past)
            weight(SB_HEADS + 1, w_new)

            for p in range(2):
                act.wait_ge(sig["la_abs"], p + 1)
                fn(la_soft, la_soft, ACT.Exp, scale=-1.0).then_inc(sig["la_log"], 1)
                act.wait_ge(sig["la_log"], 2 * p + 1)
                fn(la_soft, la_soft, ACT.Ln, bias=1.0).then_inc(sig["la_log"], 1)
            for p in range(2):
                act.wait_ge(sig["cum_ready"], 2)
                if p:
                    act.wait_ge(sig["lev_k"], LEVELS * p)
                    act.wait_ge(sig["lev_q"], LEVELS * p)
                fn(decay[0], cum[:, p, :], ACT.Exp, scale=1.0 / 16).then_inc(sig["eb_ready"], 1)
                if p:
                    act.wait_ge(sig["state_ready"], N_CH * p)
                    act.wait_ge(sig["sn_decayed"], p)
                fn(decay_last[:, 0:N_CH], cum[:, p, CH - 1:SEQ:CH], ACT.Exp, scale=1.0 / 16)
                fn(decay_last[:, N_CH:], cum[:, p, SEQ + DEC_SEQ - 1:T:DEC_SEQ], ACT.Exp,
                   scale=1.0 / 16).then_inc(sig["last_ready"], 1)
                act.wait_ge(sig["kl_diff"], p + 1)
                fn(decay[1], decay[1], ACT.Exp, scale=1.0 / 16).then_inc(sig["kl_exp"], 1)
                for li in range(1, LEVELS + 1):
                    n_tok = T if li <= 2 else SEQ
                    act.wait_ge(sig["lev_diff"], LEVELS * p + li)
                    d_ = decay[li % 2][:, 0:n_tok]
                    fn(d_, d_, ACT.Exp, scale=1.0 / 16).then_inc(sig["lev_exp"], 1)
                    if li == 2:
                        act.wait_ge(sig["klt_full"], p + 1)
                        if p:
                            act.wait_ge(sig["u_full"], p)
                        fn(kl_nat, PS[:, 6, :].rearrange("p (c n) -> p c n", c=N_CH), ACT.Copy)
                        fn(kl_new[:], PS[0:N_SAMPLE, 7, 0:P], ACT.Copy).then_inc(sig["klt_out"], 1)
                for hh in range(2):
                    h = 2 * p + hh
                    act.wait_ge(sig["og_full"], h + 1)
                    fn(flat(y[:, h])[:, 0:SEQ], PS[:, hh, :], ACT.Copy).then_inc(sig["og_out"], 1)
                act.wait_ge(sig["inter_full"], p + 1)
                if p:
                    act.wait_ge(sig["on_out"], 1 + p)
                fn(inter_new.rearrange("p b h t -> p (b h t)"), PS[:, 2, 0:64], ACT.Copy).then_inc(sig["inter_out"], 1)

            act.wait_ge(sig["nat_stored"], 16 * 2)
            act.wait_ge(sig["state_stored"], 16 * 2)
            act.wait_ge(sig["sn_out"], 2)

            def head_square(i):
                if i >= 2:
                    full(act, T0["merge"] + i - 2)
                elif i == 1:
                    act.wait_ge(sig["klt_full"], 2)
                act.wait_ge(sig["og_out"], 4)
                act.wait_ge(sig["on_out"], 3)
                fn(sq[:, i % 2, :], flat(y[:, i]), ACT.Square).then_inc(sig["m_sq"], 1)

            head_square(0)
            for i in range(KD):
                if i + 1 < KD:
                    head_square(i + 1)
                t, r = T0["merge"] + i, rstd[:, i % 2]
                full(act, t)
                if i >= 2:
                    act.wait_ge(sig["m_ready"], i - 1)
                fn(r, banks(t % 2, 0, 2), ACT.Ln, bias=eps[:],
                   scale=1.0 / (GLA_DV if i < 4 else SB_DH)).then_inc(psum_free[t % 2], 1)
                act.wait_ge(psum_free[t % 2], t // 2 + 1)
                fn(r, r, ACT.Exp, scale=-0.5).then_inc(sig["m_norm"], 1)
                act.wait_ge(sig["m_ready"], i + 1)
                fn(a_hi[:, i, :], decay[i % 2], ACT.Copy).then_inc(sig["a_hi_ready"], 1)

            def out_body(st, t, quad, use):
                full(act, t)
                fn(y[:, 2 * st.c:2 * st.c + 2].rearrange("p k a t -> p (k a) t"), banks(quad, 0, 4),
                   ACT.Copy).then_inc(psum_free[quad], 1)
                act.wait_ge(psum_free[quad], use + 1)
                for c in range(2):
                    square(3, 2 * st.c + c, flat(y[:, 2 * st.c + c]))

            for n in range(4):
                t, quad, use = ticket(Step(n), "out")
                split(Step(n), "out", t)
                out_body(Step(n), t, quad, use)
            act.wait_ge(sig["a_lo_ready"], 24)
            for k in range(2):
                t = T0["p"] + k
                full(act, t)
                fn(p_hi[:, k, 0:SEQ], PS[:, 4 * (t % 2), :], ACT.Copy)
                fn(p_hi[:, k, SEQ:T], PS[:, 4 * (t % 2) + 1, 0:N_SAMPLE], ACT.Copy).then_inc(sig["p_hi_ready"], 1)
            split(Step(0), "f2_up0", T0["p"])
            norm(3)
            boundary(1, "f2_pre", 4)
            ffn("f2", 4)

            def e_tiles(n):
                t = embed_ticket(n)
                full(act, t)
                fn(e[:, 2 * n:2 * n + 2].rearrange("p k a t -> p (k a) t"), banks(t % 2, 0, 4),
                   ACT.Copy).then_inc(psum_free[t % 2], 1)

            boundary(2, "ple_pre", 6, e_tiles)
            for n in range(4):
                t, quad, use = ticket(Step(n), "gate")
                if n < 3:
                    split(Step(n), "gate", t)
                if n == 0:
                    norm(6)
                    nc.scalar.preload_act_table(ACT.Sigmoid)
                for c in range(2):
                    k = 2 * n + c
                    act.wait_ge(*((psum_free[quad], use + 1) if c else (sig["pg_ready"], n + 1)))
                    fn(work[:, c, :], work[:, c, :], ACT.Sigmoid).then_inc(sig["pg_sig"], 1)
                for c in range(2):
                    k = 2 * n + c
                    act.wait_ge(sig["pg_out"], k + 1)
                    square(7, k, flat(y[:, k]))
            nc.scalar.preload_act_table_set("natural_log_exp_and_others")
            norm(7)
            for k in range(KD):
                t = T0["y"] + k
                full(act, t)
                cols = slice(k * P, (k + 1) * P)
                fn(rows[:, 0:4, cols], PS[:, 4 * (t % 2), :].rearrange("p (n c) -> p n c", n=4), ACT.Copy)
                fn(rows[0:N_SAMPLE, 4, cols], PS[0:N_SAMPLE, 4 * (t % 2) + 1, 0:P], ACT.Copy).then_inc(psum_free[t % 2], 1)

        @block.vector
        def _(dve):
            v = nc.vector

            def split(st, name):
                nxt, w0 = Step(st.c + 1, st.i), W0[name]
                slot, width = nxt.parity(w0), widths[w0 + st.c + 1]
                dve.wait_ge(sig["split_hi"], w0 + nxt.n + 1)
                v.tensor_tensor(w_lo[:, slot, 0:width], raw[:, slot, 0:width],
                                w_hi[:, slot, 0:width].bitcast(F32), ALU.subtract).then_inc(sig["split_lo"], 1)

            def input_tile(k, name, stage_no):
                c = VEC[name] + k
                dve.wait_ge(sig["a_hi_ready"], 8 * stage_no + k + 1)
                v.scalar_tensor_tensor(a_lo[:, k, :], flat(x[:, k]), vec[:, c:c + 1], a_hi[:, k, :].bitcast(F32),
                                       ALU.mult, ALU.subtract).then_inc(sig["a_lo_ready"], 1)

            def boundary(b, j, post, pre=None, stage_no=None):
                dve.wait_ge(sig["rstd_ready"], j + 1)

                def update(k):
                    n, c = 8 * b + k, VEC[post] + k
                    v.scalar_tensor_tensor(work[:, k % 2, :], flat(y[:, k]), vec[:, c:c + 1], flat(rstd[:, j % 2]),
                                           ALU.mult, ALU.mult).then_inc(sig["upd_ready"], 1)

                update(0)
                for k in range(KD):
                    n = 8 * b + k
                    if k:
                        dve.wait_ge(sig["x_ready"], n)
                    if k + 1 < KD:
                        update(k + 1)
                    dve.wait_ge(sig["upd_ready"], n + 1)
                    v.tensor_tensor(flat(x[:, k]), work[:, k % 2, :], flat(x[:, k]), ALU.add).then_inc(sig["x_ready"], 1)
                    if pre and k:
                        input_tile(k - 1, pre, stage_no)
                if pre:
                    input_tile(KD - 1, pre, stage_no)

            def stage(name, n, body, after_first=None):
                def one(st):
                    t, quad, use = ticket(st, name)
                    if st.c or name not in SPLIT_EARLY:
                        split(st, name)
                    if st.c == 0 and after_first is not None:
                        dve.wait_ge(sig["rstd_ready"], after_first + 1)
                    body(st, t, quad, use)
                one(Step(0))
                steps(dve, 1, n - 1, one)
                one(Step(n - 1))

            def up(name, j):
                base = up_base[name]

                def body(st, t, quad, use):
                    n, r = base + st.n, rstd[:, j % 2]
                    full(dve, t)
                    dve.wait_ge(sig["h_lo_ready"], n)
                    v.tensor_tensor(gs, banks(quad, 0, 2), r, ALU.mult).then_inc(sig["g_ready"], 1)
                    v.tensor_tensor(us, banks(quad, 2, 2), r, ALU.mult).then_inc(psum_free[quad], 1)
                    dve.wait_ge(psum_free[quad], use + 1)
                    dve.wait_ge(sig["silu_ready"], n + 1)
                    v.tensor_tensor(us, us, gs, ALU.mult).then_inc(sig["h_raw"], 1)
                    dve.wait_ge(sig["h_hi_ready"], n + 1)
                    hs = bass.ds(st.n, 1)
                    v.tensor_tensor(h_lo[:, hs, :].rearrange("p a t -> p (a t)"), flat(us),
                                    h_hi[:, hs, :].bitcast(F32).rearrange("p a t -> p (a t)"),
                                    ALU.subtract).then_inc(sig["h_lo_ready"], 1)
                return body

            def down1(st, t, quad, use):
                full(dve, t)
                yt = y[:, bass.ds(st.n, 1)].rearrange("p k a t -> p (k a) t")
                v.tensor_tensor(yt, banks(quad, 0, 2), yt, ALU.add).then_inc(psum_free[quad], 1)

            def ffn(name, j):
                stage(f"{name}_up0", GROUPS[0], up(f"{name}_up0", j), after_first=j)
                stage(f"{name}_down0", KD, lambda st, t, quad, use: None)
                stage(f"{name}_up1", GROUPS[1], up(f"{name}_up1", j))
                stage(f"{name}_down1", KD, down1)

            full(dve, 0)
            v.tensor_copy(vec[:], PS[:, 0, 0:N_VEC]).then_inc(sig["vec_ready"], 1)
            v.tensor_copy(bias[:], PS[:, 1, 0:SB_HEADS]).then_inc(psum_free[0], 1)
            dve.wait_ge(sig["vec_ready"], 1)
            for name in ("f1_post", "f2_post"):
                c = VEC[name]
                v.tensor_scalar(vec[:, c:c + 8], vec[:, c:c + 8], 0.5, None, ALU.mult).then_inc(sig["vec_ready"], 1)
            for k in range(KD + 1):
                if k < KD:
                    t = T0["x"] + k
                    full(dve, t)
                    v.tensor_copy(flat(x[:, k])[:, SEQ:T], PS[:, 4 * (t % 2) + 1, 0:N_SAMPLE])
                    v.tensor_copy(flat(x[:, k])[:, 0:SEQ], PS[:, 4 * (t % 2), :]).then_inc(psum_free[t % 2], 1)
                if k == 2:
                    dve.wait_ge(sig["split_hi"], 1)
                    v.tensor_tensor(w_lo[:, 0, :], raw[:, 0, :], w_hi[:, 0, :].bitcast(F32),
                                    ALU.subtract).then_inc(sig["split_lo"], 1)
                if k == 5:
                    split(Step(0), "f1_up0")
                if k >= 1:
                    input_tile(k - 1, "f1_pre", 0)
            ffn("f1", 0)
            split(Step(0), "in")
            boundary(0, 1, "f1_post", "mix_pre", 1)

            def project(st, t, quad, use):
                full(dve, t)
                if st.c == 12:
                    v.tensor_tensor(glr[:], PS[0:GLA_RANK, 4 * quad:4 * quad + 2, 0:HALF], rstd[0:GLA_RANK, 0],
                                    ALU.mult).then_inc(psum_free[quad], 1)
                elif st.c == 0:
                    for c in range(2):
                        ins = v.scalar_tensor_tensor(proj[:, GQ + c], banks(quad, 2 * c, 2), GLA_DK ** -0.5,
                                                     rstd[:, 0], ALU.mult, ALU.mult)
                    ins.then_inc(psum_free[quad], 1)
                else:
                    v.tensor_tensor(proj[:, bass.ds(2 * st.n, 2)],
                                    banks(quad, 0, 4).rearrange("p (c a) t -> p c a t", c=2),
                                    rstd[:, 0:1].broadcast_to([P, 2, 2, HALF]), ALU.mult).then_inc(psum_free[quad], 1)

            stage("in", 13, project, after_first=2)
            for n, dst, src in ((1, v_nat[:], lambda q: PS[:, 4 * q:4 * q + 4, :]),
                                (3, new_nat[:], lambda q: PS[0:N_SAMPLE, 4 * q:4 * q + 3, :])):
                t = T0["natural"] + n
                full(dve, t)
                v.tensor_copy(dst, src(t % 2)).then_inc(psum_free[t % 2], 1)

            def magnitudes(h):
                z_ = sb_z[h % 2]
                dve.wait_ge(sig["z_out"], h + 1)
                diag = z_[:, 0:512].rearrange("p (j q) -> p j q", j=4)
                v.tensor_tensor(diag, diag, neg_diag[:].unsqueeze(1).broadcast_to([P, 4, P]),
                                ALU.add).then_inc(sig["z_masked"], 1)
                dve.wait_ge(sig["z_masked"], h + 1)
                if h >= 2:
                    dve.wait_ge(sig["c_full"], h - 1)
                v.scalar_tensor_tensor(sb_s[h % 2], z_, -1.0, z_, ALU.mult, ALU.max).then_inc(sig["abs_ready"], 1)

            def softplus(n, z_, s_):
                dve.wait_ge(sig["soft_log"], n + 1)
                v.scalar_tensor_tensor(s_, z_, 0.0, s_, ALU.max, ALU.add).then_inc(sig["sp_ready"], 1)

            def exponents(h):
                z_, w_ = sb_z[h % 2], sb_w[h % 2]
                dve.wait_ge(sig["c_full"], h + 1)
                if h >= 2:
                    dve.wait_ge(sig["o_full"], h - 1)
                v.tensor_tensor(w_[:, 0:512], z_[:, 0:512], PS[:, 4, :], ALU.subtract)
                v.tensor_tensor(w_[:, 512:1280].rearrange("p (a n) -> p a n", a=2),
                                z_[:, 512:1280].rearrange("p (a n) -> p a n", a=2), PS[:, 5:7, 0:384],
                                ALU.subtract).then_inc(sig["d_ready"], 1)

            def head_out(h):
                r = slice(64 * (h % 2), 64 * (h % 2) + 64)
                dve.wait_ge(sig["o_full"], h + 1)
                v.tensor_copy(flat(y[:, 4 + h // 2])[r, 0:SEQ], PS[r, 3, :]).then_inc(sig["o_out"], 1)

            magnitudes(0)
            softplus(0, sb_z[0], sb_s[0])
            for h in range(SB_HEADS):
                if h + 1 < SB_HEADS:
                    magnitudes(h + 1)
                exponents(h)
                if h + 1 < SB_HEADS:
                    softplus(h + 1, sb_z[(h + 1) % 2], sb_s[(h + 1) % 2])
                if h >= 1:
                    head_out(h - 1)
            head_out(SB_HEADS - 1)

            new = slice(0, N_SAMPLE)
            cols = bias_cols.rearrange("p a b c -> p (a b c)")
            dve.wait_ge(sig["setup_new"], 1)
            dve.wait_ge(sig["zs_full"], 1)
            dve.wait_ge(sig["z_out"], SB_HEADS + 2)
            v.scalar_tensor_tensor(z_past.rearrange("p (a n) -> p a n", a=2),
                                   z_past.rearrange("p (a n) -> p a n", a=2), SB_DH ** -0.5,
                                   cols.unsqueeze(1).broadcast_to([P, 2, 256]), ALU.mult, ALU.add).then_inc(sig["zs_out"], 1)
            v.scalar_tensor_tensor(z_new, PS[new, 7, 0:256], SB_DH ** -0.5, cols[new, :], ALU.mult,
                                   ALU.add).then_inc(sig["zs_out"], 1)
            dve.wait_ge(sig["zs_out"], 2)
            v.tensor_tensor(z_new, z_new, neg_cols.rearrange("p a b c -> p (a b c)"), ALU.add).then_inc(sig["z_masked"], 1)
            v.scalar_tensor_tensor(s_past, z_past, -1.0, z_past, ALU.mult, ALU.max).then_inc(sig["abs_ready"], 1)
            dve.wait_ge(sig["z_masked"], SB_HEADS + 1)
            v.scalar_tensor_tensor(s_new, z_new, -1.0, z_new, ALU.mult, ALU.max).then_inc(sig["abs_ready"], 1)
            softplus(SB_HEADS, z_past, s_past)
            softplus(SB_HEADS + 1, z_new, s_new)
            dve.wait_ge(sig["c_full"], SB_HEADS + 1)
            v.tensor_tensor(w_past, z_past, PS[:, 0, :], ALU.subtract).then_inc(sig["d_ready"], 1)
            v.tensor_tensor(w_new, z_new, PS[new, 1, 0:256], ALU.subtract).then_inc(sig["d_ready"], 1)
            for p in range(2):
                dve.wait_ge(sig["la_full"], p + 1)
                dve.wait_ge(sig["cum_ready"], p)
                v.tensor_scalar(rstd[:, 0], PS[:, 6:8, 0:HALF], vec[:, 64 + p:65 + p], None,
                                ALU.add).then_inc(sig["la_sum"], 1)
                dve.wait_ge(sig["la_sum"], p + 1)
                v.scalar_tensor_tensor(la_soft, la_raw, -1.0, la_raw, ALU.mult, ALU.max).then_inc(sig["la_abs"], 1)
                dve.wait_ge(sig["la_log"], 2 * p + 2)
                v.scalar_tensor_tensor(la_raw, la_raw, 0.0, la_soft, ALU.min, ALU.subtract).then_inc(sig["la_soft_ready"], 1)
                dve.wait_ge(sig["la_soft_ready"], p + 1)
                for c in range(N_CH):
                    tok = slice(c * P, (c + 1) * P)
                    v.tensor_tensor_scan(cum[:, p, tok], ones[:], la_raw[:, tok], 0.0, ALU.mult, ALU.add)
                v.tensor_tensor_scan(cum[:, p, SEQ:T], scan_keep[:], la_raw[:, SEQ:T], 0.0, ALU.mult,
                                     ALU.add).then_inc(sig["cum_ready"], 1)
            dve.wait_ge(sig["n_out"], DEC_BATCH * N_PAGES)
            for hh in range(2):
                r = slice(64 * hh, 64 * hh + 64)
                dst = y[r, 4:8].rearrange("p k a t -> p k (a t)")[:, :, SEQ:T].rearrange("p k (b t) -> p k b t", t=DEC_SEQ)
                src = PS[r, 2:6, 0:64].rearrange("p k (b h t) -> p k h b t", h=2, t=DEC_SEQ)[:, :, hh]
                ins = v.tensor_copy(dst, src)
            ins.then_inc(sig["on_out"], 1)

            for p in range(2):
                n_att = (LEVELS + 1) * p
                gq, gk = flat(proj[:, GQ + p]), flat(proj[:, GK + p])
                dve.wait_ge(sig["cum_ready"], 2)
                chunks = cum[:, p, 0:SEQ].rearrange("p (c t) -> p c t", t=CH)
                batches = cum[:, p, SEQ:T].rearrange("p (c t) -> p c t", t=DEC_SEQ)
                if p:
                    dve.wait_ge(sig["lev_k"], LEVELS * p)
                    dve.wait_ge(sig["lev_q"], LEVELS * p)
                v.tensor_tensor(decay[1][:, 0:SEQ].rearrange("p (c t) -> p c t", t=CH),
                                chunks[:, :, CH - 1:CH].broadcast_to([P, N_CH, CH]), chunks, ALU.subtract)
                v.tensor_tensor(decay[1][:, SEQ:T].rearrange("p (c t) -> p c t", t=DEC_SEQ),
                                batches[:, :, DEC_SEQ - 1:DEC_SEQ].broadcast_to([P, DEC_BATCH, DEC_SEQ]), batches,
                                ALU.subtract).then_inc(sig["kl_diff"], 1)
                dve.wait_ge(sig["eb_ready"], p + 1)
                if p:
                    dve.wait_ge(sig["og_full"], 2 * p)
                    dve.wait_ge(sig["inter_full"], p)
                    dve.wait_ge(sig["qe_ready"], 2 * p)
                v.tensor_tensor(q_dec, gq, decay[0], ALU.mult).then_inc(sig["qe_ready"], 1)
                v.memset(q_new, 0.0).then_inc(sig["qz_ready"], 1)
                dve.wait_ge(sig["qe_ready"], 2 * p + 1)
                dve.wait_ge(sig["qz_ready"], p + 1)
                for hh in range(2):
                    r = slice(64 * hh, 64 * hh + 64)
                    ins = v.tensor_copy(q_new[r, :, hh, :], q_dec[r, SEQ:T].rearrange("p (b t) -> p b t", t=DEC_SEQ))
                ins.then_inc(sig["qe_ready"], 1)
                dve.wait_ge(sig["kl_exp"], p + 1)
                if p:
                    dve.wait_ge(sig["klt_full"], p)
                v.tensor_tensor(kl, gk, decay[1], ALU.mult).then_inc(sig["kl_ready"], 1)

                def level_diff(li):
                    half, n_tok = 1 << (li - 1), (T if li <= 2 else SEQ)
                    if li >= 3:
                        dve.wait_ge(sig["lev_k"], LEVELS * p + li - 2)
                        dve.wait_ge(sig["lev_q"], LEVELS * p + li - 2)
                    elif li == 1:
                        dve.wait_ge(sig["kl_ready"], p + 1)
                    b_ = cum[:, p, 0:n_tok].rearrange("p (n a t) -> p n a t", a=2, t=half)
                    d_ = decay[li % 2][:, 0:n_tok].rearrange("p (n a t) -> p n a t", a=2, t=half)
                    ref = b_[:, :, 0, half - 1:half].broadcast_to([P, n_tok // (2 * half), half])
                    v.tensor_tensor(d_[:, :, 0, :], ref, b_[:, :, 0, :], ALU.subtract)
                    v.tensor_tensor(d_[:, :, 1, :], b_[:, :, 1, :], ref, ALU.subtract).then_inc(sig["lev_diff"], 1)

                def level_q(li):
                    n_tok = T if li <= 2 else SEQ
                    dve.wait_ge(sig["lev_exp"], LEVELS * p + li)
                    if n_att + li >= 3:
                        dve.wait_ge(sig["lev_full"], n_att + li - 1)
                    v.tensor_tensor(q_lev[li % 2][:, 0:n_tok], gq[:, 0:n_tok], decay[li % 2][:, 0:n_tok],
                                    ALU.mult).then_inc(sig["lev_q"], 1)

                def level_scores(li):
                    dve.wait_ge(sig["lev_full"], n_att + li + 1)
                    src = PS[:, 2 * (li % 2):2 * (li % 2) + 2, :].rearrange("p a (c t) -> p (a c) t", t=P)
                    src_new = PS[0:N_SAMPLE, 4:6, 0:N_SAMPLE]
                    if li == 0:
                        v.tensor_tensor(att_new, src_new, ident[0:N_SAMPLE, 0:N_SAMPLE].unsqueeze(1).broadcast_to(
                            [N_SAMPLE, 2, N_SAMPLE]), ALU.mult)
                        v.tensor_tensor(att, src, ident[:].unsqueeze(1).broadcast_to([P, 8, P]),
                                        ALU.mult).then_inc(sig["att_out"], 1)
                        return
                    dve.wait_ge(sig["att_out"], n_att + li)
                    mask = level_mask[:, li - 1, :].bitcast(U32)
                    if li <= 2:
                        v.copy_predicated(att_new, mask[0:N_SAMPLE, 0:N_SAMPLE].unsqueeze(1).broadcast_to(
                            [N_SAMPLE, 2, N_SAMPLE]), src_new)
                    v.copy_predicated(att, mask.unsqueeze(1).broadcast_to([P, 8, P]), src).then_inc(sig["att_out"], 1)

                if p:
                    dve.wait_ge(sig["on_full"], p)
                level_diff(1)
                for li in range(1, LEVELS + 1):
                    if li < LEVELS:
                        level_diff(li + 1)
                    level_q(li)
                    level_scores(li - 1)
                    if li == 4:
                        dve.wait_ge(sig["klt_out"], p + 1)
                        if p:
                            dve.wait_ge(sig["sn_full"], p)
                        v.tensor_tensor(kl_batch, kl_new[:].unsqueeze(1).broadcast_to([N_SAMPLE, DEC_BATCH, P]),
                                        batch_mask[0:N_SAMPLE, :].unsqueeze(2).broadcast_to([N_SAMPLE, DEC_BATCH, P]),
                                        ALU.mult).then_inc(sig["klb_ready"], 1)
                level_scores(LEVELS)
                dve.wait_ge(sig["u_full"], p + 1)
                dve.wait_ge(sig["last_ready"], p + 1)
                if p:
                    dve.wait_ge(sig["state_stored"], 16 * p)
                    dve.wait_ge(sig["state_ready"], N_CH * p)
                v.tensor_copy(state[:, 0, :], PS[:, 5, 0:P]).then_inc(sig["state_ready"], 1)
                for c in range(1, N_CH):
                    dve.wait_ge(sig["state_ready"], N_CH * p + c)
                    v.scalar_tensor_tensor(state[:, c, :], state[:, c - 1, :], decay_last[:, c:c + 1],
                                           PS[:, 5, c * P:(c + 1) * P], ALU.mult, ALU.add).then_inc(sig["state_ready"], 1)
                dve.wait_ge(sig["on_full"], p + 1)
                dve.wait_ge(sig["inter_out"], p + 1)
                for hh in range(2):
                    ins = v.tensor_tensor(flat(y[:, 2 * p + hh])[:, SEQ:T].rearrange("p (b t) -> p b t", t=DEC_SEQ),
                                          PS[:, 3, hh * N_SAMPLE:(hh + 1) * N_SAMPLE].rearrange("p (b t) -> p b t", t=DEC_SEQ),
                                          inter_new[:, :, hh, :], ALU.add)
                ins.then_inc(sig["on_out"], 1)
                dve.wait_ge(sig["sn_full"], p + 1)
                dve.wait_ge(sig["sn_decayed"], p + 1)
                for hh in range(2):
                    r = slice(64 * hh, 64 * hh + 64)
                    for part, b0 in ((0, 6), (1, 4)):
                        src = PS[r, b0:b0 + 2, :].rearrange("p a (b h v) -> p (a b) h v", b=2, h=2)[:, :, hh, :]
                        st_ = state_new[r, 4 * part:4 * part + 4, :]
                        ins = v.tensor_tensor(st_, src, st_, ALU.add)
                ins.then_inc(sig["sn_out"], 1)

            for i in range(KD):
                m_, c = decay[i % 2], (VEC["gla_norm"] if i < 4 else VEC["sb_norm"])
                dve.wait_ge(sig["m_norm"], i + 1)
                if i >= 2:
                    dve.wait_ge(sig["a_lo_ready"], 16 + i - 1)
                out = v.scalar_tensor_tensor(m_, flat(y[:, i]), vec[:, c:c + 1], flat(rstd[:, i % 2]), ALU.mult, ALU.mult)
                if i < 4:
                    out.then_inc(sig["m_mid"], 1)
                    dve.wait_ge(sig["m_mid"], i + 1)
                    dve.wait_ge(sig["gg_ready"], 1)
                    out = v.tensor_tensor(m_, m_, flat(proj[:, GG + i]), ALU.mult)
                out.then_inc(sig["m_ready"], 1)
                dve.wait_ge(sig["a_hi_ready"], 16 + i + 1)
                v.tensor_tensor(a_lo[:, i, :], m_, a_hi[:, i, :].bitcast(F32), ALU.subtract).then_inc(sig["a_lo_ready"], 1)
            for n in range(4):
                split(Step(n), "out")
            for k in range(2):
                t = T0["p"] + k
                dve.wait_ge(sig["p_hi_ready"], k + 1)
                v.tensor_tensor(p_lo[:, k, 0:SEQ], PS[:, 4 * (t % 2), :], p_hi[:, k, 0:SEQ].bitcast(F32), ALU.subtract)
                v.tensor_tensor(p_lo[:, k, SEQ:T], PS[:, 4 * (t % 2) + 1, 0:N_SAMPLE], p_hi[:, k, SEQ:T].bitcast(F32),
                                ALU.subtract).then_inc(psum_free[t % 2], 1)
            split(Step(0), "f2_up0")
            boundary(1, 3, "mix_post", "f2_pre", 3)
            ffn("f2", 4)
            split(Step(0), "embed")
            t = embed_ticket(0)
            full(dve, t)
            v.tensor_copy(e[:, 0:2].rearrange("p k a t -> p (k a) t"), banks(t % 2, 0, 4)).then_inc(psum_free[t % 2], 1)
            boundary(2, 5, "f2_post", "ple_pre", 4)
            for n in range(4):
                t, quad, use = ticket(Step(n), "gate")
                if n < 3:
                    split(Step(n), "gate")
                dve.wait_ge(sig["rstd_ready"], 7)
                full(dve, t)
                dve.wait_ge(sig["x_ready"], 8 * 3)
                dve.wait_ge(sig["pg_out"], 2 * n)
                for c in range(2):
                    ins = v.tensor_tensor(work[:, c, :].rearrange("p (a t) -> p a t", a=2), banks(quad, 2 * c, 2),
                                          rstd[:, 0], ALU.mult).then_inc(psum_free[quad] if c else sig["pg_ready"], 1)
                for c in range(2):
                    k = 2 * n + c
                    dve.wait_ge(sig["pg_sig"], k + 1)
                    v.tensor_tensor(flat(y[:, k]), work[:, c, :], flat(e[:, k]), ALU.mult).then_inc(sig["pg_out"], 1)
            boundary(3, 7, "ple_post")

        @block.gpsimd
        def _(pool):
            g = nc.gpsimd
            made = [0]

            def then(ins):
                ins.then_inc(sig["pool_step"], 1)
                made[0] += 1
                pool.wait_ge(sig["pool_step"], made[0])

            then(g.memset(ident[:], 0.0))
            then(g.affine_select(out=ident[:], in_=ident[:], compare_op=ALU.not_equal, fill=1.0, base=0,
                                 pattern=[[-1, P]], channel_multiplier=1))
            then(g.memset(ones[:], 1.0))
            then(g.memset(eps[:], EPS))
            pool.sem_inc(sig["masks_made"], 1)
            then(g.memset(ones64[:], 1.0))
            then(g.memset(ones64[0:64, 64:P], 0.0))
            then(g.memset(ones64[64:P, 0:64], 0.0))
            then(g.affine_select(out=tri[:], in_=ones[:], compare_op=ALU.is_ge, fill=0.0, base=0,
                                 pattern=[[-1, P]], channel_multiplier=1))
            then(g.memset(neg_diag[:], 0.0))
            then(g.affine_select(out=neg_diag[:], in_=neg_diag[:], compare_op=ALU.is_gt, fill=MASKED, base=0,
                                 pattern=[[1, P]], channel_multiplier=-1))

            def add_square(j, k):
                n = 8 * j + k
                pool.wait_ge(sig["sq_ready"], n + 1)
                if k == 0:
                    if j:
                        full(pool, sum_ticket[j - 1])
                    g.tensor_copy(sum_sq[:], sq[:, 0, :]).then_inc(sig["sq_used"], 1)
                else:
                    pool.wait_ge(sig["sq_used"], n)
                    g.tensor_tensor(sum_sq[:], sum_sq[:], sq[:, k % 2, :], ALU.add).then_inc(sig["sq_used"], 1)

            for k in range(KD):
                add_square(0, k)
            then(g.memset(level_mask[:], 0.0))
            for l in range(LEVELS):
                half, n = 1 << l, P >> (l + 1)
                m_ = level_mask[:, l, :].rearrange("p (n a t) -> p n a t", a=2, t=half)[:, :, 1, :]
                then(g.memset(m_, 1.0))
                then(g.affine_select(out=m_, in_=m_, compare_op=ALU.is_ge, fill=0.0, base=0,
                                     pattern=[[-2 * half, n], [0, half]], channel_multiplier=1))
                then(g.affine_select(out=m_, in_=m_, compare_op=ALU.is_ge, fill=0.0, base=half - 1,
                                     pattern=[[2 * half, n], [0, half]], channel_multiplier=-1))
            then(g.memset(batch_mask[:], 1.0))
            then(g.affine_select(out=batch_mask[:], in_=batch_mask[:], compare_op=ALU.is_ge, fill=0.0, base=0,
                                 pattern=[[-DEC_SEQ, DEC_BATCH]], channel_multiplier=1))
            then(g.affine_select(out=batch_mask[:], in_=batch_mask[:], compare_op=ALU.is_ge, fill=0.0,
                                 base=DEC_SEQ - 1, pattern=[[DEC_SEQ, DEC_BATCH]], channel_multiplier=-1))
            nn = neg_new[:].rearrange("p b t -> p (b t)")
            then(g.tensor_tensor(nn, level_mask[0:N_SAMPLE, 0, 0:N_SAMPLE], level_mask[0:N_SAMPLE, 1, 0:N_SAMPLE], ALU.add))
            then(g.tensor_scalar(nn, nn, -MASKED, MASKED, ALU.mult, ALU.add))
            then(g.memset(scan_keep[:], 1.0))
            then(g.memset(scan_keep[:, 0:N_SAMPLE:DEC_SEQ], 0.0))
            pool.sem_inc(sig["masks_made"], 1)

            for k in range(KD):
                add_square(1, k)
            for k in range(KD):
                add_square(2, k)
            for n, dst, src, done in ((0, o[2][0, 0].rearrange("(c p) h d -> p c (h d)", p=P), k_nat[:], "k_stored"),
                                      (1, o[3][0, 0].rearrange("(c p) h d -> p c (h d)", p=P), v_nat[:], "v_stored"),
                                      (3, o[5][0].rearrange("b t h d -> (b t) (h d)"), new_nat[:, 0, :], "nat_stored"),
                                      (3, o[6][0].rearrange("b t h d -> (b t) (h d)"), new_nat[:, 1, :], "nat_stored")):
                t = T0["natural"] + n
                pool.wait_ge(psum_free[t % 2], t // 2 + 1)
                pool.dma_start(dst, src).then_inc(sig[done], 16)

            def query(h):
                r = slice(64 * (h % 2), 64 * (h % 2) + 64)
                if h >= 2:
                    pool.wait_ge(sig["z_full"], h - 1)
                g.tensor_copy(q_pad[h % 2][r, 0:SEQ], flat(proj[:, SQ + h // 2])[r, 0:SEQ]).then_inc(sig["q_pad_ready"], 1)
                pool.wait_ge(sig["q_pad_ready"], h + 1)

            for h in range(2):
                then(g.memset(q_pad[h], 0.0))
                query(h)
            then(g.memset(q_block, 0.0))
            for hh in range(2):
                r = slice(64 * hh, 64 * hh + 64)
                q_ = proj[r, SQ:SQ + 4].rearrange("p k a t -> p k (a t)")[:, :, SEQ:T].rearrange(
                    "p k (b t) -> p k b t", t=DEC_SEQ)
                then(g.tensor_copy(q_block[r].rearrange("p k b (h t) -> p k b h t", h=2)[:, :, :, hh], q_))
                then(g.tensor_copy(neg_cols.rearrange("p k b (h t) -> p k b h t", h=2)[:, :, :, hh],
                                   neg_new[:].unsqueeze(1).broadcast_to([N_SAMPLE, 4, DEC_BATCH, DEC_SEQ])))
            for p in range(4):
                then(g.tensor_copy(bias_cols[:, p].rearrange("p b (h t) -> p b h t", h=2),
                                   bias[:, 2 * p:2 * p + 2].unsqueeze(1).unsqueeze(3).broadcast_to(
                                       [P, DEC_BATCH, 2, DEC_SEQ])))
            pool.sem_inc(sig["setup_new"], 1)
            for h in range(2, SB_HEADS):
                query(h)

            old = a["state_gla"][0].rearrange("b (p h) d v -> p (h d) b v", p=2)
            new_out = o[7][0].rearrange("b (p h) d v -> p (h d) b v", p=2)
            state_out = o[4][0, 0].rearrange("(p h) d v -> p (h d) v", p=2)
            pool.wait_ge(sig["c_full"], SB_HEADS)
            pool.wait_ge(sig["d_ready"], SB_HEADS)
            pool.dma_start(state_old, old[0]).then_inc(sig["state_in"], 16)
            for p in range(2):
                for li in range(1, LEVELS + 1):
                    n_tok, n_att = (T if li <= 2 else SEQ), (LEVELS + 1) * p
                    pool.wait_ge(sig["lev_exp"], LEVELS * p + li)
                    if n_att + li >= 3:
                        pool.wait_ge(sig["lev_full"], n_att + li - 1)
                    g.tensor_tensor(k_lev[li % 2][:, 0:n_tok], flat(proj[:, GK + p])[:, 0:n_tok],
                                    decay[li % 2][:, 0:n_tok], ALU.mult).then_inc(sig["lev_k"], 1)
                pool.wait_ge(sig["last_ready"], p + 1)
                pool.wait_ge(sig["state_in"], 16 * (p + 1))
                if p:
                    pool.wait_ge(sig["new_stored"], 16)
                g.tensor_tensor(state_new, state_old,
                                decay_last[:, N_CH:].unsqueeze(2).broadcast_to([P, DEC_BATCH, P]),
                                ALU.mult).then_inc(sig["sn_decayed"], 1)
                pool.wait_ge(sig["state_ready"], N_CH * (p + 1))
                pool.dma_start(state_out[p], state[:, N_CH - 1, :]).then_inc(sig["state_stored"], 16)
                pool.wait_ge(sig["sn_out"], p + 1)
                pool.dma_start(new_out[p], state_new).then_inc(sig["new_stored"], 16)
                if p == 0:
                    pool.wait_ge(sig["inter_full"], 1)
                    pool.dma_start(state_old, old[1]).then_inc(sig["state_in"], 16)

            pool.wait_ge(sig["m_ready"], KD)
            for n in range(5):
                rows_n = P if n < 4 else N_SAMPLE
                src = a["p_prompt"][0, 0, n * P:(n + 1) * P, :] if n < 4 else a["p_sample"][0].rearrange("b t d -> (b t) d")
                pool.dma_start(rows[0:rows_n, n, 0:PLE_DIM], src).then_inc(sig["p_in"], 16)
            for j in range(3, len(NORMS)):
                for k in range(KD):
                    add_square(j, k)


_INS = ["x_prompt", "x_sample", "cache_sb_k", "cache_sb_v", "state_gla", "page_table", "p_prompt", "p_sample",
        "f1_pre", "f1_in", "f1_out", "f1_post", "mix_pre", "w_in", "gate_w", "gate_b", "gla_norm", "sb_norm",
        "sb_bias", "w_out", "mix_post", "f2_pre", "f2_in", "f2_out", "f2_post", "ple_pre", "ple_w_gate",
        "ple_w_up", "ple_post"]
_OUTS = [(1, SEQ, D_MODEL), (DEC_BATCH, DEC_SEQ, D_MODEL), (1, 1, SEQ, SB_HEADS, SB_DH),
         (1, 1, SEQ, SB_HEADS, SB_DH), (1, 1, GLA_HEADS, GLA_DK, GLA_DV),
         (1, DEC_BATCH, DEC_SEQ, SB_HEADS, SB_DH), (1, DEC_BATCH, DEC_SEQ, SB_HEADS, SB_DH),
         (1, DEC_BATCH, GLA_HEADS, GLA_DK, GLA_DV)]


def kernel(**inputs):
    import numpy as np
    import concourse.bacc as bacc
    from concourse.bass_utils import run_bass_kernel_spmd

    nc = bacc.Bacc("TRN2", target_bir_lowering=False, num_devices=1)
    arrays, ins = {}, {}
    for name in _INS:
        v = np.ascontiguousarray(inputs[name])
        arrays[f"in_{name}"] = v
        ins[name] = nc.dram_tensor(f"in_{name}", v.shape, mybir.dt.from_np(v.dtype), kind="ExternalInput").ap()
    outs = [nc.dram_tensor(f"out_{i}", s, F32, kind="ExternalOutput").ap() for i, s in enumerate(_OUTS)]
    build(nc, ins, outs)
    r = run_bass_kernel_spmd(nc, [arrays], core_ids=[0])
    return tuple(r.results[0][f"out_{i}"] for i in range(len(_OUTS)))
```

```python
from contextlib import ExitStack

import concourse.bass as bass
from concourse import mybir

F32 = mybir.dt.float32
F32R = mybir.dt.float32r
I32 = mybir.dt.int32
U32 = mybir.dt.uint32
ALU = mybir.AluOpType
ACT = mybir.ActivationFunctionType

P = 128
D_MODEL = 1024
SEQ = 512
DEC_BATCH = 8
DEC_SEQ = 4
N_SAMPLE = DEC_BATCH * DEC_SEQ
T = SEQ + N_SAMPLE
HALF = T // 2
KD = D_MODEL // P
D_FF = 2816
N_PAGES = 2
PLE_DIM = 256
GLA_HEADS, GLA_DK, GLA_DV, GLA_RANK = 4, 64, 128, 16
SB_HEADS, SB_DH = 8, 64
EPS = 1e-6
MASKED = -1e30
F_TILES = D_FF // P
GROUPS = (12, 10)
G_MAX = max(GROUPS)
SLOT = 8 * 256
LEVELS = 7
CH = 128
N_CH = SEQ // CH

VEC = {"f1_pre": 0, "f1_post": 8, "mix_pre": 16, "mix_post": 24, "f2_pre": 32, "f2_post": 40,
       "ple_pre": 48, "ple_post": 56, "gate_b": 64, "gla_norm": 66, "sb_norm": 67}
N_VEC = 68

GQ, GK, GG, SQ, SK, SV, GV = 0, 2, 4, 8, 12, 16, 20
W_IN_STEPS = [(0, GQ), (256, GK), (1024, GG), (1280, GG + 2),
              (1552, SQ), (1808, SQ + 2), (2064, SK), (2320, SK + 2), (2576, SV), (2832, SV + 2),
              (512, GV), (768, GV + 2)]
GLR_COL = 1536


class Step:

    def __init__(self, c, i=0):
        self.c, self.i = c, i
        self.n = c + 2 * i

    def parity(self, base):
        return (base + self.c) % 2

    def half(self, base):
        return (base + self.c) // 2 + self.i


def steps(eng, first, end, body):
    pairs = (end - first) // 2
    if pairs > 1:
        with eng.Fori(0, pairs) as i:
            body(Step(first, i))
            body(Step(first + 1, i))
    elif pairs:
        body(Step(first))
        body(Step(first + 1))
    if (end - first) % 2:
        body(Step(end - 1))


def plan():
    at, w, t = {}, 0, 0
    parts = [("vectors", 0, 1), ("x", 0, KD)]
    for name in ("f1", "f2"):
        parts += [(f"{name}_up0", GROUPS[0], GROUPS[0] + 1), (f"{name}_down0", KD, KD),
                  (f"{name}_up1", GROUPS[1], GROUPS[1]), (f"{name}_down1", KD, KD)]
        parts += [(f"{name}_post", 0, 1)] if name == "f1" else [("embed_first", 0, 1), (f"{name}_post", 0, 1)]
        if name == "f1":
            parts += [("in", 13, 14), ("natural", 0, 4), ("merge", 0, KD), ("out", 4, 4), ("p", 0, 2), ("out_post", 0, 1)]
    parts += [("embed", 1, 3), ("gate", 4, 5), ("gate_post", 0, 1), ("y", 0, KD)]
    for name, n_w, n_t in parts:
        at[name] = (w, t)
        w, t = w + n_w, t + n_t
    at["end"] = (w, t)
    return at


def flat(ap):
    return ap.rearrange("p a t -> p (a t)")


def build(nc, a, o):
    at = plan()
    widths = []
    for name in ("f1", "f2"):
        for g in GROUPS:
            widths += [SLOT] * g + [g * P] * KD
        if name == "f1":
            widths += [SLOT] * 12 + [KD * GLA_RANK] + [SLOT] * 4
    widths += [SLOT] * 5
    n_w = at["end"][0]
    assert len(widths) == n_w

    ctx = ExitStack()
    with ctx:
        def sb(name, shape, dt=F32, where=ctx):
            return where.enter_context(nc.sbuf_tensor(name, shape, dt))

        def sem(name):
            return ctx.enter_context(nc.semaphore(name))

        PS = ctx.enter_context(nc.psum_tensor("PS", [P, 8, 512], F32))

        x = sb("x", [P, KD, 2, HALF])
        y = sb("y", [P, KD, 2, HALF])
        raw = sb("raw", [P, 2, SLOT])
        with nc.sbuf_tensor("w_hi", [P, 2, SLOT], F32R) as w_hi, nc.sbuf_tensor("w_lo", [P, 2, SLOT], F32R) as w_lo:
            pass
        hold_w = sb("hold_w", [P, 2, 2, SLOT])
        ident = sb("ident", [P, P])
        ones = sb("ones", [P, P])
        tri = sb("tri", [P, P])
        ones64 = sb("ones64", [P, P])
        neg_diag = sb("neg_diag", [P, P])
        level_mask = sb("level_mask", [P, LEVELS, P])
        batch_mask = sb("batch_mask", [P, DEC_BATCH])
        neg_new = sb("neg_new", [N_SAMPLE, DEC_BATCH, DEC_SEQ])
        scan_keep = sb("scan_keep", [P, N_SAMPLE])
        eps = sb("eps", [P, 1])
        vec_rows = sb("vec_rows", [N_VEC, P])
        vec = sb("vec", [P, N_VEC])
        bias_row = sb("bias_row", [1, SB_HEADS])
        bias = sb("bias", [P, SB_HEADS])
        gate_w = sb("gate_w", [GLA_RANK, 2 * P])
        table = sb("table", [1, DEC_BATCH * N_PAGES], I32)
        sum_sq = sb("sum_sq", [P, T])
        sq = sb("sq", [P, 2, T])
        rstd = sb("rstd", [P, 2, 2, HALF])
        work = sb("work", [P, 2, T])
        glr = sb("glr", [GLA_RANK, 2, HALF])
        with nc.sbuf_tensor("p_hi", [P, 2, T], F32R) as p_hi, nc.sbuf_tensor("p_lo", [P, 2, T], F32R) as p_lo:
            pass
        extra = sb("extra", [P, 3 * 1280])
        with nc.sbuf_tensor("a_hi", [P, KD, T], F32R) as a_hi, nc.sbuf_tensor("a_lo", [P, KD, T], F32R) as a_lo:
            pass
        with ExitStack() as s:
            k_nat = sb("k_nat", [P, N_CH, 512], F32, s)
            v_nat = sb("v_nat", [P, N_CH, 512], F32, s)
            gv_nat = sb("gv_nat", [P, N_CH, 512], F32, s)
            new_nat = sb("new_nat", [N_SAMPLE, 3, 512], F32, s)
            state_0 = sb("state_0", [P, N_CH, P], F32, s)
            kl_new = sb("kl_new", [N_SAMPLE, P], F32, s)
            decay_last = sb("decay_last", [P, 2, N_CH + DEC_BATCH], F32, s)
        hold_a = sb("hold_a", [P, 2 * KD * T])
        with nc.sbuf_tensor("h_hi", [P, G_MAX, T], F32R) as h_hi, nc.sbuf_tensor("h_lo", [P, G_MAX, T], F32R) as h_lo:
            pass
        with nc.sbuf_tensor("proj", [P, 24, 2, HALF], F32) as proj:
            pass
        with nc.sbuf_tensor("rows", [P, 5, D_MODEL], F32) as rows, nc.sbuf_tensor("e", [P, KD, 2, HALF], F32) as e:
            pass
        hold_h = sb("hold_h", [P, 2 * G_MAX * T])

        def scratch(owner, at_, shape):
            n = 1
            for s_ in shape[1:]:
                n *= s_
            v = owner[0:shape[0], at_:at_ + n]
            if len(shape) == 3:
                return v.rearrange("p (a b) -> p a b", a=shape[1])
            if len(shape) == 4:
                return v.rearrange("p (a b c) -> p a b c", a=shape[1], b=shape[2])
            return v

        work_flat = work[:].rearrange("p a t -> p (a t)")
        gs = scratch(work_flat, 0, [P, 2, HALF])
        us = scratch(work_flat, T, [P, 2, HALF])
        dead = proj[:, SV:SV + 8].rearrange("p k a t -> p (k a t)")
        extra_flat = extra[:]

        sb_z = [scratch(dead, 1280 * n, [P, 1280]) for n in range(2)]
        sb_s = [scratch(dead, 2560, [P, 1280]), scratch(extra_flat, 0, [P, 1280])]
        sb_w = [scratch(extra_flat, 1280 * n, [P, 1280]) for n in (1, 2)]
        y_flat = y[:].rearrange("p k a t -> p (k a t)")
        sq_flat = sq[:].rearrange("p a t -> p (a t)")
        k_page = scratch(y_flat, 0, [P, 4, 512])
        spare = [hold_w[:, n, (at["out"][0] + 1) % 2, :] for n in range(2)]
        v_page = [k_nat[:, c] for c in range(N_CH)] + [
            w_[:, c * 512:(c + 1) * 512] for w_ in spare for c in range(4)] + [v_nat[:, c] for c in range(N_CH)]
        k_turned = scratch(work_flat, 0, [P, 2, 512])
        q_pad = [rstd[:, n].rearrange("p a t -> p (a t)") for n in range(2)]
        q_block = scratch(sq_flat, 0, [P, 4, DEC_BATCH, 8])
        bias_cols = scratch(sq_flat, 256, [P, 4, DEC_BATCH, 8])
        neg_cols = scratch(sq_flat, 512, [N_SAMPLE, 4, DEC_BATCH, 8])
        z_new = scratch(sq_flat, 768, [N_SAMPLE, 256])
        z_past = scratch(dead, 3840, [P, 512])
        s_past = scratch(extra_flat, 0, [P, 512])
        s_new = scratch(extra_flat, 512, [N_SAMPLE, 256])
        w_past = scratch(y_flat, 0, [P, 512])
        w_new = scratch(y_flat, 512, [N_SAMPLE, 256])
        att = [scratch(spare[0], 1024 * p, [P, 8, P]) for p in range(2)]
        state = [state_0[:], scratch(spare[1], 0, [P, N_CH, P])]
        state_new = [scratch(dead, 1024 * p, [P, DEC_BATCH, P]) for p in range(2)]
        state_old = scratch(dead, 2048, [P, DEC_BATCH, P])
        kl_batch = scratch(dead, 3072, [N_SAMPLE, DEC_BATCH, P])
        q_new = [scratch(dead, n, [P, DEC_BATCH, 2, DEC_SEQ]) for n in (4096, 4288)]
        att_new = scratch(dead, 4160, [N_SAMPLE, 2, N_SAMPLE])
        decay = [scratch(extra_flat, T * n, [P, T]) for n in (0, 1)]
        k_lev = [scratch(extra_flat, T * n, [P, T]) for n in (2, 3)]
        kl_nat = scratch(extra_flat, 5 * T, [P, N_CH, P])
        q_lev = [scratch(n_[:].rearrange("p c n -> p (c n)"), 0, [P, 2, T]) for n_ in (v_nat, k_nat)]
        cum = scratch(work_flat, 0, [P, 2, T])
        la_raw, la_soft = rstd[:, 0].rearrange("p a t -> p (a t)"), sum_sq[:]
        q_dec, kl = [sq[:, 0, :], scratch(extra_flat, T * 4, [P, T])], sq[:, 1, :]
        GLA_LEVELS = [(p, li) for p in range(2) for li in range(LEVELS + 1)]

        def number(p, li):
            return LEVELS * p + li

        def before(m):
            return m + 1 + (m > LEVELS)

        names = """vec_in x_in table_in page_in0 page_in1 page_in2 page_in3 vpage_in0 vpage_in1 vpage_in2 vpage_in3 vpage_in4 vpage_in5 vpage_in6 vpage_in7 vpage_in8 vpage_in9 vpage_in10 vpage_in11 vpage_in12 vpage_in13 vpage_in14 vpage_in15
            state_in p_in raw_in0 raw_in1 out_done ident_made ones_made masks_made pool_step
            split_hi split_lo psum_full psum_free0 psum_free1 vec_ready bias_ready
            a_hi_ready a_lo_ready sq_ready sq_used sum_ready rstd_ready log_ready
            upd_ready x_ready g_ready silu_ready h_raw h_hi_ready h_lo_ready
            p_hi_ready p_lo_ready glr_ready
            z_full z_out z_masked abs_ready e_ready soft_log sp_ready c_full d_ready w_ready o_full o_out
            setup_new kt_full kt_out zs_full zs_out n_out
            la_full la_sum la_abs la_log la_soft_ready cum_ready
            eb_ready qe_ready kl_diff kl_exp kl_ready klt_full klt_out klb_ready last_ready
            lev_diff lev_exp lev_q lev_k lev_full att_out u_full state_ready
            og_full og_out on_full on_out sn_full sn_decayed sn_out
            q_zero diag_half qz_ready q_pad_ready k_stored v_stored nat_stored state_stored new_stored m_mid pg_ready pg_sig pg_out gg_ready m_sq m_norm m_ready rows_out""".split()
        sig = {n: sem(n) for n in names}
        raw_in = [sig["raw_in0"], sig["raw_in1"]]
        psum_free = [sig["psum_free0"], sig["psum_free1"]]
        page_in = [sig[f"page_in{n}"] for n in range(4)]
        vpage_in = [sig[f"vpage_in{n}"] for n in range(16)]

        W0 = {n: v[0] for n, v in at.items()}
        T0 = {n: v[1] for n, v in at.items()}
        NORMS = ["f1_pre", "f1_post", "mix_pre", "mix_post", "f2_pre", "f2_post", "ple_pre", "ple_post"]
        sum_ticket = [T0["f1_up0"] + 1, T0["f1_post"], T0["in"] + 1, T0["out_post"], T0["f2_up0"] + 1,
                      T0["f2_post"], T0["gate"] + 1, T0["gate_post"]]

        def banks(quad, first, n):
            return PS[:, 4 * quad + first:4 * quad + first + n, 0:HALF]

        def full(eng, t, quad_free=None):
            eng.wait_ge(sig["psum_full"], t + 1)

        def ticket(st, name):
            base = T0[name]
            if name in ("f1_up0", "f2_up0", "in", "gate") and st.c >= 1:
                base += 1
            return base + st.n, st.parity(base), st.half(base)

        def embed_ticket(s_):
            return T0["embed"] + s_ - 1 if s_ else T0["embed_first"]

        SPLIT_EARLY = ("f1_up0", "in", "f2_up0")

        block = ctx.enter_context(nc.Block())

        @block.sync
        def _(sp):
            def load(w, slot, parts, wait=True):
                if wait:
                    sp.wait_ge(sig["split_lo"], w - 1)
                for dst, src in parts:
                    sp.dma_start(dst, src).then_inc(raw_in[slot], 16)

            def up(name, g0):
                src = a[f"{name}_in"][0].rearrange("(k p) n -> p k n", p=P)

                def parts(st, slot):
                    dst = raw[:, slot, :].rearrange("p (k c n) -> p k c n", k=KD, c=2)
                    return [(dst[:, :, c, :], src[:, :, bass.ds(c * D_FF + (g0 + st.n) * P, P)]) for c in range(2)]
                return parts

            def down(name, g0, g):
                src = a[f"{name}_out"][0].rearrange("(f p) n -> p f n", p=P)

                def parts(st, slot):
                    dst = raw[:, slot, 0:g * P].rearrange("p (k n) -> p k n", k=g)
                    return [(dst[:, c * g // 2:(c + 1) * g // 2, :],
                             src[:, g0 + c * g // 2:g0 + (c + 1) * g // 2, bass.ds(st.n * P, P)]) for c in range(2)]
                return parts

            def wide(src, col, n=256):
                def parts(st, slot):
                    dst = raw[:, slot, 0:KD * n].rearrange("p (k n) -> p k n", k=KD)
                    v = src.rearrange("(k p) n -> p k n", p=P)
                    return [(dst[:, 4 * c:4 * c + 4, :], v[:, 4 * c:4 * c + 4, bass.ds(col(st), n)]) for c in range(2)]
                return parts

            def stage(name, n, parts, first=0):
                w0 = W0[name]
                steps(sp, first, n, lambda st: load(w0 + st.n, st.parity(w0), parts(st, st.parity(w0))))

            def pages():
                sp.wait_ge(sig["table_in"], 16)
                page_no = [sp.value_load(table[0:1, j:j + 1], min_val=0, max_val=a["cache_sb_k"].shape[1] - 1)
                           for j in range(DEC_BATCH * N_PAGES)]

                def page(dst, cache, j, landed):
                    sp.dma_start(dst, cache[0, bass.ds(page_no[j], 1)].rearrange("a s h d -> s (a h d)")).then_inc(landed, 16)

                sp.wait_ge(sig["upd_ready"], KD)
                for j in range(DEC_BATCH * N_PAGES):
                    if j >= 4:
                        sp.wait_ge(sig["kt_full"], j - 3)
                    page(k_page[:, j % 4, :], a["cache_sb_k"], j, page_in[j % 4])
                for j in range(DEC_BATCH * N_PAGES):
                    if j == 0:
                        sp.wait_ge(sig["k_stored"], 16)
                    elif j == 4:
                        full(sp, T0["natural"] - 1)
                    elif j == 12:
                        sp.wait_ge(sig["v_stored"], 16)
                        sp.wait_ge(sig["o_full"], SB_HEADS)
                    page(v_page[j], a["cache_sb_v"], j, vpage_in[j])

            sp.dma_start(table[:], a["page_table"].rearrange("b n -> (b n)").unsqueeze(0)).then_inc(sig["table_in"], 16)
            for n in range(5):
                rows_n = P if n < 4 else N_SAMPLE
                src = a["x_prompt"][0, n * P:(n + 1) * P, :] if n < 4 else a["x_sample"].rearrange("b t d -> (b t) d")
                sp.dma_start(rows[0:rows_n, n, :], src).then_inc(sig["x_in"], 16)

            first = up("f1", 0)
            for n in range(2):
                load(n, n, first(Step(n), n), wait=False)
            stage("f1_up0", GROUPS[0], first, first=2)
            for name in ("f1", "f2"):
                if name == "f2":
                    stage("f2_up0", GROUPS[0], up(name, 0))
                stage(f"{name}_down0", KD, down(name, 0, GROUPS[0]))
                stage(f"{name}_up1", GROUPS[1], up(name, GROUPS[0]))
                stage(f"{name}_down1", KD, down(name, GROUPS[0], GROUPS[1]))
                if name == "f1":
                    for s_, (col, _t) in enumerate(W_IN_STEPS):
                        w = W0["in"] + s_
                        load(w, w % 2, wide(a["w_in"][0], lambda st: col)(None, w % 2))
                    w = W0["in"] + 12
                    load(w, w % 2, wide(a["w_in"][0], lambda st: GLR_COL, GLA_RANK)(None, w % 2))
                    out_parts = wide(a["w_out"][0], lambda st: st.n * 256)
                    for n in range(2):
                        w = W0["out"] + n
                        load(w, w % 2, out_parts(Step(n), w % 2))
                    pages()
                    stage("out", 4, out_parts, first=2)
            w = W0["embed"]
            up_w = a["ple_w_up"][0].rearrange("(k p) n -> p k n", p=P)
            load(w, w % 2, [(raw[:, w % 2, k * D_MODEL:(k + 1) * D_MODEL], up_w[:, k, :]) for k in range(2)])
            stage("gate", 4, wide(a["ple_w_gate"][0], lambda st: st.n * 256))
            for part in range(2):
                for quad in range(2):
                    sp.wait_ge(psum_free[quad], (T0["y"] + 4 * (part + 1) + 1 - quad) // 2)
                cols = slice(part * 512, (part + 1) * 512)
                sp.dma_start(o[0][0].rearrange("(n p) d -> p n d", p=P)[:, :, cols],
                             rows[:, 0:4, cols]).then_inc(sig["out_done"], 16)
                sp.dma_start(o[1].rearrange("b t d -> (b t) d")[:, cols],
                             rows[0:N_SAMPLE, 4, cols]).then_inc(sig["out_done"], 16)
            sp.wait_ge(sig["out_done"], 16 * 4)
            sp.wait_ge(sig["k_stored"], 16)
            sp.wait_ge(sig["v_stored"], 16)
            sp.wait_ge(sig["nat_stored"], 16 * 2)
            sp.wait_ge(sig["state_stored"], 16 * 2)
            sp.wait_ge(sig["new_stored"], 16 * 2)

        @block.tensor
        def _(pe):
            mm = nc.tensor.matmul

            def open_ticket(t, quad, use):
                pe.wait_ge(psum_free[quad], use)

            def open_t(t):
                open_ticket(t, t % 2, t // 2)

            def weights(w):
                pe.wait_ge(sig["split_lo"], w + 1)

            def dense(quad, slot, tiles, n_k, rhs, ready=None, stride=None, width=P):
                stride = stride or tiles * width
                for k in range(n_k):
                    if ready:
                        ready(k)
                    for c in range(tiles):
                        cols = slice(k * stride + c * width, k * stride + (c + 1) * width)
                        for n, (wt, act) in enumerate(((w_hi, rhs[0]), (w_hi, rhs[1]), (w_lo, rhs[0]))):
                            for half in range(2):
                                last = mm(PS[0:width, 4 * quad + 2 * c + half, 0:HALF], wt[:, slot, cols],
                                          act[:, k, half * HALF:(half + 1) * HALF],
                                          start=(k == 0 and n == 0), stop=(k == n_k - 1 and n == 2))
                return last

            def sum_norm(j):
                t = sum_ticket[j]
                open_t(t)
                pe.wait_ge(sig["sq_used"], 8 * (j + 1))
                for half in range(2):
                    last = mm(PS[:, 4 * (t % 2) + half, 0:HALF], ones[:], sum_sq[:, half * HALF:(half + 1) * HALF],
                              start=True, stop=True)
                last.then_inc(sig["psum_full"], 1)

            def product(name, n, tiles, n_k, rhs, ready=None, norm=None):
                def body(st, ready=None):
                    t, quad, use = ticket(st, name)
                    weights(W0[name] + st.n)
                    open_ticket(t, quad, use)
                    dense(quad, st.parity(W0[name]), tiles, n_k, rhs, ready).then_inc(sig["psum_full"], 1)
                body(Step(0), ready)
                if norm is not None:
                    sum_norm(norm)
                steps(pe, 1, n, body)

            A = (a_hi, a_lo)
            H = (h_hi, h_lo)

            def a_tiles(stage_no):
                return lambda k: pe.wait_ge(sig["a_lo_ready"], 8 * stage_no + k + 1)

            def h_tiles(first):
                return lambda k: pe.wait_ge(sig["h_lo_ready"], first + k + 1)

            def embed(s_):
                t, slot = embed_ticket(s_), W0["embed"] % 2
                weights(W0["embed"])
                open_t(t)
                for k in range(2):
                    for c in range(2):
                        for n, (wt, act) in enumerate(((w_hi, p_hi), (w_hi, p_lo), (w_lo, p_hi))):
                            for half in range(2):
                                col = k * D_MODEL + (2 * s_ + c) * P
                                last = mm(PS[:, 4 * (t % 2) + 2 * c + half, 0:HALF], wt[:, slot, col:col + P],
                                          act[:, k, half * HALF:(half + 1) * HALF],
                                          start=(k == 0 and n == 0), stop=(k == 1 and n == 2))
                last.then_inc(sig["psum_full"], 1)

            def ffn(name, stage_no, first, norm):
                product(f"{name}_up0", GROUPS[0], 2, KD, A, a_tiles(stage_no), norm)
                product(f"{name}_down0", KD, 1, GROUPS[0], H, h_tiles(first))
                product(f"{name}_up1", GROUPS[1], 2, KD, A)
                product(f"{name}_down1", KD, 1, GROUPS[1], H, h_tiles(first + GROUPS[0]))
                if name == "f2":
                    embed(0)
                sum_norm(norm + 1)

            pe.wait_ge(sig["masks_made"], 1)
            pe.wait_ge(sig["vec_in"], 16 * 14)
            nc.tensor.transpose(PS[:, 0, 0:N_VEC], vec_rows[:], ident[0:N_VEC, 0:N_VEC])
            mm(PS[:, 1, 0:SB_HEADS], ones[0:1, :], bias_row[:], start=True, stop=True).then_inc(sig["psum_full"], 1)
            pe.wait_ge(sig["x_in"], 16 * 5)
            for k in range(KD):
                t = T0["x"] + k
                open_t(t)
                for n in range(4):
                    nc.tensor.transpose(PS[:, 4 * (t % 2), n * P:(n + 1) * P], rows[:, n, k * P:(k + 1) * P], ident[:])
                nc.tensor.transpose(PS[:, 4 * (t % 2) + 1, 0:N_SAMPLE], rows[0:N_SAMPLE, 4, k * P:(k + 1) * P],
                                    ident[0:N_SAMPLE, 0:N_SAMPLE]).then_inc(sig["psum_full"], 1)
            ffn("f1", 0, 0, 0)

            product("in", 12, 2, KD, A, a_tiles(1), 2)
            st = Step(12)
            t, quad, use = ticket(st, "in")
            weights(W0["in"] + 12)
            open_ticket(t, quad, use)
            dense(quad, st.parity(W0["in"]), 1, KD, A, width=GLA_RANK).then_inc(sig["psum_full"], 1)

            for n, tile in enumerate((SK, SV, GV)):
                t = T0["natural"] + n
                open_t(t)
                for c in range(N_CH):
                    for f in range(4):
                        last = nc.tensor.transpose(PS[:, 4 * (t % 2) + c, f * P:(f + 1) * P],
                                                   flat(proj[:, tile + f])[:, c * P:(c + 1) * P], ident[:])
                last.then_inc(sig["psum_full"], 1)
            t = T0["natural"] + 3
            open_t(t)
            for n, tile in enumerate((SK, SV, GV)):
                for f in range(4):
                    last = nc.tensor.transpose(PS[0:N_SAMPLE, 4 * (t % 2) + n, f * P:(f + 1) * P],
                                               flat(proj[:, tile + f])[:, SEQ:T], ident[:])
            last.then_inc(sig["psum_full"], 1)

            for quad in range(2):
                pe.wait_ge(psum_free[quad], (T0["merge"] + 1 - quad) // 2)

            def prompt_z(h):
                p = h // 2
                k_, q_ = flat(proj[:, SK + p]), q_pad[h % 2]
                pe.wait_ge(sig["z_out"], h)
                pe.wait_ge(sig["q_pad_ready"], h + 1)
                for j in range(4):
                    mm(PS[:, 0, j * P:(j + 1) * P], k_[:, j * P:(j + 1) * P], q_[:, j * P:(j + 1) * P],
                       start=True, stop=True)
                mm(PS[:, 1, 0:384], k_[:, 0:P], q_[:, P:SEQ], start=True, stop=True)
                mm(PS[:, 2, 0:256], k_[:, P:2 * P], q_[:, 2 * P:SEQ], start=True, stop=True)
                mm(PS[:, 2, 256:384], k_[:, 2 * P:3 * P], q_[:, 3 * P:SEQ], start=True,
                   stop=True).then_inc(sig["z_full"], 1)

            def turn_page(j):
                pe.wait_ge(page_in[j % 4], 16 * (j // 4 + 1))
                pe.wait_ge(sig["kt_out"], j)
                for f in range(4):
                    last = nc.tensor.transpose(PS[:, 7, f * P:(f + 1) * P], k_page[:, j % 4, f * P:(f + 1) * P], ident[:])
                last.then_inc(sig["kt_full"], 1)

            def page_z(b):
                pe.wait_ge(sig["kt_out"], N_PAGES * (b + 1))
                pe.wait_ge(sig["z_out"], b + 2)
                for pg in range(N_PAGES):
                    for p in range(4):
                        col = 384 + pg * 32 + p * 8
                        last = mm(PS[:, 2, col:col + 8], k_turned[:, pg, p * P:(p + 1) * P], q_block[:, p, b, :],
                                  start=True, stop=True)
                return last

            def prompt_sums(h):
                s_ = sb_s[h % 2]
                pe.wait_ge(sig["sp_ready"], h + 1)
                pe.wait_ge(sig["d_ready"], h)
                mm(PS[:, 4, :], tri[:], s_[:, 0:512], start=True, stop=True)
                mm(PS[:, 5, 0:384], tri[:], s_[:, 512:896], start=True, stop=False)
                mm(PS[:, 5, 0:384], ones[:], s_[:, 128:512], start=False, stop=False)
                mm(PS[:, 5, 128:384], ones[:], s_[:, 896:1152], start=False, stop=False)
                mm(PS[:, 5, 256:384], ones[:], s_[:, 1152:1280], start=False, stop=True)
                mm(PS[:, 6, 0:384], tri[:], s_[:, 896:1280], start=True, stop=False)
                mm(PS[:, 6, 0:256], ones[:], s_[:, 256:512], start=False, stop=False)
                mm(PS[:, 6, 128:256], ones[:], s_[:, 1152:1280], start=False, stop=False)
                mm(PS[:, 6, 256:384], ones[:], s_[:, 384:512], start=False, stop=True).then_inc(sig["c_full"], 1)

            def prompt_out(h):
                r, bank, w_ = slice(64 * (h % 2), 64 * (h % 2) + 64), 3, sb_w[h % 2]
                pe.wait_ge(sig["w_ready"], h + 1)
                pe.wait_ge(sig["o_out"], h)
                out, off = PS[r, bank], [512, 896, 1152]
                for j in range(4):
                    v_ = v_nat[:, j, h * SB_DH:(h + 1) * SB_DH]
                    last = mm(out[:, j * P:(j + 1) * P], v_, w_[:, j * P:(j + 1) * P], start=(j == 0), stop=(j in (0, 3)))
                    if j < 3:
                        n = (3 - j) * P
                        mm(out[:, (j + 1) * P:SEQ], v_, w_[:, off[j]:off[j] + n], start=(j == 0), stop=False)
                last.then_inc(sig["o_full"], 1)

            prompt_z(0)
            for h in range(SB_HEADS):
                if h == 0:
                    prompt_z(1)
                    pe.wait_ge(sig["setup_new"], 1)
                elif h + 1 < SB_HEADS:
                    page_z(h - 1)
                    prompt_z(h + 1)
                else:
                    page_z(h - 1).then_inc(sig["z_full"], 1)
                turn_page(2 * h)
                prompt_sums(h)
                turn_page(2 * h + 1)
                if h >= 1:
                    prompt_out(h - 1)
            page_z(SB_HEADS - 1).then_inc(sig["z_full"], 1)
            prompt_out(SB_HEADS - 1)

            n_pages = DEC_BATCH * N_PAGES
            pe.wait_ge(sig["kt_out"], n_pages)
            for p in range(4):
                last = mm(PS[0:N_SAMPLE, 7, p * 64:(p + 1) * 64], flat(proj[:, SK + p])[:, SEQ:T],
                          q_block[:, p].rearrange("p b n -> p (b n)"), start=True, stop=True)
            last.then_inc(sig["zs_full"], 1)

            def gate_logits(p):
                for half in range(2):
                    last = mm(PS[:, 6 + half, 0:HALF], gate_w[:, p * P:(p + 1) * P], glr[:, half], start=True, stop=True)
                last.then_inc(sig["la_full"], 1)

            pe.wait_ge(sig["d_ready"], SB_HEADS)
            pe.wait_ge(sig["zs_out"], 2)
            gate_logits(0)
            pe.wait_ge(sig["sp_ready"], SB_HEADS + 2)
            new = slice(0, N_SAMPLE)
            mm(PS[:, 0, :], tri[:], s_past, start=True, stop=False)
            mm(PS[:, 0, 0:256], ones[:], s_past[:, 256:512], start=False, stop=False)
            mm(PS[:, 0, 0:256], ones[new, :], s_new, start=False, stop=False)
            mm(PS[:, 0, 256:512], ones[new, :], s_new, start=False, stop=True)
            mm(PS[new, 1, 0:256], tri[new, new], s_new, start=True, stop=True).then_inc(sig["c_full"], 1)
            pe.wait_ge(sig["la_sum"], 1)
            gate_logits(1)
            pe.wait_ge(sig["w_ready"], SB_HEADS + 2)
            pe.wait_ge(sig["o_out"], SB_HEADS)
            for p in range(4):
                mm(PS[:, 2 + p, 0:64], new_nat[:, 1, p * P:(p + 1) * P], w_new[:, p * 64:(p + 1) * 64],
                   start=True, stop=False)
            for j in range(n_pages):
                b, pg = j // N_PAGES, j % N_PAGES
                pe.wait_ge(vpage_in[j], 16)
                for p in range(4):
                    col = p * 64 + b * 8
                    last = mm(PS[:, 2 + p, b * 8:b * 8 + 8], v_page[j][:, p * P:(p + 1) * P],
                              w_past[:, pg * 256 + col:pg * 256 + col + 8], start=False, stop=(j == n_pages - 1))
                last.then_inc(sig["n_out"], 1)

            def keys_turned(p):
                pe.wait_ge(sig["kl_ready"], p + 1)
                if p:
                    pe.wait_ge(sig["og_out"], 2 * p)
                for c in range(N_CH):
                    nc.tensor.transpose(PS[:, 6, c * P:(c + 1) * P], kl[:, c * P:(c + 1) * P], ident[:])
                nc.tensor.transpose(PS[0:N_SAMPLE, 7, 0:P], kl[:, SEQ:T], ident[:]).then_inc(sig["klt_full"], 1)

            def level(g):
                p, li = GLA_LEVELS[g]
                b0 = 2 * (g % 2)
                if li in (1, 2):
                    pe.wait_ge(sig["att_out"], g)
                elif g >= 2:
                    pe.wait_ge(sig["att_out"], g - 1)
                if p and li == 0:
                    pe.wait_ge(sig["on_out"], p + 1)
                if li == 0:
                    q_, k_ = flat(proj[:, GQ + p]), flat(proj[:, GK + p])
                    rows_ = [slice(64 * hh, 64 * hh + 64) for hh in range(2)]
                    new_ = [PS[0:N_SAMPLE, 4, hh * N_SAMPLE:(hh + 1) * N_SAMPLE] for hh in range(2)]
                    mm(new_[0], k_[rows_[0], SEQ:T], q_[rows_[0], SEQ:T], start=True,
                       stop=True).then_inc(sig["diag_half"], 1)
                    for hh, r in enumerate(rows_):
                        for c in range(N_CH):
                            tok = slice(c * P, (c + 1) * P)
                            mm(PS[:, b0 + hh, tok], k_[r, tok], q_[r, tok], start=True, stop=True)
                    pe.wait_ge(sig["diag_half"], p + 1)
                    last = mm(new_[1], k_[rows_[1], SEQ:T], q_[rows_[1], SEQ:T], start=True, stop=True)
                else:
                    m = number(p, li)
                    q_, k_ = q_lev[m % 2], k_lev[m % 2]
                    pe.wait_ge(sig["lev_q"], m)
                    pe.wait_ge(sig["lev_k"], m)
                    for c in range(N_CH):
                        tok, col = slice(c * P, (c + 1) * P), (c % 2) * 256
                        last = mm(PS[:, b0 + c // 2, col:col + 256].rearrange("p (h t) -> p h t", h=2), k_[:, tok],
                                  q_[:, :, tok], start=True, stop=True)
                    if li <= 2:
                        last = mm(PS[0:N_SAMPLE, 4, 0:2 * N_SAMPLE].rearrange("p (h t) -> p h t", h=2), k_[:, SEQ:T],
                                  q_[:, :, SEQ:T], start=True, stop=True)
                last.then_inc(sig["lev_full"], 1)

            def chunk_states(p):
                pe.wait_ge(sig["klt_out"], p + 1)
                if p:
                    pe.wait_ge(sig["og_out"], 2 * p)
                for hh in range(2):
                    h = 2 * p + hh
                    for c in range(N_CH):
                        last = mm(PS[64 * hh:64 * hh + 64, 5, c * P:(c + 1) * P],
                                  kl_nat[:, c, 64 * hh:64 * hh + 64], gv_nat[:, c, h * P:(h + 1) * P],
                                  start=True, stop=True)
                last.then_inc(sig["u_full"], 1)

            def sample_states(p, part):
                pe.wait_ge(sig["klb_ready"], p + 1)
                if part:
                    pe.wait_ge(sig["sn_out"], 2 * p + part)
                else:
                    pe.wait_ge(sig["klt_out"], p + 1)
                for n in range(4):
                    last = mm(PS[:, 6 + n // 2, (n % 2) * 256:(n % 2) * 256 + 256], kl_batch[:, 4 * part + n, :],
                              new_nat[:, 2, p * 256:(p + 1) * 256], start=True, stop=True)
                last.then_inc(sig["sn_full"], 1)

            def sample_outs(p):
                pe.wait_ge(sig["state_in"], 16 * (p + 1))
                pe.wait_ge(sig["qe_ready"], 2 * (p + 1))
                pe.wait_ge(sig["att_out"], (LEVELS + 1) * p + 3)
                out = PS[:, 4, 0:64].rearrange("p (b h t) -> p b h t", h=2, t=DEC_SEQ)
                for b in range(DEC_BATCH):
                    mm(PS[:, 4, b * 8:b * 8 + 8], state_old[:, b, :], q_new[p][:, b].rearrange("p h t -> p (h t)"),
                       start=(b == 0), stop=False)
                for hh in range(2):
                    h = 2 * p + hh
                    last = mm(out[:, :, hh, :], new_nat[:, 2, h * P:(h + 1) * P],
                              att_new[:, hh, :].rearrange("p (b t) -> p b t", t=DEC_SEQ), start=False, stop=(hh == 1))
                last.then_inc(sig["on_full"], 1)

            def outputs(p):
                pe.wait_ge(sig["att_out"], (LEVELS + 1) * (p + 1))
                pe.wait_ge(sig["state_ready"], N_CH * (p + 1))
                pe.wait_ge(sig["sn_out"], 2 * (p + 1))
                for hh in range(2):
                    h, r = 2 * p + hh, slice(64 * hh, 64 * hh + 64)
                    for c in range(N_CH):
                        tok = slice(c * P, (c + 1) * P)
                        last = mm(PS[:, 5 + hh, tok], gv_nat[:, c, h * P:(h + 1) * P], att[p][:, 2 * c + hh, :],
                                  start=True, stop=(c == 0))
                        if c:
                            last = mm(PS[:, 5 + hh, tok], state[p][r, c - 1, :], q_dec[p][r, tok], start=False, stop=True)
                    last.then_inc(sig["og_full"], 1)

            pe.wait_ge(sig["on_out"], 1)
            pe.wait_ge(sig["la_sum"], 2)
            for g in range(len(GLA_LEVELS)):
                p, li = GLA_LEVELS[g]
                level(g)
                if li == 0:
                    if p:
                        outputs(p - 1)
                    keys_turned(p)
                elif li == 2:
                    chunk_states(p)
                elif li == 3:
                    sample_states(p, 0)
                elif li == 4:
                    sample_outs(p)
                elif li == 5:
                    sample_states(p, 1)
            outputs(1)

            pe.wait_ge(sig["sn_out"], 4)
            pe.wait_ge(sig["og_out"], 4)
            pe.wait_ge(sig["on_out"], 3)
            for i in range(KD):
                t = T0["merge"] + i
                open_t(t)
                pe.wait_ge(sig["m_sq"], i + 1)
                for half in range(2):
                    last = mm(PS[:, 4 * (t % 2) + half, 0:HALF], (ones if i < 4 else ones64)[:],
                              sq[:, i % 2, half * HALF:(half + 1) * HALF], start=True, stop=True)
                last.then_inc(sig["psum_full"], 1)
            product("out", 4, 2, KD, A, a_tiles(2))
            pe.wait_ge(sig["p_in"], 16 * 5)
            for k in range(2):
                t = T0["p"] + k
                open_t(t)
                for n in range(4):
                    nc.tensor.transpose(PS[:, 4 * (t % 2), n * P:(n + 1) * P], rows[:, n, k * P:(k + 1) * P], ident[:])
                nc.tensor.transpose(PS[:, 4 * (t % 2) + 1, 0:N_SAMPLE], rows[0:N_SAMPLE, 4, k * P:(k + 1) * P],
                                    ident[0:N_SAMPLE, 0:N_SAMPLE]).then_inc(sig["psum_full"], 1)
            sum_norm(3)
            ffn("f2", 3, F_TILES, 4)
            for s_ in range(1, 4):
                embed(s_)
            product("gate", 4, 2, KD, A, a_tiles(4), 6)
            sum_norm(7)
            for k in range(KD):
                t = T0["y"] + k
                open_t(t)
                pe.wait_ge(sig["x_ready"], 8 * 3 + k + 1)
                for n in range(4):
                    nc.tensor.transpose(PS[:, 4 * (t % 2), n * P:(n + 1) * P], flat(x[:, k])[:, n * P:(n + 1) * P],
                                        ident[:])
                nc.tensor.transpose(PS[0:N_SAMPLE, 4 * (t % 2) + 1, 0:P], flat(x[:, k])[:, SEQ:T],
                                    ident[:]).then_inc(sig["psum_full"], 1)

        up_base = {"f1_up0": 0, "f1_up1": GROUPS[0], "f2_up0": F_TILES, "f2_up1": F_TILES + GROUPS[0]}
        h_slot = lambda name: 0

        @block.scalar
        def _(act):
            fn = nc.scalar.activation

            def split(st, name, t):
                nxt, w0 = Step(st.c + 1, st.i), W0[name]
                slot, width = nxt.parity(w0), widths[w0 + st.c + 1]
                act.wait_ge(raw_in[slot], 32 * (nxt.half(w0) + 1))
                if t is not None:
                    act.wait_ge(sig["psum_full"], t)
                fn(w_hi[:, slot, 0:width], raw[:, slot, 0:width], ACT.Copy).then_inc(sig["split_hi"], 1)

            def norm(j):
                t, r = sum_ticket[j], rstd[:, j % 2]
                full(act, t)
                fn(r, banks(t % 2, 0, 2), ACT.Ln, bias=eps[:], scale=1.0 / D_MODEL).then_inc(psum_free[t % 2], 1)
                act.wait_ge(psum_free[t % 2], t // 2 + 1)
                fn(r, r, ACT.Exp, scale=-0.5).then_inc(sig["rstd_ready"], 1)

            def square(j, k, src):
                n = 8 * j + k
                if n >= 2:
                    act.wait_ge(sig["sq_used"], n - 1)
                fn(sq[:, k % 2, :], src, ACT.Square).then_inc(sig["sq_ready"], 1)

            def input_tile(k, name, j):
                c = VEC[name] + k
                fn(a_hi[:, k, :], flat(x[:, k]), ACT.Copy, scale=vec[:, c:c + 1]).then_inc(sig["a_hi_ready"], 1)
                square(j, k, flat(x[:, k]))

            def boundary(b, name, j, behind=None):
                for k in range(KD):
                    act.wait_ge(sig["x_ready"], 8 * b + k + 1)
                    input_tile(k, name, j)
                    if behind and k in (1, 3, 5):
                        behind(k // 2 + 1)

            def stage(name, n, body, after_first=None, table=None):
                def one(st):
                    t, quad, use = ticket(st, name)
                    if W0[name] + st.c + 1 < n_w and (st.c or name not in SPLIT_EARLY):
                        split(st, name, t)
                    if st.c == 0 and after_first is not None:
                        norm(after_first)
                        nc.scalar.preload_act_table(table)
                    body(st, t, quad, use)
                one(Step(0))
                steps(act, 1, n - 1, one)
                one(Step(n - 1))

            def up(name):
                base = up_base[name]
                h0 = base % F_TILES

                def body(st, t, quad, use):
                    n = base + st.n
                    act.wait_ge(sig["g_ready"], n + 1)
                    fn(gs, gs, ACT.Silu).then_inc(sig["silu_ready"], 1)
                    act.wait_ge(sig["h_raw"], n + 1)
                    fn(h_hi[:, bass.ds(st.n, 1), :].rearrange("p a t -> p (a t)"), flat(us),
                       ACT.Copy).then_inc(sig["h_hi_ready"], 1)
                return body

            def down0(st, t, quad, use):
                full(act, t)
                fn(y[:, bass.ds(st.n, 1)].rearrange("p k a t -> p (k a) t"), banks(quad, 0, 2),
                   ACT.Copy).then_inc(psum_free[quad], 1)

            def down1(j):
                def body(st, t, quad, use):
                    act.wait_ge(psum_free[quad], use + 1)
                    n = 8 * j + st.n
                    act.wait_ge(sig["sq_used"], n - 1)
                    fn(sq[:, st.parity(0), :], y[:, bass.ds(st.n, 1)].rearrange("p k a t -> p (k a t)"),
                       ACT.Square).then_inc(sig["sq_ready"], 1)
                return body

            def ffn(name, j):
                stage(f"{name}_up0", GROUPS[0], up(f"{name}_up0"), after_first=j, table=ACT.Silu)
                stage(f"{name}_down0", KD, down0)
                stage(f"{name}_up1", GROUPS[1], up(f"{name}_up1"))
                nc.scalar.preload_act_table_set("natural_log_exp_and_others")
                stage(f"{name}_down1", KD, down1(j + 1))
                if name == "f1":
                    split(Step(0), "in", T0["f1_post"])
                else:
                    split(Step(0), "embed", T0["embed_first"])
                norm(j + 1)

            nc.scalar.preload_act_table_set("natural_log_exp_and_others")
            for name in NORMS:
                act.dma_start(vec_rows[VEC[name]:VEC[name] + 8, :],
                              a[name][0].rearrange("(k p) -> k p", p=P)).then_inc(sig["vec_in"], 16)
            act.dma_start(vec_rows[64:66, :], a["gate_b"][0].rearrange("(k p) -> k p", p=P)).then_inc(sig["vec_in"], 16)
            act.dma_start(vec_rows[66:67, :], a["gla_norm"]).then_inc(sig["vec_in"], 16)
            for n in range(2):
                act.dma_start(vec_rows[67:68, n * 64:(n + 1) * 64], a["sb_norm"]).then_inc(sig["vec_in"], 16)
            act.dma_start(bias_row[:], a["sb_bias"]).then_inc(sig["vec_in"], 16)
            act.dma_start(gate_w[:], a["gate_w"][0]).then_inc(sig["vec_in"], 16)

            act.wait_ge(raw_in[0], 32)
            fn(w_hi[:, 0, :], raw[:, 0, :], ACT.Copy).then_inc(sig["split_hi"], 1)
            split(Step(0), "f1_up0", None)
            act.wait_ge(sig["vec_ready"], 3)
            for k in range(KD):
                t = T0["x"] + k
                act.wait_ge(psum_free[t % 2], t // 2 + 1)
                input_tile(k, "f1_pre", 0)
            ffn("f1", 0)
            boundary(0, "mix_pre", 2)

            def in_body(st, t, quad, use):
                if st.c == 12:
                    act.wait_ge(psum_free[1 - quad], (t + 1) // 2)
                    fn(proj[:, GG:GG + 4], proj[:, GG:GG + 4], ACT.Silu).then_inc(sig["gg_ready"], 1)
                    nc.scalar.preload_act_table_set("natural_log_exp_and_others")

            stage("in", 13, in_body, after_first=2, table=ACT.Silu)

            for n, dst in ((0, k_nat), (2, gv_nat)):
                t = T0["natural"] + n
                full(act, t)
                fn(dst[:], PS[:, 4 * (t % 2):4 * (t % 2) + 4, :], ACT.Copy).then_inc(psum_free[t % 2], 1)

            act.wait_ge(sig["psum_full"], T0["merge"])

            def turned(j):
                act.wait_ge(sig["kt_full"], j + 1)
                fn(k_turned[:, j % 2, :], PS[:, 7, :], ACT.Copy).then_inc(sig["kt_out"], 1)

            def page_logits(b):
                return fn(z_past.rearrange("p (q b n) -> p q b n", q=8, b=DEC_BATCH)[:, :, b, :],
                          PS[:, 2, 384:448].rearrange("p (q n) -> p q n", q=8), ACT.Copy)

            def logits(h):
                z_ = sb_z[h % 2]
                act.wait_ge(sig["z_full"], h + 1)
                if h >= 2:
                    page_logits(h - 2)
                if h >= 2:
                    act.wait_ge(sig["d_ready"], h - 1)
                fn(z_[:, 0:512], PS[:, 0, :], ACT.Identity, bias=bias[:, h:h + 1], scale=SB_DH ** -0.5)
                fn(z_[:, 512:1280].rearrange("p (a n) -> p a n", a=2), PS[:, 1:3, 0:384], ACT.Identity,
                   bias=bias[:, h:h + 1], scale=SB_DH ** -0.5).then_inc(sig["z_out"], 1)

            def log_part(n, s_):
                act.wait_ge(sig["abs_ready"], n + 1)
                fn(s_, s_, ACT.Exp, scale=-1.0).then_inc(sig["e_ready"], 1)
                act.wait_ge(sig["e_ready"], n + 1)
                fn(s_, s_, ACT.Ln, bias=1.0).then_inc(sig["soft_log"], 1)

            def weight(n, w_):
                act.wait_ge(sig["d_ready"], n + 1)
                fn(w_, w_, ACT.Exp).then_inc(sig["w_ready"], 1)

            logits(0)
            log_part(0, sb_s[0])
            for h in range(SB_HEADS):
                if h + 1 < SB_HEADS:
                    logits(h + 1)
                else:
                    act.wait_ge(sig["z_full"], h + 2)
                    page_logits(h - 1).then_inc(sig["z_out"], 1)
                turned(2 * h)
                if h + 1 < SB_HEADS:
                    log_part(h + 1, sb_s[(h + 1) % 2])
                turned(2 * h + 1)
                weight(h, sb_w[h % 2])

            act.wait_ge(sig["z_full"], SB_HEADS + 2)
            page_logits(SB_HEADS - 1).then_inc(sig["z_out"], 1)
            log_part(SB_HEADS, s_past)
            log_part(SB_HEADS + 1, s_new)
            weight(SB_HEADS, w_past)
            weight(SB_HEADS + 1, w_new)

            for p in range(2):
                act.wait_ge(sig["la_abs"], p + 1)
                fn(la_soft, la_soft, ACT.Exp, scale=-1.0).then_inc(sig["la_log"], 1)
                act.wait_ge(sig["la_log"], 2 * p + 1)
                fn(la_soft, la_soft, ACT.Ln, bias=1.0).then_inc(sig["la_log"], 1)
            def pair_decays(p):
                act.wait_ge(sig["cum_ready"], 2)
                fn(q_dec[p], cum[:, p, :], ACT.Exp, scale=1.0 / 16).then_inc(sig["eb_ready"], 1)
                fn(decay_last[:, p, 0:N_CH], cum[:, p, CH - 1:SEQ:CH], ACT.Exp, scale=1.0 / 16)
                fn(decay_last[:, p, N_CH:], cum[:, p, SEQ + DEC_SEQ - 1:T:DEC_SEQ], ACT.Exp,
                   scale=1.0 / 16).then_inc(sig["last_ready"], 1)
                act.wait_ge(sig["kl_diff"], p + 1)
                fn(kl, kl, ACT.Exp, scale=1.0 / 16).then_inc(sig["kl_exp"], 1)

            def outputs(p):
                for hh in range(2):
                    h = 2 * p + hh
                    act.wait_ge(sig["og_full"], h + 1)
                    fn(flat(y[:, h])[:, 0:SEQ], PS[:, 5 + hh, :], ACT.Copy).then_inc(sig["og_out"], 1)

            pair_decays(0)
            for p, li in GLA_LEVELS:
                if li:
                    m, n_tok = number(p, li), T if li <= 2 else SEQ
                    act.wait_ge(sig["lev_diff"], m)
                    d_ = decay[m % 2][:, 0:n_tok]
                    fn(d_, d_, ACT.Exp, scale=1.0 / 16).then_inc(sig["lev_exp"], 1)
                if p and li == 1:
                    outputs(p - 1)
                if li == 2:
                    act.wait_ge(sig["klt_full"], p + 1)
                    if p:
                        act.wait_ge(sig["u_full"], p)
                        act.wait_ge(sig["klb_ready"], p)
                    fn(kl_nat, PS[:, 6, :].rearrange("p (c n) -> p c n", c=N_CH), ACT.Copy)
                    fn(kl_new[:], PS[0:N_SAMPLE, 7, 0:P], ACT.Copy).then_inc(sig["klt_out"], 1)
                if p == 0 and li == 6:
                    pair_decays(1)
            outputs(1)

            act.wait_ge(sig["nat_stored"], 16 * 2)
            act.wait_ge(sig["state_stored"], 16 * 2)
            act.wait_ge(sig["sn_out"], 4)

            def head_square(i):
                if i >= 2:
                    full(act, T0["merge"] + i - 2)
                elif i == 1:
                    act.wait_ge(sig["klt_full"], 2)
                act.wait_ge(sig["og_out"], 4)
                act.wait_ge(sig["on_out"], 3)
                fn(sq[:, i % 2, :], flat(y[:, i]), ACT.Square).then_inc(sig["m_sq"], 1)

            head_square(0)
            for i in range(KD):
                if i + 1 < KD:
                    head_square(i + 1)
                t, r = T0["merge"] + i, rstd[:, i % 2]
                full(act, t)
                if i >= 2:
                    act.wait_ge(sig["m_ready"], i - 1)
                fn(r, banks(t % 2, 0, 2), ACT.Ln, bias=eps[:],
                   scale=1.0 / (GLA_DV if i < 4 else SB_DH)).then_inc(psum_free[t % 2], 1)
                act.wait_ge(psum_free[t % 2], t // 2 + 1)
                fn(r, r, ACT.Exp, scale=-0.5).then_inc(sig["m_norm"], 1)
                act.wait_ge(sig["m_ready"], i + 1)
                fn(a_hi[:, i, :], decay[i % 2], ACT.Copy).then_inc(sig["a_hi_ready"], 1)

            def out_body(st, t, quad, use):
                full(act, t)
                fn(y[:, 2 * st.c:2 * st.c + 2].rearrange("p k a t -> p (k a) t"), banks(quad, 0, 4),
                   ACT.Copy).then_inc(psum_free[quad], 1)
                act.wait_ge(psum_free[quad], use + 1)
                for c in range(2):
                    square(3, 2 * st.c + c, flat(y[:, 2 * st.c + c]))

            for n in range(4):
                t, quad, use = ticket(Step(n), "out")
                split(Step(n), "out", t)
                out_body(Step(n), t, quad, use)
            act.wait_ge(sig["a_lo_ready"], 24)
            for k in range(2):
                t = T0["p"] + k
                full(act, t)
                fn(p_hi[:, k, 0:SEQ], PS[:, 4 * (t % 2), :], ACT.Copy)
                fn(p_hi[:, k, SEQ:T], PS[:, 4 * (t % 2) + 1, 0:N_SAMPLE], ACT.Copy).then_inc(sig["p_hi_ready"], 1)
            split(Step(0), "f2_up0", T0["p"])
            norm(3)
            boundary(1, "f2_pre", 4)
            ffn("f2", 4)

            def e_tiles(n):
                t = embed_ticket(n)
                full(act, t)
                fn(e[:, 2 * n:2 * n + 2].rearrange("p k a t -> p (k a) t"), banks(t % 2, 0, 4),
                   ACT.Copy).then_inc(psum_free[t % 2], 1)

            boundary(2, "ple_pre", 6, e_tiles)
            for n in range(4):
                t, quad, use = ticket(Step(n), "gate")
                if n < 3:
                    split(Step(n), "gate", t)
                if n == 0:
                    norm(6)
                    nc.scalar.preload_act_table(ACT.Sigmoid)
                for c in range(2):
                    k = 2 * n + c
                    act.wait_ge(*((psum_free[quad], use + 1) if c else (sig["pg_ready"], n + 1)))
                    fn(work[:, c, :], work[:, c, :], ACT.Sigmoid).then_inc(sig["pg_sig"], 1)
                for c in range(2):
                    k = 2 * n + c
                    act.wait_ge(sig["pg_out"], k + 1)
                    square(7, k, flat(y[:, k]))
            nc.scalar.preload_act_table_set("natural_log_exp_and_others")
            norm(7)
            for k in range(KD):
                t = T0["y"] + k
                full(act, t)
                cols = slice(k * P, (k + 1) * P)
                fn(rows[:, 0:4, cols], PS[:, 4 * (t % 2), :].rearrange("p (n c) -> p n c", n=4), ACT.Copy)
                fn(rows[0:N_SAMPLE, 4, cols], PS[0:N_SAMPLE, 4 * (t % 2) + 1, 0:P], ACT.Copy).then_inc(psum_free[t % 2], 1)

        @block.vector
        def _(dve):
            v = nc.vector

            def split(st, name):
                nxt, w0 = Step(st.c + 1, st.i), W0[name]
                slot, width = nxt.parity(w0), widths[w0 + st.c + 1]
                dve.wait_ge(sig["split_hi"], w0 + nxt.n + 1)
                v.tensor_tensor(w_lo[:, slot, 0:width], raw[:, slot, 0:width],
                                w_hi[:, slot, 0:width].bitcast(F32), ALU.subtract).then_inc(sig["split_lo"], 1)

            def input_tile(k, name, stage_no):
                c = VEC[name] + k
                dve.wait_ge(sig["a_hi_ready"], 8 * stage_no + k + 1)
                v.scalar_tensor_tensor(a_lo[:, k, :], flat(x[:, k]), vec[:, c:c + 1], a_hi[:, k, :].bitcast(F32),
                                       ALU.mult, ALU.subtract).then_inc(sig["a_lo_ready"], 1)

            def boundary(b, j, post, pre=None, stage_no=None):
                dve.wait_ge(sig["rstd_ready"], j + 1)

                def update(k):
                    n, c = 8 * b + k, VEC[post] + k
                    v.scalar_tensor_tensor(work[:, k % 2, :], flat(y[:, k]), vec[:, c:c + 1], flat(rstd[:, j % 2]),
                                           ALU.mult, ALU.mult).then_inc(sig["upd_ready"], 1)

                update(0)
                for k in range(KD):
                    n = 8 * b + k
                    if k:
                        dve.wait_ge(sig["x_ready"], n)
                    if k + 1 < KD:
                        update(k + 1)
                    dve.wait_ge(sig["upd_ready"], n + 1)
                    v.tensor_tensor(flat(x[:, k]), work[:, k % 2, :], flat(x[:, k]), ALU.add).then_inc(sig["x_ready"], 1)
                    if pre and k:
                        input_tile(k - 1, pre, stage_no)
                if pre:
                    input_tile(KD - 1, pre, stage_no)

            def stage(name, n, body, after_first=None):
                def one(st):
                    t, quad, use = ticket(st, name)
                    if st.c or name not in SPLIT_EARLY:
                        split(st, name)
                    if st.c == 0 and after_first is not None:
                        dve.wait_ge(sig["rstd_ready"], after_first + 1)
                    body(st, t, quad, use)
                one(Step(0))
                steps(dve, 1, n - 1, one)
                one(Step(n - 1))

            def up(name, j):
                base = up_base[name]

                def body(st, t, quad, use):
                    n, r = base + st.n, rstd[:, j % 2]
                    full(dve, t)
                    dve.wait_ge(sig["h_lo_ready"], n)
                    v.tensor_tensor(gs, banks(quad, 0, 2), r, ALU.mult).then_inc(sig["g_ready"], 1)
                    v.tensor_tensor(us, banks(quad, 2, 2), r, ALU.mult).then_inc(psum_free[quad], 1)
                    dve.wait_ge(psum_free[quad], use + 1)
                    dve.wait_ge(sig["silu_ready"], n + 1)
                    v.tensor_tensor(us, us, gs, ALU.mult).then_inc(sig["h_raw"], 1)
                    dve.wait_ge(sig["h_hi_ready"], n + 1)
                    hs = bass.ds(st.n, 1)
                    v.tensor_tensor(h_lo[:, hs, :].rearrange("p a t -> p (a t)"), flat(us),
                                    h_hi[:, hs, :].bitcast(F32).rearrange("p a t -> p (a t)"),
                                    ALU.subtract).then_inc(sig["h_lo_ready"], 1)
                return body

            def down1(st, t, quad, use):
                full(dve, t)
                yt = y[:, bass.ds(st.n, 1)].rearrange("p k a t -> p (k a) t")
                v.tensor_tensor(yt, banks(quad, 0, 2), yt, ALU.add).then_inc(psum_free[quad], 1)

            def ffn(name, j):
                stage(f"{name}_up0", GROUPS[0], up(f"{name}_up0", j), after_first=j)
                stage(f"{name}_down0", KD, lambda st, t, quad, use: None)
                stage(f"{name}_up1", GROUPS[1], up(f"{name}_up1", j))
                stage(f"{name}_down1", KD, down1)

            full(dve, 0)
            v.tensor_copy(vec[:], PS[:, 0, 0:N_VEC]).then_inc(sig["vec_ready"], 1)
            v.tensor_copy(bias[:], PS[:, 1, 0:SB_HEADS]).then_inc(psum_free[0], 1)
            dve.wait_ge(sig["vec_ready"], 1)
            for name in ("f1_post", "f2_post"):
                c = VEC[name]
                v.tensor_scalar(vec[:, c:c + 8], vec[:, c:c + 8], 0.5, None, ALU.mult).then_inc(sig["vec_ready"], 1)
            for k in range(KD + 1):
                if k < KD:
                    t = T0["x"] + k
                    full(dve, t)
                    v.tensor_copy(flat(x[:, k])[:, SEQ:T], PS[:, 4 * (t % 2) + 1, 0:N_SAMPLE])
                    v.tensor_copy(flat(x[:, k])[:, 0:SEQ], PS[:, 4 * (t % 2), :]).then_inc(psum_free[t % 2], 1)
                if k == 2:
                    dve.wait_ge(sig["split_hi"], 1)
                    v.tensor_tensor(w_lo[:, 0, :], raw[:, 0, :], w_hi[:, 0, :].bitcast(F32),
                                    ALU.subtract).then_inc(sig["split_lo"], 1)
                if k == 5:
                    split(Step(0), "f1_up0")
                if k >= 1:
                    input_tile(k - 1, "f1_pre", 0)
            ffn("f1", 0)
            split(Step(0), "in")
            boundary(0, 1, "f1_post", "mix_pre", 1)

            def project(st, t, quad, use):
                full(dve, t)
                if st.c == 12:
                    v.tensor_tensor(glr[:], PS[0:GLA_RANK, 4 * quad:4 * quad + 2, 0:HALF], rstd[0:GLA_RANK, 0],
                                    ALU.mult).then_inc(psum_free[quad], 1)
                elif st.c == 0:
                    for c in range(2):
                        ins = v.scalar_tensor_tensor(proj[:, GQ + c], banks(quad, 2 * c, 2), GLA_DK ** -0.5,
                                                     rstd[:, 0], ALU.mult, ALU.mult)
                    ins.then_inc(psum_free[quad], 1)
                else:
                    v.tensor_tensor(proj[:, bass.ds(2 * st.n, 2)],
                                    banks(quad, 0, 4).rearrange("p (c a) t -> p c a t", c=2),
                                    rstd[:, 0:1].broadcast_to([P, 2, 2, HALF]), ALU.mult).then_inc(psum_free[quad], 1)

            stage("in", 13, project, after_first=2)
            for n, dst, src in ((1, v_nat[:], lambda q: PS[:, 4 * q:4 * q + 4, :]),
                                (3, new_nat[:], lambda q: PS[0:N_SAMPLE, 4 * q:4 * q + 3, :])):
                t = T0["natural"] + n
                full(dve, t)
                v.tensor_copy(dst, src(t % 2)).then_inc(psum_free[t % 2], 1)

            def magnitudes(h):
                z_ = sb_z[h % 2]
                dve.wait_ge(sig["z_out"], h + 1)
                diag = z_[:, 0:512].rearrange("p (j q) -> p j q", j=4)
                v.tensor_tensor(diag, diag, neg_diag[:].unsqueeze(1).broadcast_to([P, 4, P]),
                                ALU.add).then_inc(sig["z_masked"], 1)
                dve.wait_ge(sig["z_masked"], h + 1)
                if h >= 2:
                    dve.wait_ge(sig["c_full"], h - 1)
                v.scalar_tensor_tensor(sb_s[h % 2], z_, -1.0, z_, ALU.mult, ALU.max).then_inc(sig["abs_ready"], 1)

            def softplus(n, z_, s_):
                dve.wait_ge(sig["soft_log"], n + 1)
                v.scalar_tensor_tensor(s_, z_, 0.0, s_, ALU.max, ALU.add).then_inc(sig["sp_ready"], 1)

            def exponents(h):
                z_, w_ = sb_z[h % 2], sb_w[h % 2]
                dve.wait_ge(sig["c_full"], h + 1)
                if h >= 2:
                    dve.wait_ge(sig["o_full"], h - 1)
                v.tensor_tensor(w_[:, 0:512], z_[:, 0:512], PS[:, 4, :], ALU.subtract)
                v.tensor_tensor(w_[:, 512:1280].rearrange("p (a n) -> p a n", a=2),
                                z_[:, 512:1280].rearrange("p (a n) -> p a n", a=2), PS[:, 5:7, 0:384],
                                ALU.subtract).then_inc(sig["d_ready"], 1)

            def head_out(h):
                r = slice(64 * (h % 2), 64 * (h % 2) + 64)
                dve.wait_ge(sig["o_full"], h + 1)
                v.tensor_copy(flat(y[:, 4 + h // 2])[r, 0:SEQ], PS[r, 3, :]).then_inc(sig["o_out"], 1)

            magnitudes(0)
            softplus(0, sb_z[0], sb_s[0])
            for h in range(SB_HEADS):
                if h + 1 < SB_HEADS:
                    magnitudes(h + 1)
                exponents(h)
                if h + 1 < SB_HEADS:
                    softplus(h + 1, sb_z[(h + 1) % 2], sb_s[(h + 1) % 2])
                if h >= 1:
                    head_out(h - 1)
            head_out(SB_HEADS - 1)

            new = slice(0, N_SAMPLE)
            cols = bias_cols.rearrange("p a b c -> p (a b c)")
            dve.wait_ge(sig["setup_new"], 1)
            dve.wait_ge(sig["zs_full"], 1)
            dve.wait_ge(sig["z_out"], SB_HEADS + 2)
            v.scalar_tensor_tensor(z_past.rearrange("p (a n) -> p a n", a=2),
                                   z_past.rearrange("p (a n) -> p a n", a=2), SB_DH ** -0.5,
                                   cols.unsqueeze(1).broadcast_to([P, 2, 256]), ALU.mult, ALU.add).then_inc(sig["zs_out"], 1)
            v.scalar_tensor_tensor(z_new, PS[new, 7, 0:256], SB_DH ** -0.5, cols[new, :], ALU.mult,
                                   ALU.add).then_inc(sig["zs_out"], 1)
            dve.wait_ge(sig["zs_out"], 2)
            v.tensor_tensor(z_new, z_new, neg_cols.rearrange("p a b c -> p (a b c)"), ALU.add).then_inc(sig["z_masked"], 1)
            v.scalar_tensor_tensor(s_past, z_past, -1.0, z_past, ALU.mult, ALU.max).then_inc(sig["abs_ready"], 1)
            dve.wait_ge(sig["z_masked"], SB_HEADS + 1)
            v.scalar_tensor_tensor(s_new, z_new, -1.0, z_new, ALU.mult, ALU.max).then_inc(sig["abs_ready"], 1)
            softplus(SB_HEADS, z_past, s_past)
            softplus(SB_HEADS + 1, z_new, s_new)
            dve.wait_ge(sig["c_full"], SB_HEADS + 1)
            v.tensor_tensor(w_past, z_past, PS[:, 0, :], ALU.subtract).then_inc(sig["d_ready"], 1)
            v.tensor_tensor(w_new, z_new, PS[new, 1, 0:256], ALU.subtract).then_inc(sig["d_ready"], 1)
            for p in range(2):
                dve.wait_ge(sig["la_full"], p + 1)
                dve.wait_ge(sig["cum_ready"], p)
                v.tensor_scalar(rstd[:, 0], PS[:, 6:8, 0:HALF], vec[:, 64 + p:65 + p], None,
                                ALU.add).then_inc(sig["la_sum"], 1)
                dve.wait_ge(sig["la_sum"], p + 1)
                v.scalar_tensor_tensor(la_soft, la_raw, -1.0, la_raw, ALU.mult, ALU.max).then_inc(sig["la_abs"], 1)
                dve.wait_ge(sig["la_log"], 2 * p + 2)
                v.scalar_tensor_tensor(la_raw, la_raw, 0.0, la_soft, ALU.min, ALU.subtract).then_inc(sig["la_soft_ready"], 1)
                dve.wait_ge(sig["la_soft_ready"], p + 1)
                for c in range(N_CH):
                    tok = slice(c * P, (c + 1) * P)
                    v.tensor_tensor_scan(cum[:, p, tok], ones[:], la_raw[:, tok], 0.0, ALU.mult, ALU.add)
                v.tensor_tensor_scan(cum[:, p, SEQ:T], scan_keep[:], la_raw[:, SEQ:T], 0.0, ALU.mult,
                                     ALU.add).then_inc(sig["cum_ready"], 1)
            dve.wait_ge(sig["n_out"], DEC_BATCH * N_PAGES)
            for hh in range(2):
                r = slice(64 * hh, 64 * hh + 64)
                dst = y[r, 4:8].rearrange("p k a t -> p k (a t)")[:, :, SEQ:T].rearrange("p k (b t) -> p k b t", t=DEC_SEQ)
                src = PS[r, 2:6, 0:64].rearrange("p k (b h t) -> p k h b t", h=2, t=DEC_SEQ)[:, :, hh]
                ins = v.tensor_copy(dst, src)
            ins.then_inc(sig["on_out"], 1)

            gq = [flat(proj[:, GQ + p]) for p in range(2)]
            gk = [flat(proj[:, GK + p]) for p in range(2)]

            def pair_diffs(p):
                chunks = cum[:, p, 0:SEQ].rearrange("p (c t) -> p c t", t=CH)
                batches = cum[:, p, SEQ:T].rearrange("p (c t) -> p c t", t=DEC_SEQ)
                dve.wait_ge(sig["cum_ready"], 2)
                if p:
                    dve.wait_ge(sig["klt_full"], p)
                v.tensor_tensor(kl[:, 0:SEQ].rearrange("p (c t) -> p c t", t=CH),
                                chunks[:, :, CH - 1:CH].broadcast_to([P, N_CH, CH]), chunks, ALU.subtract)
                v.tensor_tensor(kl[:, SEQ:T].rearrange("p (c t) -> p c t", t=DEC_SEQ),
                                batches[:, :, DEC_SEQ - 1:DEC_SEQ].broadcast_to([P, DEC_BATCH, DEC_SEQ]), batches,
                                ALU.subtract).then_inc(sig["kl_diff"], 1)

            def pair_products(p):
                dve.wait_ge(sig["eb_ready"], p + 1)
                v.tensor_tensor(q_dec[p], gq[p], q_dec[p], ALU.mult).then_inc(sig["qe_ready"], 1)
                v.memset(q_new[p], 0.0).then_inc(sig["qz_ready"], 1)
                dve.wait_ge(sig["kl_exp"], p + 1)
                v.tensor_tensor(kl, gk[p], kl, ALU.mult).then_inc(sig["kl_ready"], 1)
                dve.wait_ge(sig["qe_ready"], 2 * p + 1)
                dve.wait_ge(sig["qz_ready"], p + 1)
                for hh in range(2):
                    r = slice(64 * hh, 64 * hh + 64)
                    ins = v.tensor_copy(q_new[p][r, :, hh, :], q_dec[p][r, SEQ:T].rearrange("p (b t) -> p b t", t=DEC_SEQ))
                ins.then_inc(sig["qe_ready"], 1)

            def level_diff(m):
                p, li = (m - 1) // LEVELS, (m - 1) % LEVELS + 1
                half, n_tok = 1 << (li - 1), (T if li <= 2 else SEQ)
                if m >= 3:
                    dve.wait_ge(sig["lev_k"], m - 2)
                    dve.wait_ge(sig["lev_q"], m - 2)
                b_ = cum[:, p, 0:n_tok].rearrange("p (n a t) -> p n a t", a=2, t=half)
                d_ = decay[m % 2][:, 0:n_tok].rearrange("p (n a t) -> p n a t", a=2, t=half)
                ref = b_[:, :, 0, half - 1:half].broadcast_to([P, n_tok // (2 * half), half])
                v.tensor_tensor(d_[:, :, 0, :], ref, b_[:, :, 0, :], ALU.subtract)
                v.tensor_tensor(d_[:, :, 1, :], b_[:, :, 1, :], ref, ALU.subtract).then_inc(sig["lev_diff"], 1)

            def level_q(m):
                p, li = (m - 1) // LEVELS, (m - 1) % LEVELS + 1
                half, n_tok = 1 << (li - 1), (T if li <= 2 else SEQ)
                dve.wait_ge(sig["lev_exp"], m)
                if m >= 3:
                    dve.wait_ge(sig["lev_full"], before(m - 2))
                else:
                    dve.wait_ge(sig["q_zero"], m)
                for hh in range(2):
                    r = slice(64 * hh, 64 * hh + 64)
                    upper = lambda t_: t_[r, 0:n_tok].rearrange("p (n a t) -> p n a t", a=2, t=half)[:, :, 1, :]
                    ins = v.tensor_tensor(upper(q_lev[m % 2][:, hh, :]), upper(gq[p]), upper(decay[m % 2]), ALU.mult)
                ins.then_inc(sig["lev_q"], 1)

            def level_scores(g):
                p, li = GLA_LEVELS[g]
                dve.wait_ge(sig["lev_full"], g + 1)
                src = PS[:, 2 * (g % 2):2 * (g % 2) + 2, :].rearrange("p a (c t) -> p (a c) t", t=P)
                src_new = PS[0:N_SAMPLE, 4, 0:2 * N_SAMPLE].rearrange("p (h t) -> p h t", h=2)
                if li == 0:
                    if p:
                        dve.wait_ge(sig["on_full"], p)
                    v.tensor_tensor(att_new, src_new, ident[0:N_SAMPLE, 0:N_SAMPLE].unsqueeze(1).broadcast_to(
                        [N_SAMPLE, 2, N_SAMPLE]), ALU.mult)
                    v.tensor_tensor(att[p].rearrange("p (c h) t -> p h c t", h=2),
                                    src.rearrange("p (h c) t -> p h c t", h=2),
                                    ident[:].unsqueeze(1).unsqueeze(1).broadcast_to([P, 2, N_CH, P]), ALU.mult).then_inc(sig["att_out"], 1)
                    return
                dve.wait_ge(sig["att_out"], g)
                mask = level_mask[:, li - 1, :].bitcast(U32)
                if li <= 2:
                    v.copy_predicated(att_new, mask[0:N_SAMPLE, 0:N_SAMPLE].unsqueeze(1).broadcast_to(
                        [N_SAMPLE, 2, N_SAMPLE]), src_new)
                v.copy_predicated(att[p], mask.unsqueeze(1).broadcast_to([P, 8, P]), src).then_inc(sig["att_out"], 1)

            def new_keys(p):
                dve.wait_ge(sig["klt_out"], p + 1)
                if p:
                    dve.wait_ge(sig["sn_full"], 2 * p)
                v.tensor_tensor(kl_batch, kl_new[:].unsqueeze(1).broadcast_to([N_SAMPLE, DEC_BATCH, P]),
                                batch_mask[0:N_SAMPLE, :].unsqueeze(2).broadcast_to([N_SAMPLE, DEC_BATCH, P]),
                                ALU.mult).then_inc(sig["klb_ready"], 1)

            def chunk_states(p):
                dve.wait_ge(sig["u_full"], p + 1)
                dve.wait_ge(sig["last_ready"], p + 1)
                v.tensor_copy(state[p][:, 0, :], PS[:, 5, 0:P]).then_inc(sig["state_ready"], 1)
                for c in range(1, N_CH):
                    dve.wait_ge(sig["state_ready"], N_CH * p + c)
                    v.scalar_tensor_tensor(state[p][:, c, :], state[p][:, c - 1, :], decay_last[:, p, c:c + 1],
                                           PS[:, 5, c * P:(c + 1) * P], ALU.mult, ALU.add).then_inc(sig["state_ready"], 1)

            def sample_states(p, part):
                dve.wait_ge(sig["sn_full"], 2 * p + part + 1)
                dve.wait_ge(sig["sn_decayed"], p + 1)
                for hh in range(2):
                    r = slice(64 * hh, 64 * hh + 64)
                    src = PS[r, 6:8, :].rearrange("p a (b h v) -> p a b h v", b=2, h=2)[:, :, :, hh, :]
                    st_ = state_new[p][r, 4 * part:4 * part + 4, :].rearrange("p (a b) v -> p a b v", a=2)
                    ins = v.tensor_tensor(st_, src, st_, ALU.add)
                ins.then_inc(sig["sn_out"], 1)

            def sample_outs(p):
                dve.wait_ge(sig["on_full"], p + 1)
                src = PS[:, 4, 0:64].rearrange("p (b h t) -> p h b t", h=2, t=DEC_SEQ)
                dst = y[:, 2 * p:2 * p + 2].rearrange("p k a t -> p k (a t)")[:, :, SEQ:T].rearrange(
                    "p k (b t) -> p k b t", t=DEC_SEQ)
                v.tensor_copy(dst, src).then_inc(sig["on_out"], 1)

            pair_diffs(0)
            level_diff(1)
            pair_products(0)
            for g in range(len(GLA_LEVELS)):
                p, li = GLA_LEVELS[g]
                if li:
                    m = number(p, li)
                    if m < 2 * LEVELS:
                        level_diff(m + 1)
                    level_q(m)
                if g:
                    level_scores(g - 1)
                if li == 3:
                    new_keys(p)
                elif li == 4:
                    chunk_states(p)
                elif li == 5:
                    sample_states(p, 0)
                    if p == 0:
                        pair_diffs(1)
                elif li == 6:
                    sample_outs(p)
                elif li == 7:
                    sample_states(p, 1)
                    if p == 0:
                        pair_products(1)
            level_scores(len(GLA_LEVELS) - 1)

            for i in range(KD):
                m_, c = decay[i % 2], (VEC["gla_norm"] if i < 4 else VEC["sb_norm"])
                dve.wait_ge(sig["m_norm"], i + 1)
                if i >= 2:
                    dve.wait_ge(sig["a_lo_ready"], 16 + i - 1)
                out = v.scalar_tensor_tensor(m_, flat(y[:, i]), vec[:, c:c + 1], flat(rstd[:, i % 2]), ALU.mult, ALU.mult)
                if i < 4:
                    out.then_inc(sig["m_mid"], 1)
                    dve.wait_ge(sig["m_mid"], i + 1)
                    dve.wait_ge(sig["gg_ready"], 1)
                    out = v.tensor_tensor(m_, m_, flat(proj[:, GG + i]), ALU.mult)
                out.then_inc(sig["m_ready"], 1)
                dve.wait_ge(sig["a_hi_ready"], 16 + i + 1)
                v.tensor_tensor(a_lo[:, i, :], m_, a_hi[:, i, :].bitcast(F32), ALU.subtract).then_inc(sig["a_lo_ready"], 1)
            for n in range(4):
                split(Step(n), "out")
            for k in range(2):
                t = T0["p"] + k
                dve.wait_ge(sig["p_hi_ready"], k + 1)
                v.tensor_tensor(p_lo[:, k, 0:SEQ], PS[:, 4 * (t % 2), :], p_hi[:, k, 0:SEQ].bitcast(F32), ALU.subtract)
                v.tensor_tensor(p_lo[:, k, SEQ:T], PS[:, 4 * (t % 2) + 1, 0:N_SAMPLE], p_hi[:, k, SEQ:T].bitcast(F32),
                                ALU.subtract).then_inc(psum_free[t % 2], 1)
            split(Step(0), "f2_up0")
            boundary(1, 3, "mix_post", "f2_pre", 3)
            ffn("f2", 4)
            split(Step(0), "embed")
            t = embed_ticket(0)
            full(dve, t)
            v.tensor_copy(e[:, 0:2].rearrange("p k a t -> p (k a) t"), banks(t % 2, 0, 4)).then_inc(psum_free[t % 2], 1)
            boundary(2, 5, "f2_post", "ple_pre", 4)
            for n in range(4):
                t, quad, use = ticket(Step(n), "gate")
                if n < 3:
                    split(Step(n), "gate")
                dve.wait_ge(sig["rstd_ready"], 7)
                full(dve, t)
                dve.wait_ge(sig["x_ready"], 8 * 3)
                dve.wait_ge(sig["pg_out"], 2 * n)
                for c in range(2):
                    ins = v.tensor_tensor(work[:, c, :].rearrange("p (a t) -> p a t", a=2), banks(quad, 2 * c, 2),
                                          rstd[:, 0], ALU.mult).then_inc(psum_free[quad] if c else sig["pg_ready"], 1)
                for c in range(2):
                    k = 2 * n + c
                    dve.wait_ge(sig["pg_sig"], k + 1)
                    v.tensor_tensor(flat(y[:, k]), work[:, c, :], flat(e[:, k]), ALU.mult).then_inc(sig["pg_out"], 1)
            boundary(3, 7, "ple_post")

        @block.gpsimd
        def _(pool):
            g = nc.gpsimd
            made = [0]

            def then(ins):
                ins.then_inc(sig["pool_step"], 1)
                made[0] += 1
                pool.wait_ge(sig["pool_step"], made[0])

            then(g.memset(ident[:], 0.0))
            then(g.affine_select(out=ident[:], in_=ident[:], compare_op=ALU.not_equal, fill=1.0, base=0,
                                 pattern=[[-1, P]], channel_multiplier=1))
            then(g.memset(ones[:], 1.0))
            then(g.memset(eps[:], EPS))
            pool.sem_inc(sig["masks_made"], 1)
            then(g.memset(ones64[:], 1.0))
            then(g.memset(ones64[0:64, 64:P], 0.0))
            then(g.memset(ones64[64:P, 0:64], 0.0))
            then(g.affine_select(out=tri[:], in_=ones[:], compare_op=ALU.is_ge, fill=0.0, base=0,
                                 pattern=[[-1, P]], channel_multiplier=1))
            then(g.memset(neg_diag[:], 0.0))
            then(g.affine_select(out=neg_diag[:], in_=neg_diag[:], compare_op=ALU.is_gt, fill=MASKED, base=0,
                                 pattern=[[1, P]], channel_multiplier=-1))

            def add_square(j, k):
                n = 8 * j + k
                pool.wait_ge(sig["sq_ready"], n + 1)
                if k == 0:
                    if j:
                        full(pool, sum_ticket[j - 1])
                    g.tensor_copy(sum_sq[:], sq[:, 0, :]).then_inc(sig["sq_used"], 1)
                else:
                    pool.wait_ge(sig["sq_used"], n)
                    g.tensor_tensor(sum_sq[:], sum_sq[:], sq[:, k % 2, :], ALU.add).then_inc(sig["sq_used"], 1)

            for k in range(KD):
                add_square(0, k)
            then(g.memset(level_mask[:], 0.0))
            for l in range(LEVELS):
                half, n = 1 << l, P >> (l + 1)
                m_ = level_mask[:, l, :].rearrange("p (n a t) -> p n a t", a=2, t=half)[:, :, 1, :]
                then(g.memset(m_, 1.0))
                then(g.affine_select(out=m_, in_=m_, compare_op=ALU.is_ge, fill=0.0, base=0,
                                     pattern=[[-2 * half, n], [0, half]], channel_multiplier=1))
                then(g.affine_select(out=m_, in_=m_, compare_op=ALU.is_ge, fill=0.0, base=half - 1,
                                     pattern=[[2 * half, n], [0, half]], channel_multiplier=-1))
            then(g.memset(batch_mask[:], 1.0))
            then(g.affine_select(out=batch_mask[:], in_=batch_mask[:], compare_op=ALU.is_ge, fill=0.0, base=0,
                                 pattern=[[-DEC_SEQ, DEC_BATCH]], channel_multiplier=1))
            then(g.affine_select(out=batch_mask[:], in_=batch_mask[:], compare_op=ALU.is_ge, fill=0.0,
                                 base=DEC_SEQ - 1, pattern=[[DEC_SEQ, DEC_BATCH]], channel_multiplier=-1))
            nn = neg_new[:].rearrange("p b t -> p (b t)")
            then(g.tensor_tensor(nn, level_mask[0:N_SAMPLE, 0, 0:N_SAMPLE], level_mask[0:N_SAMPLE, 1, 0:N_SAMPLE], ALU.add))
            then(g.tensor_scalar(nn, nn, -MASKED, MASKED, ALU.mult, ALU.add))
            then(g.memset(scan_keep[:], 1.0))
            then(g.memset(scan_keep[:, 0:N_SAMPLE:DEC_SEQ], 0.0))
            pool.sem_inc(sig["masks_made"], 1)

            for k in range(KD):
                add_square(1, k)
            for k in range(KD):
                add_square(2, k)
            for n, dst, src, done in ((0, o[2][0, 0].rearrange("(c p) h d -> p c (h d)", p=P), k_nat[:], "k_stored"),
                                      (1, o[3][0, 0].rearrange("(c p) h d -> p c (h d)", p=P), v_nat[:], "v_stored"),
                                      (3, o[5][0].rearrange("b t h d -> (b t) (h d)"), new_nat[:, 0, :], "nat_stored"),
                                      (3, o[6][0].rearrange("b t h d -> (b t) (h d)"), new_nat[:, 1, :], "nat_stored")):
                t = T0["natural"] + n
                pool.wait_ge(psum_free[t % 2], t // 2 + 1)
                pool.dma_start(dst, src).then_inc(sig[done], 16)

            def query(h):
                r = slice(64 * (h % 2), 64 * (h % 2) + 64)
                if h >= 2:
                    pool.wait_ge(sig["z_full"], h - 1)
                g.tensor_copy(q_pad[h % 2][r, 0:SEQ], flat(proj[:, SQ + h // 2])[r, 0:SEQ]).then_inc(sig["q_pad_ready"], 1)
                pool.wait_ge(sig["q_pad_ready"], h + 1)

            for h in range(2):
                then(g.memset(q_pad[h], 0.0))
                query(h)
            then(g.memset(q_block, 0.0))
            for hh in range(2):
                r = slice(64 * hh, 64 * hh + 64)
                q_ = proj[r, SQ:SQ + 4].rearrange("p k a t -> p k (a t)")[:, :, SEQ:T].rearrange(
                    "p k (b t) -> p k b t", t=DEC_SEQ)
                then(g.tensor_copy(q_block[r].rearrange("p k b (h t) -> p k b h t", h=2)[:, :, :, hh], q_))
                then(g.tensor_copy(neg_cols.rearrange("p k b (h t) -> p k b h t", h=2)[:, :, :, hh],
                                   neg_new[:].unsqueeze(1).broadcast_to([N_SAMPLE, 4, DEC_BATCH, DEC_SEQ])))
            for p in range(4):
                then(g.tensor_copy(bias_cols[:, p].rearrange("p b (h t) -> p b h t", h=2),
                                   bias[:, 2 * p:2 * p + 2].unsqueeze(1).unsqueeze(3).broadcast_to(
                                       [P, DEC_BATCH, 2, DEC_SEQ])))
            pool.sem_inc(sig["setup_new"], 1)
            for h in range(2, SB_HEADS):
                query(h)

            old = a["state_gla"][0].rearrange("b (p h) d v -> p (h d) b v", p=2)
            new_out = o[7][0].rearrange("b (p h) d v -> p (h d) b v", p=2)
            state_out = o[4][0, 0].rearrange("(p h) d v -> p (h d) v", p=2)
            pool.wait_ge(sig["c_full"], SB_HEADS)
            pool.wait_ge(sig["d_ready"], SB_HEADS)
            pool.dma_start(state_old, old[0]).then_inc(sig["state_in"], 16)
            for m, used in ((1, 4), (2, DEC_BATCH * N_PAGES)):
                pool.wait_ge(sig["n_out"], used)
                g.memset(q_lev[m % 2], 0.0).then_inc(sig["q_zero"], 1)
            for p, li in GLA_LEVELS:
                if li:
                    m, n_tok = number(p, li), T if li <= 2 else SEQ
                    half = 1 << (li - 1)
                    pool.wait_ge(sig["lev_exp"], m)
                    if m >= 3:
                        pool.wait_ge(sig["lev_full"], before(m - 2))
                    g.tensor_tensor(k_lev[m % 2][:, 0:n_tok], flat(proj[:, GK + p])[:, 0:n_tok],
                                    decay[m % 2][:, 0:n_tok], ALU.mult).then_inc(sig["lev_k"], 1)
                if li == 3:
                    pool.wait_ge(sig["last_ready"], p + 1)
                    pool.wait_ge(sig["state_in"], 16 * (p + 1))
                    g.tensor_tensor(state_new[p], state_old,
                                    decay_last[:, p, N_CH:].unsqueeze(2).broadcast_to([P, DEC_BATCH, P]),
                                    ALU.mult).then_inc(sig["sn_decayed"], 1)
                if li == 6:
                    pool.wait_ge(sig["state_ready"], N_CH * (p + 1))
                    pool.dma_start(state_out[p], state[p][:, N_CH - 1, :]).then_inc(sig["state_stored"], 16)
                    if p == 0:
                        pool.wait_ge(sig["on_full"], 1)
                        pool.wait_ge(sig["sn_decayed"], 1)
                        pool.dma_start(state_old, old[1]).then_inc(sig["state_in"], 16)
                if p and li == 2:
                    pool.wait_ge(sig["sn_out"], 2)
                    pool.dma_start(new_out[0], state_new[0]).then_inc(sig["new_stored"], 16)
            pool.wait_ge(sig["sn_out"], 4)
            pool.dma_start(new_out[1], state_new[1]).then_inc(sig["new_stored"], 16)

            pool.wait_ge(sig["m_ready"], KD)
            for n in range(5):
                rows_n = P if n < 4 else N_SAMPLE
                src = a["p_prompt"][0, 0, n * P:(n + 1) * P, :] if n < 4 else a["p_sample"][0].rearrange("b t d -> (b t) d")
                pool.dma_start(rows[0:rows_n, n, 0:PLE_DIM], src).then_inc(sig["p_in"], 16)
            for j in range(3, len(NORMS)):
                for k in range(KD):
                    add_square(j, k)


_INS = ["x_prompt", "x_sample", "cache_sb_k", "cache_sb_v", "state_gla", "page_table", "p_prompt", "p_sample",
        "f1_pre", "f1_in", "f1_out", "f1_post", "mix_pre", "w_in", "gate_w", "gate_b", "gla_norm", "sb_norm",
        "sb_bias", "w_out", "mix_post", "f2_pre", "f2_in", "f2_out", "f2_post", "ple_pre", "ple_w_gate",
        "ple_w_up", "ple_post"]
_OUTS = [(1, SEQ, D_MODEL), (DEC_BATCH, DEC_SEQ, D_MODEL), (1, 1, SEQ, SB_HEADS, SB_DH),
         (1, 1, SEQ, SB_HEADS, SB_DH), (1, 1, GLA_HEADS, GLA_DK, GLA_DV),
         (1, DEC_BATCH, DEC_SEQ, SB_HEADS, SB_DH), (1, DEC_BATCH, DEC_SEQ, SB_HEADS, SB_DH),
         (1, DEC_BATCH, GLA_HEADS, GLA_DK, GLA_DV)]


def kernel(**inputs):
    import numpy as np
    import concourse.bacc as bacc
    from concourse.bass_utils import run_bass_kernel_spmd

    nc = bacc.Bacc("TRN2", target_bir_lowering=False, num_devices=1)
    arrays, ins = {}, {}
    for name in _INS:
        v = np.ascontiguousarray(inputs[name])
        arrays[f"in_{name}"] = v
        ins[name] = nc.dram_tensor(f"in_{name}", v.shape, mybir.dt.from_np(v.dtype), kind="ExternalInput").ap()
    outs = [nc.dram_tensor(f"out_{i}", s, F32, kind="ExternalOutput").ap() for i, s in enumerate(_OUTS)]
    build(nc, ins, outs)
    r = run_bass_kernel_spmd(nc, [arrays], core_ids=[0])
    return tuple(r.results[0][f"out_{i}"] for i in range(len(_OUTS)))
```
